# Optimizing a Trainium2 kernel written in Bass

```python
import math
import jax
import jax.numpy as jnp
from jax import lax
import numpy as np

D_MODEL = 2048
BATCH = 1
SEQ = 256
DEPTH = 1

HEAD_DIM = 128
MIX_HEADS = D_MODEL // HEAD_DIM
FOX_HEADS = MIX_HEADS // 4
SWA_HEADS = MIX_HEADS // 2
SWA_KV_HEADS = SWA_HEADS // 4
GLA_HEADS = MIX_HEADS - FOX_HEADS - SWA_HEADS
GLA_DK = HEAD_DIM // 2
GLA_DV = HEAD_DIM
GLA_GATE_RANK = 16
GLA_TAU = 16.0
GLA_CHUNK = 64
MIX_WIDTH = MIX_HEADS * HEAD_DIM
Q_BLOCK = 128
SWA_WINDOW = 128
NUM_BUCKETS = 32
T5_MAX_DISTANCE = 128
XATTN_HEADS = 4
MEM_LEN = 256
D_FF = ((8 * D_MODEL // 3 + 255) // 256) * 256
CONV_WIDTH = 3
EPS = 1e-6

IN_SPLITS = (FOX_HEADS * HEAD_DIM, FOX_HEADS * HEAD_DIM, FOX_HEADS * HEAD_DIM, FOX_HEADS,
             SWA_HEADS * HEAD_DIM, SWA_KV_HEADS * HEAD_DIM, SWA_KV_HEADS * HEAD_DIM,
             GLA_HEADS * GLA_DK, GLA_HEADS * GLA_DK, GLA_HEADS * GLA_DV, GLA_HEADS * GLA_DV,
             GLA_GATE_RANK)
IN_COLS = sum(IN_SPLITS)
IN_SPLIT_POINTS = tuple(int(v) for v in np.cumsum(IN_SPLITS)[:-1])

kernel_name = 'hybrid_fox_swa_gla_trunk'

def rms_norm(x, g):
    xf = x.astype(jnp.float32)
    y = xf * lax.rsqrt(jnp.mean(xf * xf, axis=-1, keepdims=True) + EPS)
    return (y * g.astype(jnp.float32)).astype(x.dtype)

def fox_attention(q, k, v, f_logit):
    B, H, T, Dh = q.shape
    nb = T // Q_BLOCK
    c = jnp.cumsum(jax.nn.log_sigmoid(f_logit.astype(jnp.float32)), axis=-1)
    qb = q.reshape(B, H, nb, Q_BLOCK, Dh).transpose(2, 0, 1, 3, 4)
    cb = c.reshape(B, H, nb, Q_BLOCK).transpose(2, 0, 1, 3)
    kpos = jnp.arange(T)
    scale = Dh ** -0.5

    def block(args):
        qi, ci, i = args
        s = jnp.einsum('bhqd,bhkd->bhqk', qi, k).astype(jnp.float32) * scale
        s = s + ci[..., None] - c[:, :, None, :]
        qpos = i * Q_BLOCK + jnp.arange(Q_BLOCK)
        s = jnp.where(kpos[None, :] <= qpos[:, None], s, -jnp.inf)
        p = jax.nn.softmax(s, axis=-1).astype(v.dtype)
        return jnp.einsum('bhqk,bhkd->bhqd', p, v)

    o = lax.map(block, (qb, cb, jnp.arange(nb)))
    return o.transpose(1, 2, 0, 3, 4).reshape(B, H, T, Dh)

def t5_bucket(rel):
    n = jnp.maximum(rel, 0)
    max_exact = NUM_BUCKETS // 2
    nf = jnp.maximum(n, 1).astype(jnp.float32)
    large = max_exact + (jnp.log(nf / max_exact) / math.log(T5_MAX_DISTANCE / max_exact)
                         * (NUM_BUCKETS - max_exact)).astype(jnp.int32)
    large = jnp.minimum(large, NUM_BUCKETS - 1)
    return jnp.where(n < max_exact, n, large)

def swa_attention(q, k, v, sinks, t5_bias):
    B, Hq, T, Dh = q.shape
    Hkv = k.shape[1]
    G = Hq // Hkv
    W = SWA_WINDOW
    nb = T // W
    qb = q.reshape(B, Hkv, G, nb, W, Dh)

    def band(a):
        ab = a.reshape(B, Hkv, nb, W, Dh)
        prev = jnp.pad(ab[:, :, :-1], ((0, 0), (0, 0), (1, 0), (0, 0), (0, 0)))
        return jnp.concatenate([prev, ab], axis=3)

    kb, vb = band(k), band(v)
    s = jnp.einsum('bhgnqd,bhnkd->bhgnqk', qb, kb).astype(jnp.float32) * (Dh ** -0.5)
    i = jnp.arange(W)
    j = jnp.arange(2 * W)
    rel = (W + i)[:, None] - j[None, :]
    bias = t5_bias[t5_bucket(rel)].astype(jnp.float32)
    bias = jnp.transpose(bias, (2, 0, 1)).reshape(Hkv, G, 1, W, 2 * W)
    s = s + bias
    in_window = (rel >= 0) & (rel < W)
    blk = jnp.arange(nb)
    valid = in_window[None] & ((blk[:, None, None] > 0) | (j[None, None, :] >= W))
    s = jnp.where(valid, s, -jnp.inf)
    sink = jnp.broadcast_to(sinks.astype(jnp.float32).reshape(1, Hkv, G, 1, 1, 1), s.shape[:-1] + (1,))
    p = jax.nn.softmax(jnp.concatenate([s, sink], axis=-1), axis=-1)[..., :-1].astype(v.dtype)
    o = jnp.einsum('bhgnqk,bhnkd->bhgnqd', p, vb)
    return o.reshape(B, Hq, T, Dh)

def gla_chunked(q, k, v, log_a):
    B, H, T, dk = q.shape
    dv = v.shape[-1]
    C = GLA_CHUNK
    nc = T // C
    f32 = jnp.float32
    qc = (q.astype(f32) * (dk ** -0.5)).reshape(B, H, nc, C, dk)
    kc = k.astype(f32).reshape(B, H, nc, C, dk)
    vc = v.astype(f32).reshape(B, H, nc, C, dv)
    gc = log_a.astype(f32).reshape(B, H, nc, C, dk)
    b = jnp.cumsum(gc, axis=3)
    b_last = b[:, :, :, -1:, :]
    q_t = qc * jnp.exp(b)
    k_t = kc * jnp.exp(-b)
    k_end = kc * jnp.exp(b_last - b)
    causal = jnp.tril(jnp.ones((C, C), dtype=bool))
    A = jnp.where(causal, jnp.einsum('bhnqd,bhnkd->bhnqk', q_t, k_t), 0.0)
    o_intra = jnp.einsum('bhnqk,bhnkd->bhnqd', A, vc)
    kv = jnp.einsum('bhnkd,bhnke->bhnde', k_end, vc)
    decay = jnp.exp(b_last[:, :, :, 0, :])

    def step(S, inp):
        dec, kv_n = inp
        return dec[..., None] * S + kv_n, S

    S0 = jnp.zeros((B, H, dk, dv), f32)
    _, S_prev = lax.scan(step, S0, (jnp.moveaxis(decay, 2, 0), jnp.moveaxis(kv, 2, 0)))
    S_prev = jnp.moveaxis(S_prev, 0, 2)
    o_inter = jnp.einsum('bhnqd,bhnde->bhnqe', q_t, S_prev)
    return (o_intra + o_inter).reshape(B, H, T, dv).astype(v.dtype)

def hybrid_mixer(xn, w_in, b_f, sinks, t5_bias, w_gate, b_gate, gla_g, w_out):
    B, T, _ = xn.shape
    proj = xn @ w_in
    (fq, fk, fv, ff, sq, sk, sv, gq, gk, gv, gr, glr) = jnp.split(proj, IN_SPLIT_POINTS, axis=-1)

    def heads(a, n):
        return a.reshape(B, T, n, -1).transpose(0, 2, 1, 3)

    def merge(a):
        return a.transpose(0, 2, 1, 3).reshape(B, T, -1)

    o_fox = fox_attention(heads(fq, FOX_HEADS), heads(fk, FOX_HEADS), heads(fv, FOX_HEADS),
                          (ff + b_f).transpose(0, 2, 1))
    o_swa = swa_attention(heads(sq, SWA_HEADS), heads(sk, SWA_KV_HEADS), heads(sv, SWA_KV_HEADS),
                          sinks, t5_bias)
    log_a = jax.nn.log_sigmoid((glr @ w_gate + b_gate).astype(jnp.float32)) / GLA_TAU
    o_gla = gla_chunked(heads(gq, GLA_HEADS), heads(gk, GLA_HEADS), heads(gv, GLA_HEADS),
                        heads(log_a, GLA_HEADS))
    o_gla = merge(rms_norm(o_gla, gla_g)) * jax.nn.silu(gr)
    o = jnp.concatenate([merge(o_fox), merge(o_swa), o_gla], axis=-1)
    return o @ w_out

def cross_attention(xn, memn, wq, wkv, wo):
    B, T, _ = xn.shape
    M = memn.shape[1]
    q = (xn @ wq).reshape(B, T, XATTN_HEADS, HEAD_DIM)
    k, v = jnp.split((memn @ wkv).reshape(B, M, 2 * XATTN_HEADS, HEAD_DIM), 2, axis=2)
    s = jnp.einsum('bthd,bmhd->bhtm', q, k).astype(jnp.float32) * (HEAD_DIM ** -0.5)
    p = jax.nn.softmax(s, axis=-1).astype(v.dtype)
    o = jnp.einsum('bhtm,bmhd->bthd', p, v).reshape(B, T, XATTN_HEADS * HEAD_DIM)
    return o @ wo

def conv_ffn(xn, w_up, conv_w, conv_b, w_down):
    T = xn.shape[1]
    u = xn @ w_up
    up = jnp.pad(u, ((0, 0), (CONV_WIDTH - 1, 0), (0, 0)))
    uc = conv_b + conv_w[CONV_WIDTH - 1] * u
    for j in range(CONV_WIDTH - 1):
        uc = uc + conv_w[j] * up[:, j:j + T]
    gate, val = jnp.split(uc, 2, axis=-1)
    return (jax.nn.silu(gate) * val) @ w_down

def setup_inputs(seed: int = 0) -> dict:
    key = jax.random.key(seed)
    ks = jax.random.split(key, 24)
    nrm = jax.random.normal
    f32 = jnp.float32
    XW = XATTN_HEADS * HEAD_DIM
    return {
        'x': nrm(ks[0], (BATCH, SEQ, D_MODEL), f32),
        'mem': nrm(ks[1], (BATCH, MEM_LEN, D_MODEL), f32),
        'w_in': nrm(ks[2], (DEPTH, D_MODEL, IN_COLS), f32) * D_MODEL ** -0.5,
        'b_fox_f': 3.0 + 0.5 * nrm(ks[3], (DEPTH, FOX_HEADS), f32),
        'swa_sinks': 0.5 * nrm(ks[4], (DEPTH, SWA_HEADS), f32),
        't5_bias': 0.5 * nrm(ks[5], (NUM_BUCKETS, SWA_HEADS), f32),
        'w_gla_gate': nrm(ks[6], (DEPTH, GLA_GATE_RANK, GLA_HEADS * GLA_DK), f32) * GLA_GATE_RANK ** -0.5,
        'b_gla_gate': 0.1 * nrm(ks[7], (DEPTH, GLA_HEADS * GLA_DK), f32),
        'gla_norm': 1.0 + 0.02 * nrm(ks[8], (DEPTH, GLA_DV), f32),
        'w_mix_out': nrm(ks[9], (DEPTH, MIX_WIDTH, D_MODEL), f32) * MIX_WIDTH ** -0.5,
        'norm_mix': 1.0 + 0.02 * nrm(ks[10], (DEPTH, D_MODEL), f32),
        'norm_xattn': 1.0 + 0.02 * nrm(ks[11], (DEPTH, D_MODEL), f32),
        'norm_mem': 1.0 + 0.02 * nrm(ks[12], (DEPTH, D_MODEL), f32),
        'wq_x': nrm(ks[13], (DEPTH, D_MODEL, XW), f32) * D_MODEL ** -0.5,
        'wkv_x': nrm(ks[14], (DEPTH, D_MODEL, 2 * XW), f32) * D_MODEL ** -0.5,
        'wo_x': nrm(ks[15], (DEPTH, XW, D_MODEL), f32) * XW ** -0.5,
        'norm_ffn': 1.0 + 0.02 * nrm(ks[16], (DEPTH, D_MODEL), f32),
        'w_up': nrm(ks[17], (DEPTH, D_MODEL, 2 * D_FF), f32) * D_MODEL ** -0.5,
        'conv_w': nrm(ks[18], (DEPTH, CONV_WIDTH, 2 * D_FF), f32) * CONV_WIDTH ** -0.5,
        'conv_b': 0.02 * nrm(ks[19], (DEPTH, 2 * D_FF), f32),
        'w_down': nrm(ks[20], (DEPTH, D_FF, D_MODEL), f32) * D_FF ** -0.5,
        'final_norm': 1.0 + 0.02 * nrm(ks[21], (D_MODEL,), f32),
    }

def reference(x, mem, w_in, b_fox_f, swa_sinks, t5_bias, w_gla_gate, b_gla_gate, gla_norm,
              w_mix_out, norm_mix, norm_xattn, norm_mem, wq_x, wkv_x, wo_x, norm_ffn,
              w_up, conv_w, conv_b, w_down, final_norm):
    h = x
    for l in range(DEPTH):
        h = h + hybrid_mixer(rms_norm(h, norm_mix[l]), w_in[l], b_fox_f[l], swa_sinks[l], t5_bias,
                             w_gla_gate[l], b_gla_gate[l], gla_norm[l], w_mix_out[l])
        h = h + cross_attention(rms_norm(h, norm_xattn[l]), rms_norm(mem, norm_mem[l]),
                                wq_x[l], wkv_x[l], wo_x[l])
        h = h + conv_ffn(rms_norm(h, norm_ffn[l]), w_up[l], conv_w[l], conv_b[l], w_down[l])
    return rms_norm(h, final_norm)


_drawn_inputs = setup_inputs


def setup_inputs(seed=0):
    import zlib

    import numpy as np

    out = dict(_drawn_inputs(seed))
    spreads = {}
    factors = {'swa_sinks': 7.696,
     'b_gla_gate': 4.257,
     'gla_norm': 8.0,
     'norm_mix': 3.222,
     'norm_xattn': 8.0,
     'norm_mem': 8.0,
     'norm_ffn': 12.187,
     'conv_b': 11.81,
     'final_norm': 7.625}
    for name, (base, spread) in spreads.items():
        noise = np.random.default_rng([zlib.crc32(name.encode()), seed]).standard_normal(out[name].shape)
        drawn = base * np.exp(spread * noise) if base else spread * noise
        out[name] = jnp.asarray(drawn.astype(out[name].dtype))
    for name, factor in factors.items():
        out[name] = (out[name] * factor).astype(out[name].dtype)
    return out
```

```python
from contextlib import ExitStack

import numpy as np

import concourse.bass as bass
from concourse import mybir

F32 = mybir.dt.float32
F32R = mybir.dt.float32r
ACT = mybir.ActivationFunctionType
ALU = mybir.AluOpType
AX = mybir.AxisListType

P = 128
D = 2048
T = 256
TT = T // P
KT = D // P
HD = 128
FOX, SWA, SWA_KV, GLA, XH = 4, 8, 2, 4, 4
GLA_DK, GLA_DV, GLA_RANK, CHUNK = 64, 128, 16, 64
NCH = T // CHUNK
D_FF = 5632
FT = D_FF // P
NBUCKET, MAXDIST = 32, 128
EPS = 1e-6
SCALE = float(HD) ** -0.5
NEG = -1.0e30
UNIT = 2048
SUB = UNIT // 2
RAW = 4
LOOK = 2

WIN = {}
_at = 0
for _n, _w in (("fq", FOX * HD), ("fk", FOX * HD), ("fv", FOX * HD), ("ff", FOX), ("sq", SWA * HD),
               ("sk", SWA_KV * HD), ("sv", SWA_KV * HD), ("gq", GLA * GLA_DK), ("gk", GLA * GLA_DK),
               ("gv", GLA * GLA_DV), ("gr", GLA * GLA_DV), ("glr", GLA_RANK)):
    WIN[_n] = _at
    _at += _w

FQ, FK, SQ, SK, GQ, GK, GR = 0, 1024, 2048, 4096, 4608, 5120, 5632
FV, SV, GV, MK, MV = 6656, 7680, 8192, 9216, 10240
WORK = 11264
NTMP = 0
MTMP = 7168
BIAS = 9216
XQ = 4096
G_MIX, G_X, G_MEM, G_FFN, B_GATE, G_GLA, NPRM = 0, 16, 32, 48, 64, 66, 67


class Unit:

    def __init__(self, kind, w, k0, nk, c0, nc, first, last, dest=0, scale=1.0, xt="a", half=0, tiles=(), ring=None):
        self.kind, self.w, self.k0, self.nk, self.c0, self.nc = kind, w, k0, nk, c0, nc
        self.first, self.last = first, last
        self.dest, self.scale, self.xt = dest, scale, xt
        self.half, self.tiles, self.ring = half, tiles, ring
        self.banks = []


def plan():
    units, jobs = [], {}

    def job(slot, name, arg=None):
        jobs.setdefault(slot, []).append((name, arg))

    def cols(w, c0, ncols, dest, scale, xt):
        for c in range(0, ncols, 256):
            for half in range(2):
                units.append(Unit("cols", w, 8 * half, 8, c0 + c, 256, half == 0, half == 1,
                                  dest=dest + c * T // P, scale=scale, xt=xt))

    def rows(w, c0, ncols, dest, xt):
        nk = UNIT // ncols
        for k in range(0, KT, nk):
            units.append(Unit("rows", w, k, nk, c0, ncols, k == 0, k + nk == KT, dest=dest, xt=xt))

    def wide(w, order, tiles, ring):
        for half in range(2):
            for i, k in enumerate(order):
                units.append(Unit("wide", w, k, 2, 1024 * half, 1024, i == 0, i == len(order) - 1,
                                  half=half, tiles=tiles, ring=ring))

    cols("w_in", WIN["fk"], 512, FK, 1.0, "a")
    rows("w_in", WIN["fv"], 512, FV, "a")
    cols("w_in", WIN["fq"], 512, FQ, SCALE, "a")
    cols("w_in", WIN["gk"], 256, GK, 1.0, "a")
    cols("w_in", WIN["gq"], 256, GQ, float(GLA_DK) ** -0.5, "a")
    rows("w_in", WIN["gv"], 512, GV, "a")
    cols("w_in", WIN["gr"], 512, GR, 1.0, "a")
    cols("w_in", WIN["sk"], 256, SK, 1.0, "a")
    rows("w_in", WIN["sv"], 256, SV, "a")
    cols("w_in", WIN["sq"], 1024, SQ, SCALE, "a")
    tiles = [FQ + T * h for h in range(FOX)] + [SQ + T * h for h in range(SWA)] + [FK + T * h for h in range(GLA)]
    n_mix = len(units)
    wide("w_mix_out", [0, 2, 12, 14, 4, 6, 8, 10], tiles, "a")
    n_mk = len(units)
    cols("wkv_x", 0, 512, MK, 1.0, "b")
    n_wq = len(units)
    cols("wq_x", 0, 512, XQ, SCALE, "a")
    rows("wkv_x", 512, 512, MV, "b")
    n_wo = len(units)
    wide("wo_x", [0, 2], [XQ + T * h for h in range(XH)], "b")
    n_up = len(units)

    group = 0
    for u, x in enumerate(units):
        if x.kind == "wide":
            x.banks = [4 * x.half + i for i in range(4)]
        if x.first and x.kind != "wide":
            pair = group % 2
            group += 1
        if x.kind != "wide":
            x.banks = [2 * pair, 2 * pair + 1]
        if x.last:
            job(u, "evac_" + x.kind, u)
    for c in range(4):
        job(c, "mem_norm", c)
    job(4, "gates_in")
    job(6, "gates_t")
    job(7, "fox_gates")
    job(8, "bias_load")
    for h in range(FOX):
        heads(job, ("fox", h, h), 10 + h)
    job(14, "gla_z")
    job(15, "gla_decay")
    job(17, "gla_scale")
    job(18, "gla_scores")
    job(20, "gla_kv")
    job(22, "gla_out")
    job(23, "gla_rms")
    job(24, "gla_norm")
    job(24, "gla_silu")
    job(25, "gla_o")
    for h in range(SWA):
        heads(job, ("swa", h, FOX + h), n_mix - 6 + h)
    job(n_mix + 15, "norm", 2)
    job(n_mix + 17, "norm_t", 2)
    for h, slot in enumerate((n_wq + 2, n_wq + 3, n_wq + 4, n_wq + 4)):
        heads(job, ("x", h, FOX + SWA + h), slot, n_wo - 1)
    job(n_up - 1, "norm", 3)
    job(n_up - 1, "norm_t", 3)
    stages = ["head_o", "head_t", "head_n", "head_s"]
    for some in jobs.values():
        some.sort(key=lambda x: 0 if x[0].startswith("evac") else 1 + stages.index(x[0]) if x[0] in stages else 9)
    return units, jobs, n_mix, n_up


def heads(job, head, slot, out_slot=None):
    for i, stage in enumerate(("head_s", "head_n", "head_t")):
        job(slot + i, stage, head)
    job(out_slot or slot + 3, "head_o", head)


def bucket(n):
    half = NBUCKET // 2
    if n < half:
        return n
    big = half + int(np.float32(np.log(np.float32(n) / np.float32(half)))
                     / np.float32(np.log(MAXDIST / half)) * np.float32(NBUCKET - half))
    return min(big, NBUCKET - 1)


def onehot_table():
    t = np.zeros((NBUCKET, P), np.float32)
    for y in range(P):
        t[bucket((-y) % P), y] = 1.0
    return t


def trunk(nc, x, mem, w_in, b_fox_f, swa_sinks, t5_bias, w_gla_gate, b_gla_gate, gla_norm, w_mix_out,
          norm_mix, norm_xattn, norm_mem, wq_x, wkv_x, wo_x, norm_ffn, w_up, conv_w, conv_b, w_down,
          final_norm, t5_onehot, out):
    weights = {"w_in": w_in[0], "w_mix_out": w_mix_out[0], "wkv_x": wkv_x[0], "wq_x": wq_x[0], "wo_x": wo_x[0],
               "w_up": w_up[0], "w_down": w_down[0]}
    units, jobs, N_MIX, UP0 = plan()
    UP_ITERS = FT // 2
    DOWN0 = UP0 + 4 * UP_ITERS
    HALF = FT // 2
    GAIN = DOWN0 + 2 * HALF
    assert UP0 % RAW == 0 and DOWN0 % RAW == 0 and HALF % RAW == 2

    ctx = ExitStack()
    with ctx:
        def sb(name, shape, dt=F32):
            return ctx.enter_context(nc.sbuf_tensor("sb_" + name, shape, dt))

        def sem(name):
            return ctx.enter_context(nc.semaphore(name))

        raw = sb("raw", [P, RAW, UNIT])
        wt_hi = sb("wt_hi", [P, 4, SUB], F32R)
        wt_lo = sb("wt_lo", [P, 4, SUB], F32R)
        xt = {"a": sb("xt_a", [P, KT, 2 * T], F32R), "b": sb("xt_b", [P, KT, 2 * T], F32R)}
        h = sb("h", [P, TT, D])
        work = sb("work", [P, WORK])
        att = sb("att", [P, 2560])
        low = sb("low", [P, 2, 2, T])
        ident = sb("ident", [P, P])
        prm = sb("prm", [P, NPRM])
        conv = sb("conv", [P, 4, 2 * FT])
        fox_mask = sb("fox_mask", [P, 3 * P])
        ones = sb("ones", [P, T])
        sumsq = sb("sumsq", [P, TT, 4])
        meansq = sb("meansq", [P, 8])
        rstd = sb("rstd", [P, 8])
        mhalf = sb("mhalf", [P, 8])
        negmax = sb("negmax", [P, 3, 2])
        rowmax = sb("rowmax", [P, 3, 2])
        den = sb("den", [P, 3, 2])
        sink_e = sb("sink_e", [P, 3, 2])
        rden = sb("rden", [P, 3, 2])
        sinks = sb("sinks", [P, SWA])
        b_fox = sb("b_fox", [FOX, 1])
        ps = ctx.enter_context(nc.psum_tensor("ps", [P, 8, 512], F32))
        bias_dram = nc.dram_tensor("bias_rows", [SWA, P * P], F32, kind="Internal").ap()

        def wk(at, *shape):
            n = int(np.prod(shape))
            v = work[:, at:at + n]
            if len(shape) == 2:
                v = v.rearrange("p (a b) -> p a b", b=shape[1])
            if len(shape) == 3:
                v = v.rearrange("p (a b c) -> p a b c", b=shape[1], c=shape[2])
            return v

        probs = att[:, 0:1536].rearrange("p (r n) -> p r n", r=3)
        probs_t = att[:, 1536:2560].rearrange("p (r n) -> p r n", r=2)
        rows_prm = att[0:NPRM, 0:P]
        rows_conv = att[0:2 * FT, P:P + 512].rearrange("p (a b) -> p a b", a=4)
        t5_sb = att[0:NBUCKET, 640:640 + SWA]
        onehot_sb = att[0:NBUCKET, 656:656 + P]
        bias_row = att[0:SWA, 784:784 + P]
        gate_w_in = att[:, 1024:1024 + KT * 20].rearrange("p (k n) -> p k n", n=20)
        gla_w = work[0:GLA_RANK, SK:SK + GLA * GLA_DK]
        sel = work[0:FOX, GR:GR + 512].rearrange("p (h n) -> p h n", h=FOX)
        glr_t = work[0:GLA_RANK, GR + 512:GR + 768]
        gate_nat = work[:, GR + 768:GR + 808].rearrange("p (t n) -> p t n", n=20)
        c_sel = work[0:FOX, SQ:SQ + 1024].rearrange("p (h n) -> p h n", h=FOX)
        neg_c = work[0:FOX, SQ + 1024:SQ + 1280]
        f_z = work[0:FOX, SQ + 1280:SQ + 1536]
        f_m = work[0:FOX, SQ + 1536:SQ + 1792]
        f_e = work[0:FOX, SQ + 1792:SQ + 2048]
        g_z = wk(SV, 512)
        g_m = wk(SK, 512)
        g_b = wk(SQ + 1536, 512)
        g_e = wk(GR, 512)
        g_kend_t = probs_t[:, 0, :]
        g_kend = probs_t[:, 1, :].rearrange("p (t n) -> p t n", t=TT)
        g_at = wk(FV, GLA, NCH, CHUNK)
        g_s = wk(SQ, GLA, NCH - 1, GLA_DV)
        g_o = att[:, 0:1024].rearrange("p (t n) -> p t n", t=TT)
        g_sq = att[:, 1536:2560].rearrange("p (t n) -> p t n", t=TT)
        bias_m = work[:, BIAS:BIAS + 2048].rearrange("p (h m k) -> p h m k", h=SWA, m=2)
        junk = att[:, 1024:1536]
        u_pad = att[:, 0:4 * (T + 2)].rearrange("p (i n) -> p i n", i=4)
        cv = att[:, 1032:1032 + 4 * T].rearrange("p (i n) -> p i n", i=4)
        act_t = work[:, :]

        raw_in = [sem(f"raw_in{i}") for i in range(RAW)]
        hi_done = sem("hi_done")
        lo_done = sem("lo_done")
        sub_used = sem("sub_used")
        stat_hi = sem("stat_hi")
        stat_lo = sem("stat_lo")
        bank_full = {b: sem(f"bank_full{b}") for b in range(4, 8)}
        low_ready = sem("low_ready")
        proj_done = sem("proj_done")
        x_in = [sem(f"x_in{t}") for t in range(TT)]
        mem_in = sem("mem_in")
        small_in = sem("small_in")
        c_ready = sem("c_ready")
        pool_step = sem("pool_step")
        dve_step = sem("dve_step")
        act_step = sem("act_step")
        prm_ready = sem("prm_ready")
        bias_out = sem("bias_out")
        bias_in = sem("bias_in")
        bias_done = sem("bias_done")
        stats_a = sem("stats_a")
        stats_d = sem("stats_d")
        h_added = sem("h_added")
        meansq_ready = sem("meansq_ready")
        rstd_ready = sem("rstd_ready")
        xn_a = sem("xn_a")
        xn_d = sem("xn_d")
        xt_hi = sem("xt_hi")
        xt_ready = sem("xt_ready")
        scored = sem("scored")
        exped = sem("exped")
        normed = sem("normed")
        pt_ready = sem("pt_ready")
        o_ready = sem("o_ready")
        gate_nat_ready = sem("gate_nat_ready")
        gate_t_ready = sem("gate_t_ready")
        gate_a = sem("gate_a")
        fox_ready = sem("fox_ready")
        gla_d = sem("gla_d")
        gla_a = sem("gla_a")
        gla_p = sem("gla_p")
        gla_done = sem("gla_done")
        u_ready = sem("u_ready")
        cv_init = sem("cv_init")
        cv_tap = sem("cv_tap")
        cv_done = sem("cv_done")
        silu_done = sem("silu_done")
        act_done = sem("act_done")
        out_ready = sem("out_ready")
        out_written = sem("out_written")

        STAT0 = sum(2 for w in units if w.kind == "wide")
        wides = [u for u, w in enumerate(units) if w.kind == "wide"]
        groups = [u for u, w in enumerate(units) if w.last and w.kind != "wide"]
        cols_groups = [u for u in groups if units[u].kind == "cols"]
        n_proj, n_low = len(groups), len(cols_groups)
        PROJ = {"fv": 3, "fq": 5, "gk": 6, "gq": 7, "gv": 8, "gr": 10, "sv": 12, "sq": 16, "xq": 20, "mv": 21}
        assert n_proj == PROJ["mv"]
        reader = {4: (prm_ready, 2), 5: (prm_ready, 3)}
        free = {}
        full = {}
        fills = {b: 0 for b in range(4, 8)}
        fills[4] = fills[5] = 1

        def out_bank(head):
            return 6 + head[1] % 2 if head[0] == "x" else 6

        def head_probs_t(head):
            kind, i, a = head
            return wk(NTMP + 2 * T * i, 2 * T) if kind == "x" else probs_t[:, a % 2, :]

        def take(key, b, semaphore, count):
            free[key, b] = reader.get(b)
            reader[b] = (semaphore, count)
            if b >= 4:
                fills[b] += 1
                full[key, b] = fills[b]

        for m in range(8):
            take(("norm_t", 0, m), 4 + m % 4, xt_ready, m + 1)
        chunks = 0
        chunk0 = {}
        for u, w in enumerate(units):
            if w.first and w.kind == "wide":
                for i in range(4):
                    b = 4 * w.half + i
                    free["unit", u, b] = reader.get(b)
                    reader[b] = (h_added, chunks + i + 1)
                last = next(v for v in range(u, len(units)) if units[v].last)
                chunk0[last] = chunks
                chunks += 4
            elif w.first:
                last = next(v for v in range(u, len(units)) if units[v].last)
                for b in w.banks:
                    free["unit", u, b] = reader.get(b)
                    reader[b] = (proj_done, groups.index(last) + 1)
            for name, arg in jobs.get(u, []):
                if name == "mem_norm":
                    for m in (2 * arg, 2 * arg + 1):
                        take(("norm_t", 1, m), 4 + m % 4, xt_ready, 8 + m + 1)
                elif name == "norm_t":
                    for m in range(8):
                        take((name, arg, m), 4 + m % 4, xt_ready, 8 * arg + m + 1)
                elif name == "gates_in":
                    take(name, 7, gate_nat_ready, 1)
                elif name == "gates_t":
                    take(name, 7, gate_t_ready, 2)
                elif name == "gla_z":
                    take(name, 7, gla_d, 1)
                elif name == "gla_scores":
                    take(name, 7, gla_d, 5)
                    take(name, 4, gla_a, 5)
                    take(name, 6, gla_a, 5)
                elif name == "gla_kv":
                    take(name, 4, gla_d, 6)
                    take(name, 7, gla_d, 6)
                elif name == "gla_out":
                    take(name, 6, gla_d, 7)
                    take(name, 7, gla_d, 7)
                elif name == "gla_o":
                    take(name, 6, gla_done, 1)
                    take(name, 7, gla_done, 1)
                elif name == "head_s":
                    take((name, arg[2]), 4, exped if arg[0] == "x" else scored, arg[2] + 1)
                elif name == "head_t":
                    take((name, arg[2]), 5, pt_ready, arg[2] + 1)
                elif name == "head_o":
                    take((name, arg[2]), out_bank(arg), o_ready, arg[2] + 1)
        down_free = {b: reader[b] for b in range(4, 8)}
        up_free = {b: reader[b] for b in range(4)}
        DOWN_CHUNK0 = chunks

        def stationary_of(u):
            for v in (u + LOOK, u + 1):
                if v < len(units) and units[v].kind == "wide" and (v == u + 1) == (units[v].w == "wo_x"):
                    return v
            return None

        def head_sources(head):
            kind, i, _ = head
            if kind == "fox":
                v = wk(FV, TT, 512)[:, :, HD * i:HD * i + HD]
                return FQ + T * i, FK + T * i, v, PROJ["fq"] - 1 + i // 2, PROJ["fv"]
            if kind == "swa":
                g = i // (SWA // SWA_KV)
                v = wk(SV, TT, 256)[:, :, HD * g:HD * g + HD]
                return SQ + T * i, SK + T * g, v, PROJ["sq"] - 3 + i // 2, PROJ["sv"]
            v = wk(MV, TT, 512)[:, :, HD * i:HD * i + HD]
            return XQ + T * i, MK + T * i, v, PROJ["xq"] - 1 + i // 2, PROJ["mv"]

        XN_AT = [NTMP, MTMP, NTMP, NTMP]
        GAIN_ROW = [G_MIX, G_MEM, G_X, G_FFN]
        XT_OF = [xt["a"], xt["b"], xt["a"], xt["a"]]

        def norm_source(k, t):
            return work[:, MTMP + D * t:MTMP + D * t + D] if k == 1 else h[:, t, :]

        small_loads = (
            (rows_prm[G_MIX:G_MIX + 16], norm_mix[0].rearrange("(k p) -> k p", p=P)),
            (rows_prm[G_X:G_X + 16], norm_xattn[0].rearrange("(k p) -> k p", p=P)),
            (rows_prm[G_MEM:G_MEM + 16], norm_mem[0].rearrange("(k p) -> k p", p=P)),
            (rows_prm[G_FFN:G_FFN + 16], norm_ffn[0].rearrange("(k p) -> k p", p=P)),
            (rows_prm[B_GATE:B_GATE + 2], b_gla_gate[0].rearrange("(k p) -> k p", p=P)),
            (rows_prm[G_GLA:G_GLA + 1], gla_norm),
            (rows_conv[:, 0:3, :], conv_w[0].rearrange("j (k p) -> k j p", p=P)),
            (rows_conv[:, 3, :], conv_b[0].rearrange("(k p) -> k p", p=P)),
            (t5_sb, t5_bias),
            (onehot_sb, t5_onehot),
            (sinks[:], bass.AP(tensor=swa_sinks.tensor, offset=0, ap=[[0, P], [1, SWA]])),
            (b_fox[:], bass.AP(tensor=b_fox_f.tensor, offset=0, ap=[[1, FOX], [1, 1]])),
            (gla_w, w_gla_gate[0]),
            (gate_w_in[:, :, 0:FOX],
             weights["w_in"].rearrange("(k p) c -> p k c", p=P)[:, :, WIN["ff"]:WIN["ff"] + FOX]),
            (gate_w_in[:, :, FOX:20],
             weights["w_in"].rearrange("(k p) c -> p k c", p=P)[:, :, WIN["glr"]:WIN["glr"] + GLA_RANK]),
        )
        N_SMALL = len(small_loads)

        block = ctx.enter_context(nc.Block())


        @block.sync
        def _(sp):
            def load(j, c, src):
                if c >= RAW:
                    sp.wait_ge(lo_done, 8 * j + (2 * c - 2 * RAW + 2))
                i = c % RAW
                sp.dma_start(raw[:, i, :].rearrange("p (k n) -> p k n", k=src.shape[1]), src).then_inc(raw_in[i], 16)

            def up_source(j, i):
                wt = weights["w_up"].rearrange("(k p) c -> p k c", p=P)
                return wt[:, 8 * (i % 2):8 * (i % 2) + 8, bass.ds(j * 256 + (i // 2) * D_FF, 256)]

            def down_source(i, half):
                wt = weights["w_down"].rearrange("(k p) c -> p k c", p=P)
                return wt[:, bass.ds(i * 2, 2), 1024 * half:1024 * half + 1024]

            for t in range(TT):
                sp.dma_start(h[:, t, :], x[0, P * t:P * t + P, :]).then_inc(x_in[t], 16)
            for u, w in enumerate(units):
                wt = weights[w.w].rearrange("(k p) c -> p k c", p=P)
                load(0, u, wt[:, w.k0:w.k0 + w.nk, w.c0:w.c0 + w.nc])
                if u == 1:
                    sp.dma_start(wk(MTMP, TT, D), mem[0].rearrange("(t p) d -> p t d", p=P)).then_inc(mem_in, 16)
            with sp.Fori(0, UP_ITERS) as j:
                for i in range(4):
                    load(j, UP0 + i, up_source(j, i))
            with sp.Fori(0, HALF // 4) as j:
                for i in range(4):
                    load(j, DOWN0 + i, down_source(4 * j + i, 0))
            for i in range(4 * (HALF // 4), HALF):
                load(0, DOWN0 + i, down_source(i, 0))
            for i in range(HALF % 4):
                load(0, DOWN0 + HALF + i, down_source(i, 1))
            with sp.Fori(0, HALF // 4) as j:
                for i in range(HALF % 4, HALF % 4 + 4):
                    load(j, DOWN0 + HALF + i, down_source(4 * j + i, 1))
            sp.wait_ge(lo_done, 2 * GAIN - 2 * RAW + 2)
            gain = bass.AP(tensor=final_norm.tensor, offset=0, ap=[[0, P], [1, D]])
            sp.dma_start(raw[:, GAIN % RAW, :], gain).then_inc(raw_in[GAIN % RAW], 16)
            for i in range(4 * TT):
                c, t = i // TT, i % TT
                sp.wait_ge(out_ready, i + 1)
                sp.dma_start(out[0, P * t:P * t + P, 512 * c:512 * c + 512],
                             h[:, t, 512 * c:512 * c + 512]).then_inc(out_written, 16)
            sp.wait_ge(out_written, 16 * 4 * TT)

        @block.gpsimd
        def _(pool):
            G = nc.gpsimd
            n = [0]

            def step(ins):
                n[0] += 1
                ins.then_inc(pool_step, 1)
                pool.wait_ge(pool_step, n[0])

            step(G.memset(ident[:], 0.0))
            G.affine_select(out=ident[:], in_=ident[:], compare_op=ALU.not_equal, fill=1.0, base=0,
                            pattern=[[-1, P]], channel_multiplier=1).then_inc(c_ready, 1)
            step(G.memset(mhalf[:], -0.5))
            step(G.memset(ones[:], 1.0))
            step(G.memset(fox_mask[:], 0.0))
            step(G.memset(work[0:FOX, GR:GR + 512], 0.0))

            def rms(k, cols=TT):
                pool.wait_ge(meansq_ready, k + 1)
                step(G.tensor_scalar(meansq[:, 0:cols], meansq[:, 0:cols], EPS, None, ALU.add))
                G.tensor_tensor(rstd[:, 0:cols], meansq[:, 0:cols], mhalf[:, 0:cols], ALU.pow).then_inc(rstd_ready, 1)

            rms(0)
            for c in (0, 2):
                m = fox_mask[:, P * c:P * c + P]
                G.affine_select(out=m, in_=m, compare_op=ALU.is_ge, fill=NEG, base=0,
                                pattern=[[-1, P]], channel_multiplier=1).then_inc(c_ready, 1)
            G.affine_select(out=sel, in_=sel, compare_op=ALU.not_equal, fill=1.0, base=0,
                            pattern=[[-1, FOX], [0, P]], channel_multiplier=1).then_inc(c_ready, 1)
            pool.wait_ge(xn_a, 4)
            pool.wait_ge(xn_d, 4)
            rms(1)
            pool.wait_ge(bias_in, 16)
            G.affine_select(out=bias_m[:, :, 0, :], in_=bias_m[:, :, 1, :], compare_op=ALU.is_ge, fill=NEG,
                            base=0, pattern=[[0, SWA], [-1, P]], channel_multiplier=1).then_inc(bias_done, 1)
            pool.wait_ge(bias_done, 1)
            G.affine_select(out=bias_m[:, :, 1, :], in_=bias_m[:, :, 1, :], compare_op=ALU.is_gt, fill=NEG,
                            base=0, pattern=[[0, SWA], [1, P]], channel_multiplier=-1).then_inc(bias_done, 1)
            pool.wait_ge(bank_full[6], full[("head_o", FOX - 1), 6])
            G.memset(wk(FV, 1024), 0.0).then_inc(gla_p, 1)
            G.memset(wk(SQ, 1536), 0.0).then_inc(gla_p, 1)
            pool.wait_ge(gla_p, 2)
            pool.wait_ge(gla_a, 5)
            for half in range(2):
                for hh in range(GLA):
                    m = g_at[64 * half:64 * half + 64, hh, half::2, :]
                    ins = G.affine_select(out=m, in_=m, compare_op=ALU.is_ge, fill=0.0, base=0,
                                          pattern=[[0, NCH // 2], [1, CHUNK]], channel_multiplier=-1)
            ins.then_inc(gla_p, 1)
            pool.wait_ge(xn_a, 8)
            pool.wait_ge(xn_d, 8)
            rms(2, 8)
            pool.wait_ge(gla_d, 8)
            rms(3)
            for k in (4, 5):
                pool.wait_ge(xn_a, 4 * k - 4)
                pool.wait_ge(xn_d, 4 * k - 4)
                rms(k)

        @block.scalar
        def _(act):
            n = [0]

            def step(ins):
                n[0] += 1
                ins.then_inc(act_step, 1)
                act.wait_ge(act_step, n[0])

            def A(out_, in_, f=ACT.Copy, **kw):
                return nc.scalar.activation(out_, in_, f, **kw)

            def split_hi(j, c):
                act.wait_ge(raw_in[c % RAW], 16 * j + 16 * (c // RAW + 1))
                for s in range(2):
                    if 2 * c + s >= 4:
                        act.wait_ge(sub_used, 8 * j + (2 * c + s - 3))
                    A(wt_hi[:, (2 * c + s) % 4, :], raw[:, c % RAW, SUB * s:SUB * s + SUB]).then_inc(hi_done, 1)

            def norm_rows(k, c):
                A(work[:, XN_AT[k] + 512 * c:XN_AT[k] + 512 * c + 512],
                  norm_source(k, 0)[:, 512 * c:512 * c + 512], scale=rstd[:, 0:1]).then_inc(xn_a, 1)

            def norm_hi(k, m):
                b = 4 + m % 4
                act.wait_ge(bank_full[b], full[("norm_t", k, m), b])
                for i in range(2):
                    kk = 2 * m + i
                    ins = A(XT_OF[k][:, kk, 0:T], ps[:, b, T * i:T * i + T],
                            scale=prm[:, GAIN_ROW[k] + kk:GAIN_ROW[k] + kk + 1])
                ins.then_inc(xt_hi, 1)

            for dst, src in small_loads:
                act.dma_start(dst, src).then_inc(small_in, 16)
            nc.scalar.preload_act_table_set("natural_log_exp_and_others")
            act.wait_ge(x_in[0], 16)
            A(work[:, NTMP:NTMP + D], h[:, 0, :], ACT.Square, accum_out=sumsq[:, 0, 0:1]).then_inc(stats_a, 1)
            act.wait_ge(rstd_ready, 1)
            for c in range(4):
                norm_rows(0, c)
            split_hi(0, 0)
            act.wait_ge(prm_ready, 3)
            for m in range(8):
                norm_hi(0, m)
            split_hi(0, 1)
            act.wait_ge(mem_in, 16)
            for t in range(TT):
                A(xt["b"][:, 4 * t:4 * t + 4, :].rearrange("p a b -> p (a b)"), norm_source(1, t),
                  ACT.Square, accum_out=sumsq[:, t, 1:2]).then_inc(stats_a, 1)
            act.wait_ge(rstd_ready, 2)
            act.wait_ge(stats_a, 3)
            for c in range(4):
                norm_rows(1, c)
            repeated = bass.AP(tensor=bias_row.tensor, offset=bias_row.offset,
                               ap=[list(bias_row.ap[0]), [0, P], [1, P]])
            act.dma_start(bias_dram.rearrange("h (r y) -> h r y", y=P), repeated).then_inc(bias_out, 16)

            def wide_squares(base, half, nth):
                if half == 0 and nth > 4:
                    act.wait_ge(meansq_ready, (nth + 2) // 2)
                act.wait_ge(stats_a, nth - 1)
                for i in range(4):
                    c, t = i // TT, i % TT
                    col = 1024 * half + 512 * c
                    act.wait_ge(h_added, base + i + 1)
                    ins = A(junk, h[:, t, col:col + 512], ACT.Square, accum_out=sumsq[:, t, 2 * half + c:2 * half + c + 1])
                    if i < 3:
                        step(ins)
                ins.then_inc(stats_a, 1)

            def do(name, arg):
                if name == "evac_cols":
                    w, g = units[arg], cols_groups.index(arg)
                    act.wait_ge(sub_used, 2 * arg + 2)
                    if g >= 2:
                        act.wait_ge(proj_done, groups.index(cols_groups[g - 2]) + 1)
                    A(low[:, g % 2, :, :], ps[:, w.banks[0]:w.banks[0] + 2, T:2 * T], scale=w.scale).then_inc(low_ready, 1)
                elif name == "evac_wide":
                    wide_squares(chunk0[arg], units[arg].half, 4 + sorted(chunk0).index(arg))
                elif name == "mem_norm":
                    for m in (2 * arg, 2 * arg + 1):
                        norm_hi(1, m)
                elif name == "norm":
                    act.wait_ge(rstd_ready, arg + 2)
                    for c in range(4):
                        norm_rows(arg, c)
                elif name == "norm_t":
                    for m in range(8):
                        norm_hi(arg, m)
                elif name == "bias_load":
                    act.wait_ge(bias_out, 16)
                    src = bass.AP(tensor=bias_dram.tensor, offset=0, ap=[[P - 1, P], [P * P, SWA], [1, P]])
                    act.dma_start(bias_m[:, :, 1, :], src).then_inc(bias_in, 16)
                elif name == "gates_t":
                    act.wait_ge(gate_t_ready, 3)
                    step(A(f_e, f_e, ACT.Exp))
                    A(f_e, f_e, ACT.Ln, bias=1.0).then_inc(gate_a, 1)
                elif name == "head_s":
                    kind, i, a = arg
                    r = a % 3
                    act.wait_ge(scored, a + 1)
                    w0, w1 = (T, 2 * T) if kind == "x" else (P, 3 * P)
                    src = ps[:, 4, :] if kind == "x" else probs[:, r, :]
                    if kind == "swa":
                        A(sink_e[:, r, :], negmax[:, r, :], ACT.Exp, bias=sinks[:, i:i + 1])
                    A(probs[:, r, 0:w0], src[:, 0:w0], ACT.Exp, bias=negmax[:, r, 0:1], accum_out=den[:, r, 0:1])
                    A(probs[:, r, w0:w1], src[:, w0:w1], ACT.Exp, bias=negmax[:, r, 1:2],
                      accum_out=den[:, r, 1:2]).then_inc(exped, 1)
                elif name == "head_t":
                    kind, i, a = arg
                    act.wait_ge(bank_full[5], full[(name, a), 5])
                    if a >= 2 and kind != "x":
                        act.wait_ge(bank_full[6], full[("head_o", a - 2), 6])
                    w = 2 * T if kind == "x" else 3 * P
                    A(head_probs_t(arg)[:, 0:w], ps[:, 5, 0:w]).then_inc(pt_ready, 1)
                elif name == "head_o":
                    kind, i, a = arg
                    b = out_bank(arg)
                    act.wait_ge(bank_full[b], full[(name, a), b])
                    q = head_sources(arg)[0]
                    A(work[:, q:q + T], ps[:, b, 0:T]).then_inc(o_ready, 1)
                elif name == "gla_z":
                    act.wait_ge(gla_d, 1)
                    step(A(g_e, g_e, ACT.Exp))
                    A(g_e, g_e, ACT.Ln, bias=1.0).then_inc(gla_a, 1)
                elif name == "gla_decay":
                    act.wait_ge(gla_d, 2)
                    A(g_z, g_b, ACT.Exp).then_inc(gla_a, 1)
                    A(g_m, g_b, ACT.Exp, scale=-1.0).then_inc(gla_a, 1)
                elif name == "gla_scale":
                    act.wait_ge(gla_d, 3)
                    A(g_kend_t, g_kend_t, ACT.Exp).then_inc(gla_a, 1)
                elif name == "gla_scores":
                    act.wait_ge(gla_p, 1)
                    for par, b in ((0, 4), (1, 6)):
                        act.wait_ge(bank_full[b], full[name, b])
                        for half in range(2):
                            q = slice(64 * half, 64 * half + 64)
                            ins = A(g_at[q, par::2, half::2, :],
                                    ps[q, b, 0:256].rearrange("p (h m c) -> p h m c", h=2, m=2))
                    ins.then_inc(gla_a, 1)
                elif name == "gla_silu":
                    act.wait_ge(proj_done, PROJ["gr"])
                    nc.scalar.preload_act_table(ACT.Silu)
                    A(wk(GR, 1024), wk(GR, 1024), ACT.Silu).then_inc(gla_a, 1)
                    nc.scalar.preload_act_table_set("natural_log_exp_and_others")

            for u in range(len(units)):
                split_hi(0, u + LOOK)
                for name, arg in jobs.get(u, []):
                    do(name, arg)
                v = stationary_of(u)
                if v:
                    w = units[v]
                    for s in range(2):
                        k = 2 * wides.index(v) + s
                        tile = w.k0 + s
                        if w.w == "w_mix_out" and tile >= FOX + SWA:
                            act.wait_ge(gla_done, 1)
                        else:
                            act.wait_ge(o_ready, tile + 1 + (FOX + SWA if w.w == "wo_x" else 0))
                        act.wait_ge(sub_used, 2 * v + s - 3)
                        A(xt[w.ring][:, k % 4, 0:T], work[:, w.tiles[tile]:w.tiles[tile] + T]).then_inc(stat_hi, 1)

            nc.scalar.preload_act_table(ACT.Silu)

            def down_stat(j, c, k):
                for s in range(2):
                    act.wait_ge(sub_used, 8 * j + (2 * c + s - 3))
                    A(xt["b"][:, (2 * c + s) % 4, 0:T], act_t[:, bass.ds(j * (8 * T) + (k + s) * T, T)]).then_inc(stat_hi, 1)

            def up(j, last=False):
                for i in range(4):
                    split_hi(j, UP0 + i + LOOK)
                    if last and i >= 2:
                        act.wait_ge(act_done, 3)
                        down_stat(0, DOWN0 + i - 2, 2 * (i - 2))
                    if i % 2 == 0:
                        continue
                    side = i // 2
                    act.wait_ge(sub_used, 8 * j + (2 * (UP0 + i) + 2))
                    act.wait_ge(u_ready, 2 * j + (side + 1))
                    A(low[:, side, :, :], ps[:, 2 * side:2 * side + 2, T:2 * T]).then_inc(low_ready, 1)
                    act.wait_ge(u_ready, 2 * j + (side + 3))
                    act.wait_ge(act_done, j + 1)
                    for c in range(2):
                        ct = 2 * j + (FT * side + c)
                        ins = A(cv[:, 2 * side + c, :], u_pad[:, 2 * side + c, 2:2 + T], ACT.Identity,
                                scale=conv[:, 2, bass.ds(ct, 1)], bias=conv[:, 3, bass.ds(ct, 1)])
                    ins.then_inc(cv_init, 1)
                    if side == 1:
                        act.wait_ge(cv_done, 2 * j + 1)
                        A(cv[:, 0:2, :], cv[:, 0:2, :], ACT.Silu).then_inc(silu_done, 1)

            with act.Fori(0, UP_ITERS - 1) as j:
                up(j)
            up(UP_ITERS - 1, last=True)

            def down(j, x):
                for i in range(4):
                    split_hi(j, DOWN0 + x + i)
                    down_stat(j, DOWN0 + x + i, 2 * ((x + i) % HALF))

            with act.Fori(0, HALF // 4) as j:
                down(j, LOOK)
            for i in range(LOOK):
                split_hi(0, DOWN0 + HALF + i)
                down_stat(0, DOWN0 + HALF + i, 2 * i)
            wide_squares(DOWN_CHUNK0, 0, 8)
            with act.Fori(0, HALF // 4) as j:
                down(j, HALF + LOOK)
            wide_squares(DOWN_CHUNK0 + 4, 1, 9)

        @block.tensor
        def _(pe):
            n_stat = [0]

            def mm(out_, a, b, start, stop):
                return nc.tensor.matmul(out_, a, b, start=start, stop=stop, skip_group_check=True)

            def wait_bank(key, b):
                if free[key, b]:
                    pe.wait_ge(*free[key, b])

            def cols_sub(slot, k0, nk, first, last, banks, X):
                for kk in range(nk):
                    for c in range(2):
                        at, b, k = 256 * kk + P * c, banks[c], k0 + kk
                        hi, lo = wt_hi[:, slot, at:at + P], wt_lo[:, slot, at:at + P]
                        if last and kk == nk - 1:
                            mm(ps[:, b, T:2 * T], lo, X[:, k, 0:T], False, False)
                            ins = mm(ps[:, b, :], hi, X[:, k, :], False, True)
                        else:
                            mm(ps[:, b, :], hi, X[:, k, :], first and kk == 0, False)
                            ins = mm(ps[:, b, T:2 * T], lo, X[:, k, 0:T], False, False)
                ins.then_inc(sub_used, 1)

            def rows_sub(slot, k0, nk, ncols, first, last, banks, X):
                for kk in range(nk):
                    hi = wt_hi[:, slot, ncols * kk:ncols * kk + ncols]
                    lo = wt_lo[:, slot, ncols * kk:ncols * kk + ncols]
                    for t in range(TT):
                        x_hi, x_lo = X[:, k0 + kk, P * t:P * t + P], X[:, k0 + kk, T + P * t:T + P * t + P]
                        o = ps[:, banks[t], 0:ncols]
                        mm(o, x_hi, hi, first and kk == 0, False)
                        mm(o, x_hi, lo, False, False)
                        ins = mm(o, x_lo, hi, False, last and kk == nk - 1)
                ins.then_inc(sub_used, 1)

            def wide_sub(slot, xs, first, last, base, X):
                for t in range(TT):
                    x_hi, x_lo = X[:, xs, P * t:P * t + P], X[:, xs, T + P * t:T + P * t + P]
                    o = [ps[:, base + TT * c + t, :] for c in range(2)]
                    hi = [wt_hi[:, slot, 512 * c:512 * c + 512] for c in range(2)]
                    lo = [wt_lo[:, slot, 512 * c:512 * c + 512] for c in range(2)]
                    for c in range(2):
                        mm(o[c], x_hi, hi[c], first, False)
                    for c in range(2):
                        mm(o[c], x_hi, lo[c], False, False)
                    for c in range(2):
                        ins = mm(o[c], x_lo, hi[c], False, last)
                ins.then_inc(sub_used, 1)

            def do_unit(u):
                w = units[u]
                if w.first:
                    for b in w.banks:
                        if free["unit", u, b]:
                            pe.wait_ge(*free["unit", u, b])
                for s in range(2):
                    pe.wait_ge(lo_done, 2 * u + s + 1)
                    slot, nk = (2 * u + s) % 4, w.nk // 2
                    first, last = w.first and s == 0, w.last and s == 1
                    if w.kind == "wide":
                        n_stat[0] += 1
                        pe.wait_ge(stat_lo, n_stat[0])
                        wide_sub(slot, (n_stat[0] - 1) % 4, first, last, 4 * w.half, xt[w.ring])
                        continue
                    k0 = w.k0 + nk * s
                    before = 8 if w.xt == "b" else 0 if u < N_MIX else 16
                    pe.wait_ge(xt_ready, before + (k0 + nk) // 2)
                    if w.kind == "cols":
                        cols_sub(slot, k0, nk, first, last, w.banks, xt[w.xt])
                    else:
                        rows_sub(slot, k0, nk, w.nc, first, last, w.banks, xt[w.xt])

            def transpose_rows(k, m):
                b = 4 + m % 4
                pe.wait_ge(xn_a, 4 * k + m // 2 + 1)
                pe.wait_ge(xn_d, 4 * k + m // 2 + 1)
                wait_bank(("norm_t", k, m), b)
                for i in range(2):
                    for t in range(TT):
                        at = XN_AT[k] + D * t + P * (2 * m + i)
                        ins = nc.tensor.transpose(ps[:, b, T * i + P * t:T * i + P * t + P], work[:, at:at + P], ident[:])
                ins.then_inc(bank_full[b], 1)

            def do(name, arg):
                if name == "mem_norm":
                    for m in (2 * arg, 2 * arg + 1):
                        transpose_rows(1, m)
                elif name == "norm_t":
                    for m in range(8):
                        transpose_rows(arg, m)
                elif name == "gates_in":
                    wait_bank(name, 7)
                    for t in range(TT):
                        for k in range(KT):
                            for part in range(2):
                                at = T * part + P * t
                                ins = mm(ps[:, 7, 20 * t:20 * t + 20], xt["a"][:, k, at:at + P].bitcast(F32),
                                         gate_w_in[:, k, :], k == 0 and part == 0, k == KT - 1 and part == 1)
                    ins.then_inc(bank_full[7], 1)
                elif name == "gates_t":
                    pe.wait_ge(gate_nat_ready, 1)
                    for t in range(TT):
                        nc.tensor.transpose(ps[0:FOX, 7, P * t:P * t + P], gate_nat[:, t, 0:FOX], ident[:])
                        ins = nc.tensor.transpose(ps[0:GLA_RANK, 7, T + P * t:T + P * t + P],
                                                  gate_nat[:, t, FOX:20], ident[:])
                    ins.then_inc(bank_full[7], 1)
                elif name == "head_s":
                    kind, i, a = arg
                    q, k, _, need, _ = head_sources(arg)
                    pe.wait_ge(proj_done, need)
                    if kind == "fox":
                        pe.wait_ge(fox_ready, 1)
                    wait_bank((name, a), 4)
                    for qb, o, w in ((0, 0, T), (1, T, T)) if kind == "x" else ((0, 0, P), (1, P, T)):
                        dst = ps[:, 4, o:o + w]
                        ins = mm(dst, work[:, q + P * qb:q + P * qb + P], work[:, k:k + w], True, kind != "fox")
                        if kind == "fox":
                            mm(dst, c_sel[:, i, P * qb:P * qb + P], ones[0:FOX, 0:w], False, False)
                            ins = mm(dst, sel[:, i, :], neg_c[:, 0:w], False, True)
                    ins.then_inc(bank_full[4], 1)
                elif name == "head_t":
                    kind, i, a = arg
                    pe.wait_ge(normed, a + 1)
                    wait_bank((name, a), 5)
                    if kind == "x":
                        moves = [(T * qb + P * kb, T * kb + P * qb) for qb in range(2) for kb in range(2)]
                    else:
                        moves = [(P * c, P * c) for c in range(3)]
                    for src, dst in moves:
                        ins = nc.tensor.transpose(ps[:, 5, dst:dst + P], probs[:, a % 3, src:src + P], ident[:])
                    ins.then_inc(bank_full[5], 1)
                elif name == "head_o":
                    kind, i, a = arg
                    _, _, v, _, need = head_sources(arg)
                    pe.wait_ge(pt_ready, a + 1)
                    pe.wait_ge(proj_done, need)
                    b, pt = out_bank(arg), head_probs_t(arg)
                    wait_bank((name, a), b)
                    mm(ps[:, b, 0:T], v[:, 0, :], pt[:, 0:T], True, False)
                    if kind == "x":
                        ins = mm(ps[:, b, 0:T], v[:, 1, :], pt[:, T:2 * T], False, True)
                    else:
                        ins = mm(ps[:, b, P:T], v[:, 1, :], pt[:, T:3 * P], False, True)
                    ins.then_inc(bank_full[b], 1)
                elif name == "gla_z":
                    wait_bank(name, 7)
                    for c in range(2):
                        ins = mm(ps[:, 7, T * c:T * c + T], gla_w[:, P * c:P * c + P], glr_t, True, True)
                    ins.then_inc(bank_full[7], 1)
                elif name == "gla_scores":
                    pe.wait_ge(gla_d, 4)
                    wait_bank(name, 7)
                    for t in range(TT):
                        for c in range(2):
                            ins = nc.tensor.transpose(ps[:, 7, T * t + P * c:T * t + P * c + P],
                                                      g_kend_t[:, T * c + P * t:T * c + P * t + P], ident[:])
                    ins.then_inc(bank_full[7], 1)
                    for par, b in ((0, 4), (1, 6)):
                        wait_bank(name, b)
                        rows = slice(64 * par, 64 * par + 64)
                        for hh in range(par, GLA, 2):
                            for c in range(NCH):
                                tok = T * (hh // 2) + CHUNK * c
                                col = 128 * (hh // 2) + 64 * (c // 2)
                                ins = mm(ps[64 * (c % 2):64 * (c % 2) + 64, b, col:col + 64],
                                         work[rows, GK + tok:GK + tok + 64], work[rows, GQ + tok:GQ + tok + 64],
                                         True, True)
                        ins.then_inc(bank_full[b], 1)
                elif name == "gla_kv":
                    pe.wait_ge(gla_d, 5)
                    pe.wait_ge(proj_done, PROJ["gv"])
                    gv = wk(GV, TT, 512)
                    for b, some in ((4, (0, 2)), (7, (1,))):
                        wait_bank(name, b)
                        for c in some:
                            tok = slice(64 * (c % 2), 64 * (c % 2) + 64)
                            for hh in range(GLA):
                                col = T * (c // 2) + P * (hh // 2)
                                ins = mm(ps[64 * (hh % 2):64 * (hh % 2) + 64, b, col:col + P],
                                         g_kend[tok, c // 2, 64 * hh:64 * hh + 64],
                                         gv[tok, c // 2, P * hh:P * hh + P], True, True)
                        ins.then_inc(bank_full[b], 1)
                elif name == "gla_out":
                    pe.wait_ge(gla_d, 6)
                    pe.wait_ge(gla_p, 3)
                    gv = wk(GV, TT, 512)
                    for t, b in ((0, 6), (1, 7)):
                        wait_bank(name, b)
                        for c in (2 * t, 2 * t + 1):
                            half = 64 * (c % 2)
                            for hh in range(GLA):
                                o = ps[half:half + 64, b, P * hh:P * hh + P]
                                ins = mm(o, g_at[:, hh, c, :], gv[:, t, P * hh:P * hh + P], True, c == 0)
                                if c:
                                    tok = GQ + T * (hh // 2) + CHUNK * c
                                    ins = mm(o, work[:, tok:tok + 64], g_s[:, hh, c - 1, :], False, True)
                        ins.then_inc(bank_full[b], 1)
                elif name == "gla_o":
                    pe.wait_ge(gla_d, 8)
                    for b in (6, 7):
                        wait_bank(name, b)
                        for i in range(2):
                            hh = 2 * (b - 6) + i
                            for t in range(TT):
                                ins = nc.tensor.transpose(ps[:, b, T * i + P * t:T * i + P * t + P],
                                                          g_o[:, t, P * hh:P * hh + P], ident[:])
                        ins.then_inc(bank_full[b], 1)

            pe.wait_ge(small_in, 16 * N_SMALL)
            pe.wait_ge(c_ready, 1)
            nc.tensor.transpose(ps[:, 4, 0:NPRM], rows_prm, ident[0:NPRM, 0:NPRM])
            mm(ps[0:SWA, 4, P:2 * P], t5_sb, onehot_sb, True, True).then_inc(bank_full[4], 1)
            for i in range(4):
                ins = nc.tensor.transpose(ps[:, 5, 2 * FT * i:2 * FT * i + 2 * FT], rows_conv[:, i, :],
                                          ident[0:2 * FT, 0:2 * FT])
            ins.then_inc(bank_full[5], 1)
            for m in range(8):
                transpose_rows(0, m)
            for u in range(len(units)):
                do_unit(u)
                for name, arg in jobs.get(u, []):
                    do(name, arg)

            def up(j):
                for i in range(4):
                    if i % 2 == 0:
                        if isinstance(j, int) and j == 0:
                            for b in (i, i + 1):
                                pe.wait_ge(*up_free[b])
                        else:
                            pe.wait_ge(u_ready, 2 * j + (i // 2 + 1))
                    for s in range(2):
                        pe.wait_ge(lo_done, 8 * j + (2 * (UP0 + i) + s + 1))
                        if isinstance(j, int) and j == 0:
                            pe.wait_ge(xt_ready, 24 + 4 * (i % 2) + 2 * s + 2)
                        cols_sub((2 * i + s) % 4, 8 * (i % 2) + 4 * s, 4, i % 2 == 0 and s == 0,
                                 i % 2 == 1 and s == 1, [i // 2 * 2, i // 2 * 2 + 1], xt["a"])

            up(0)
            with pe.Fori(1, UP_ITERS) as j:
                up(j)

            def down(j, x, n, first=False, last=False):
                for i in range(n):
                    for s in range(2):
                        pe.wait_ge(lo_done, 8 * j + (2 * (DOWN0 + x + i) + s + 1))
                        pe.wait_ge(stat_lo, 8 * j + (STAT0 + 2 * (x + i) + s + 1))
                        slot = (2 * (x + i) + s) % 4
                        wide_sub(slot, slot, first and i == 0 and s == 0, last and i == n - 1 and s == 1,
                                 4 * (x // HALF), xt["b"])

            pe.wait_ge(u_ready, 2 + 2 * UP_ITERS)
            down(0, 0, 4, first=True)
            with pe.Fori(1, HALF // 4) as j:
                down(j, 0, 4)
            down(0, 4 * (HALF // 4), HALF % 4, last=True)
            for b in range(4, 8):
                pe.wait_ge(*down_free[b])
            down(0, HALF, HALF % 4, first=True)
            with pe.Fori(0, HALF // 4 - 1) as j:
                down(j, HALF + HALF % 4, 4)
            down(HALF // 4 - 1, HALF + HALF % 4, 4, last=True)

        @block.vector
        def _(dve):
            V = nc.vector
            n = [0]

            def step(ins):
                n[0] += 1
                ins.then_inc(dve_step, 1)
                dve.wait_ge(dve_step, n[0])

            def split_lo(j, c):
                for s in range(2):
                    dve.wait_ge(hi_done, 8 * j + (2 * c + s + 1))
                    V.tensor_tensor(wt_lo[:, (2 * c + s) % 4, :], raw[:, c % RAW, SUB * s:SUB * s + SUB],
                                    wt_hi[:, (2 * c + s) % 4, :].bitcast(F32), ALU.subtract).then_inc(lo_done, 1)

            def norm_rows(k, c):
                at = XN_AT[k] + D + 512 * c
                V.tensor_scalar(work[:, at:at + 512], norm_source(k, 1)[:, 512 * c:512 * c + 512], rstd[:, 1:2],
                                None, ALU.mult).then_inc(xn_d, 1)

            def norm_lo(k, m):
                b, X = 4 + m % 4, XT_OF[k]
                dve.wait_ge(xt_hi, 8 * k + m + 1)
                for i in range(2):
                    kk = 2 * m + i
                    ins = V.scalar_tensor_tensor(X[:, kk, T:2 * T], ps[:, b, T * i:T * i + T],
                                                 prm[:, GAIN_ROW[k] + kk:GAIN_ROW[k] + kk + 1],
                                                 X[:, kk, 0:T].bitcast(F32), ALU.mult, ALU.subtract)
                ins.then_inc(xt_ready, 1)

            def mean_squares(n_norm):
                step(V.tensor_reduce(meansq[:, 0:TT], sumsq[:], AX.X, ALU.add))
                V.tensor_scalar(meansq[:, 0:TT], meansq[:, 0:TT], 1.0 / D, None, ALU.mult).then_inc(meansq_ready, 1)
                dve.wait_ge(rstd_ready, n_norm + 1)

            def wide_add(base, half, subs):
                dve.wait_ge(sub_used, subs)
                for i in range(4):
                    c, t = i // TT, i % TT
                    col = 1024 * half + 512 * c
                    V.tensor_tensor(h[:, t, col:col + 512], h[:, t, col:col + 512], ps[:, 4 * half + i, :],
                                    ALU.add).then_inc(h_added, 1)

            dve.wait_ge(x_in[1], 16)
            V.tensor_tensor_reduce(out=work[:, NTMP + D:NTMP + 2 * D], in0=h[:, 1, :], in1=h[:, 1, :], scale=1.0,
                                   scalar=0.0, op0=ALU.mult, op1=ALU.add, accum_out=sumsq[:, 1, 0:1]).then_inc(stats_d, 1)
            dve.wait_ge(stats_d, 1)
            dve.wait_ge(stats_a, 1)
            V.tensor_scalar(meansq[:, 0:TT], sumsq[:, :, 0], 1.0 / D, None, ALU.mult).then_inc(meansq_ready, 1)
            dve.wait_ge(rstd_ready, 1)
            for c in range(4):
                norm_rows(0, c)
            dve.wait_ge(bank_full[4], 1)
            V.tensor_copy(prm[:], ps[:, 4, 0:NPRM]).then_inc(prm_ready, 1)
            V.tensor_copy(bias_row, ps[0:SWA, 4, P:2 * P]).then_inc(prm_ready, 1)
            dve.wait_ge(bank_full[5], 1)
            V.tensor_copy(conv[:].rearrange("p a b -> p (a b)"), ps[:, 5, 0:8 * FT]).then_inc(prm_ready, 1)
            split_lo(0, 0)
            for m in range(8):
                norm_lo(0, m)
            split_lo(0, 1)
            dve.wait_ge(stats_a, 3)
            V.tensor_scalar(meansq[:, 0:TT], sumsq[:, :, 1], 1.0 / D, None, ALU.mult).then_inc(meansq_ready, 1)
            dve.wait_ge(rstd_ready, 2)
            for c in range(4):
                norm_rows(1, c)
            dve.wait_ge(small_in, 16 * N_SMALL)

            def do(name, arg):
                if name == "evac_cols":
                    w, g = units[arg], cols_groups.index(arg)
                    b = w.banks[0]
                    dve.wait_ge(low_ready, g + 1)
                    V.scalar_tensor_tensor(wk(w.dest, 2, T), ps[:, b:b + 2, 0:T], w.scale, low[:, g % 2, :, :],
                                           ALU.mult, ALU.add).then_inc(proj_done, 1)
                elif name == "evac_rows":
                    w = units[arg]
                    b = w.banks[0]
                    dve.wait_ge(sub_used, 2 * arg + 2)
                    V.tensor_copy(wk(w.dest, TT, w.nc), ps[:, b:b + 2, 0:w.nc]).then_inc(proj_done, 1)
                elif name == "evac_wide":
                    wide_add(chunk0[arg], units[arg].half, 2 * arg + 2)
                elif name == "mem_norm":
                    for m in (2 * arg, 2 * arg + 1):
                        norm_lo(1, m)
                elif name == "norm":
                    dve.wait_ge(stats_a, 2 * arg + 1)
                    mean_squares(arg + 1)
                    for c in range(4):
                        norm_rows(arg, c)
                elif name == "norm_t":
                    for m in range(8):
                        norm_lo(arg, m)
                elif name == "gates_in":
                    dve.wait_ge(bank_full[7], full[name, 7])
                    V.tensor_copy(gate_nat, ps[:, 7, 0:40].rearrange("p (t n) -> p t n", t=TT)).then_inc(gate_nat_ready, 1)
                elif name == "gates_t":
                    dve.wait_ge(bank_full[7], full[name, 7])
                    V.tensor_copy(glr_t, ps[0:GLA_RANK, 7, T:2 * T]).then_inc(gate_t_ready, 1)
                    V.tensor_scalar(f_z, ps[0:FOX, 7, 0:T], b_fox[:], None, ALU.add).then_inc(gate_t_ready, 1)
                    dve.wait_ge(gate_t_ready, 2)
                    step(V.tensor_scalar(f_m, f_z, 0.0, None, ALU.min))
                    V.scalar_tensor_tensor(f_e, f_m, 2.0, f_z, ALU.mult, ALU.subtract).then_inc(gate_t_ready, 1)
                elif name == "fox_gates":
                    dve.wait_ge(gate_a, 1)
                    dve.wait_ge(c_ready, 4)
                    step(V.tensor_tensor(f_m, f_m, f_e, ALU.subtract))
                    step(V.tensor_tensor_scan(f_z, ones[0:FOX, :], f_m, 0.0, ALU.mult, ALU.add))
                    V.tensor_scalar(neg_c, f_z, -1.0, None, ALU.mult)
                    for i in range(FOX):
                        ins = V.tensor_scalar(c_sel[:, i, :], f_z, sel[:, i, 0:1], None, ALU.mult)
                    ins.then_inc(fox_ready, 1)
                elif name == "head_s":
                    kind, i, a = arg
                    r = a % 3
                    dve.wait_ge(bank_full[4], full[(name, a), 4])
                    if a == 0:
                        dve.wait_ge(bias_out, 16)
                    if a >= 3:
                        dve.wait_ge(bank_full[5], full[("head_t", a - 3), 5])
                    w0, w1 = (T, 2 * T) if kind == "x" else (P, 3 * P)
                    src = ps[:, 4, :] if kind == "x" else probs[:, r, :]
                    if kind == "fox":
                        step(V.tensor_tensor(probs[:, r, 0:w1], ps[:, 4, 0:w1], fox_mask[:], ALU.add))
                    if kind == "swa":
                        dve.wait_ge(bias_done, 2)
                        V.tensor_tensor(probs[:, r, 0:T], ps[:, 4, 0:T], bias_m[:, i, :, :].rearrange("p m k -> p (m k)"),
                                        ALU.add)
                        step(V.tensor_tensor(probs[:, r, T:w1], ps[:, 4, T:w1], bias_m[:, i, 0, :], ALU.add))
                    V.tensor_reduce(rowmax[:, r, 0:1], src[:, 0:w0], AX.X, ALU.max)
                    step(V.tensor_reduce(rowmax[:, r, 1:2], src[:, w0:w1], AX.X, ALU.max))
                    if kind == "swa":
                        V.tensor_scalar(negmax[:, r, :], rowmax[:, r, :], sinks[:, i:i + 1], -1.0, ALU.max,
                                        ALU.mult).then_inc(scored, 1)
                    else:
                        V.tensor_scalar(negmax[:, r, :], rowmax[:, r, :], -1.0, None, ALU.mult).then_inc(scored, 1)
                elif name == "head_n":
                    kind, i, a = arg
                    r = a % 3
                    dve.wait_ge(exped, a + 1)
                    w0, w1 = (T, 2 * T) if kind == "x" else (P, 3 * P)
                    if kind == "swa":
                        step(V.tensor_tensor(den[:, r, :], den[:, r, :], sink_e[:, r, :], ALU.add))
                    step(V.reciprocal(rden[:, r, :], den[:, r, :]))
                    V.tensor_scalar(probs[:, r, 0:w0], probs[:, r, 0:w0], rden[:, r, 0:1], None, ALU.mult)
                    V.tensor_scalar(probs[:, r, w0:w1], probs[:, r, w0:w1], rden[:, r, 1:2], None,
                                    ALU.mult).then_inc(normed, 1)
                elif name == "gla_z":
                    dve.wait_ge(bank_full[7], full[name, 7])
                    dve.wait_ge(bank_full[4], full[("head_s", FOX - 1), 4])
                    for c in range(2):
                        ins = V.tensor_scalar(g_z[:, T * c:T * c + T], ps[:, 7, T * c:T * c + T],
                                              prm[:, B_GATE + c:B_GATE + c + 1], None, ALU.add)
                    step(ins)
                    step(V.tensor_scalar(g_m, g_z, 0.0, None, ALU.min))
                    V.scalar_tensor_tensor(g_e, g_m, 2.0, g_z, ALU.mult, ALU.subtract).then_inc(gla_d, 1)
                elif name == "gla_decay":
                    dve.wait_ge(gla_a, 1)
                    step(V.tensor_tensor(g_m, g_m, g_e, ALU.subtract))
                    step(V.tensor_scalar(g_m, g_m, 1.0 / 16.0, None, ALU.mult))
                    for c in range(2 * NCH):
                        at = slice(CHUNK * c, CHUNK * c + CHUNK)
                        ins = V.tensor_tensor_scan(g_b[:, at], ones[:, 0:CHUNK], g_m[:, at], 0.0, ALU.mult, ALU.add)
                    ins.then_inc(gla_d, 1)
                elif name == "gla_scale":
                    dve.wait_ge(bank_full[6], full[("head_o", FOX - 1), 6])
                    dve.wait_ge(gla_d, 2)
                    b4 = g_b.rearrange("p (n c) -> p n c", c=CHUNK)
                    V.tensor_tensor(g_kend_t.rearrange("p (n c) -> p n c", c=CHUNK),
                                    b4[:, :, CHUNK - 1:CHUNK].broadcast_to([P, 2 * NCH, CHUNK]), b4,
                                    ALU.subtract).then_inc(gla_d, 1)
                    dve.wait_ge(gla_a, 4)
                    dve.wait_ge(proj_done, PROJ["gq"])
                    step(V.tensor_tensor(g_kend_t, g_kend_t, wk(GK, 512), ALU.mult))
                    V.tensor_tensor(wk(GK, 512), wk(GK, 512), g_m, ALU.mult)
                    V.tensor_tensor(wk(GQ, 512), wk(GQ, 512), g_z, ALU.mult).then_inc(gla_d, 1)
                elif name == "gla_scores":
                    dve.wait_ge(bank_full[7], full[name, 7])
                    V.tensor_copy(g_kend, ps[:, 7, :].rearrange("p (t n) -> p t n", t=TT)).then_inc(gla_d, 1)
                elif name == "gla_kv":
                    dve.wait_ge(gla_p, 2)
                    dve.wait_ge(bank_full[4], full[name, 4])
                    dve.wait_ge(bank_full[7], full[name, 7])
                    for par in range(2):
                        rows = slice(64 * par, 64 * par + 64)
                        ins = V.tensor_copy(g_s[rows, par::2, 0, :], ps[rows, 4, 0:T].rearrange("p (h n) -> p h n", h=2))
                    step(ins)
                    for c, b, at in ((1, 7, 0), (2, 4, T)):
                        for par in range(2):
                            rows = slice(64 * par, 64 * par + 64)
                            for i in range(2):
                                last = T * i + CHUNK * c + CHUNK - 1
                                ins = V.scalar_tensor_tensor(g_s[rows, 2 * i + par, c, :], g_s[rows, 2 * i + par, c - 1, :],
                                                             g_z[rows, last:last + 1],
                                                             ps[rows, b, at + P * i:at + P * i + P], ALU.mult, ALU.add)
                        if c == 1:
                            step(ins)
                    ins.then_inc(gla_d, 1)
                elif name == "gla_out":
                    dve.wait_ge(bank_full[6], full[name, 6])
                    dve.wait_ge(bank_full[7], full[name, 7])
                    V.tensor_copy(g_o, ps[:, 6:8, :]).then_inc(gla_d, 1)
                elif name == "gla_rms":
                    dve.wait_ge(gla_d, 7)
                    step(V.tensor_tensor(g_sq, g_o, g_o, ALU.mult))
                    step(V.tensor_reduce(meansq[:, 0:8], g_sq.rearrange("p t (h n) -> p (t h) n", n=GLA_DV), AX.X, ALU.add))
                    V.tensor_scalar(meansq[:, 0:8], meansq[:, 0:8], 1.0 / GLA_DV, None, ALU.mult).then_inc(meansq_ready, 1)
                elif name == "gla_norm":
                    dve.wait_ge(rstd_ready, 3)
                    o8 = g_o.rearrange("p t (h n) -> p (t h) n", n=GLA_DV)
                    V.tensor_tensor(o8, o8, rstd[:, 0:8].unsqueeze(2).broadcast_to([P, 8, GLA_DV]),
                                    ALU.mult).then_inc(gla_d, 1)
                elif name == "gla_o":
                    dve.wait_ge(gla_a, 6)
                    for b in (6, 7):
                        dve.wait_ge(bank_full[b], full[name, b])
                        at = 512 * (b - 6)
                        ins = V.scalar_tensor_tensor(wk(FK + at, 512), ps[:, b, :], prm[:, G_GLA:G_GLA + 1],
                                                     wk(GR + at, 512), ALU.mult, ALU.mult)
                    ins.then_inc(gla_done, 1)

            for u in range(len(units)):
                split_lo(0, u + LOOK)
                for name, arg in jobs.get(u, []):
                    do(name, arg)
                v = stationary_of(u)
                if v:
                    w = units[v]
                    for s in range(2):
                        k, at = 2 * wides.index(v) + s, w.tiles[w.k0 + s]
                        dve.wait_ge(stat_hi, k + 1)
                        V.tensor_tensor(xt[w.ring][:, k % 4, T:2 * T], work[:, at:at + T],
                                        xt[w.ring][:, k % 4, 0:T].bitcast(F32), ALU.subtract).then_inc(stat_lo, 1)

            def down_stat(j, c, k):
                for s in range(2):
                    dve.wait_ge(stat_hi, 8 * j + (STAT0 + 2 * (c - DOWN0) + s + 1))
                    X = xt["b"][:, (2 * c + s) % 4, :]
                    V.tensor_tensor(X[:, T:2 * T], act_t[:, bass.ds(j * (8 * T) + (k + s) * T, T)],
                                    X[:, 0:T].bitcast(F32), ALU.subtract).then_inc(stat_lo, 1)

            V.memset(u_pad[:, :, 0:2], 0.0).then_inc(act_done, 1)
            dve.wait_ge(act_done, 1)
            V.tensor_copy(rden[:, 0, :], rstd[:, 0:2]).then_inc(u_ready, 1)
            V.tensor_copy(rden[:, 1, :], rstd[:, 0:2]).then_inc(u_ready, 1)

            def up(j, last=False):
                for i in range(4):
                    split_lo(j, UP0 + i + LOOK)
                    if last and i >= 2:
                        down_stat(0, DOWN0 + i - 2, 2 * (i - 2))
                    if i % 2 == 0:
                        continue
                    side = i // 2
                    mine = slice(2 * side, 2 * side + 2)
                    dve.wait_ge(low_ready, 2 * j + (n_low + side + 1))
                    V.tensor_tensor(u_pad[:, mine, 2:2 + T], ps[:, mine, 0:T], low[:, side, :, :], ALU.add).then_inc(u_ready, 1)
                    dve.wait_ge(cv_init, 2 * j + (side + 1))
                    for tap, done in ((1, cv_tap), (0, cv_done)):
                        for c in range(2):
                            x2 = 2 * side + c
                            ct = 2 * j + (FT * side + c)
                            ins = V.scalar_tensor_tensor(cv[:, x2, :], u_pad[:, x2, tap:tap + T],
                                                         conv[:, tap, bass.ds(ct, 1)], cv[:, x2, :], ALU.mult, ALU.add)
                        ins.then_inc(done, 1)
                        dve.wait_ge(done, 2 * j + (side + 1))
                dve.wait_ge(silu_done, j + 1)
                V.tensor_tensor(act_t[:, bass.ds(j * (2 * T), 2 * T)].rearrange("p (a b) -> p a b", a=2), cv[:, 0:2, :],
                                cv[:, 2:4, :], ALU.mult).then_inc(act_done, 1)

            with dve.Fori(0, UP_ITERS - 1) as j:
                up(j)
            up(UP_ITERS - 1, last=True)

            def down(j, x):
                for i in range(4):
                    split_lo(j, DOWN0 + x + i)
                    down_stat(j, DOWN0 + x + i, 2 * ((x + i) % HALF))

            with dve.Fori(0, HALF // 4) as j:
                down(j, LOOK)
            for i in range(LOOK):
                split_lo(0, DOWN0 + HALF + i)
                down_stat(0, DOWN0 + HALF + i, 2 * i)
            wide_add(DOWN_CHUNK0, 0, 2 * (DOWN0 + HALF))
            with dve.Fori(0, HALF // 4) as j:
                down(j, HALF + LOOK)
            wide_add(DOWN_CHUNK0 + 4, 1, 2 * (DOWN0 + 2 * HALF))
            dve.wait_ge(stats_a, 9)
            mean_squares(5)
            dve.wait_ge(raw_in[GAIN % RAW], 16 * (GAIN // RAW + 1))
            for c in range(4):
                for t in range(TT):
                    y = h[:, t, 512 * c:512 * c + 512]
                    V.scalar_tensor_tensor(y, y, rstd[:, t:t + 1], raw[:, GAIN % RAW, 512 * c:512 * c + 512],
                                           ALU.mult, ALU.mult).then_inc(out_ready, 1)


_INS = ["x", "mem", "w_in", "b_fox_f", "swa_sinks", "t5_bias", "w_gla_gate", "b_gla_gate", "gla_norm", "w_mix_out",
        "norm_mix", "norm_xattn", "norm_mem", "wq_x", "wkv_x", "wo_x", "norm_ffn", "w_up", "conv_w", "conv_b",
        "w_down", "final_norm"]


def kernel(**inputs):
    import concourse.bacc as bacc
    from concourse.bass_utils import run_bass_kernel_spmd

    nc = bacc.Bacc("TRN2", target_bir_lowering=False, num_devices=1)
    arrays, args = {}, []
    for name in _INS + ["t5_onehot"]:
        a = onehot_table() if name == "t5_onehot" else np.ascontiguousarray(inputs[name])
        arrays[f"in_{name}"] = a
        args.append(nc.dram_tensor(f"in_{name}", a.shape, mybir.dt.from_np(a.dtype), kind="ExternalInput").ap())
    out = nc.dram_tensor("out_y", inputs["x"].shape, F32, kind="ExternalOutput").ap()
    trunk(nc, *args, out)
    r = run_bass_kernel_spmd(nc, [arrays], core_ids=[0])
    return r.results[0]["out_y"]
```

```python
from contextlib import ExitStack

import numpy as np

import concourse.bass as bass
from concourse import mybir

F32 = mybir.dt.float32
F32R = mybir.dt.float32r
ACT = mybir.ActivationFunctionType
ALU = mybir.AluOpType
AX = mybir.AxisListType

P = 128
D = 2048
T = 256
TT = T // P
KT = D // P
HD = 128
FOX, SWA, SWA_KV, GLA, XH = 4, 8, 2, 4, 4
GLA_DK, GLA_DV, GLA_RANK, CHUNK = 64, 128, 16, 64
NCH = T // CHUNK
D_FF = 5632
FT = D_FF // P
NBUCKET, MAXDIST = 32, 128
EPS = 1e-6
SCALE = float(HD) ** -0.5
NEG = -1.0e30
UNIT = 2048
SUB = UNIT // 2
RAW = 4
LOOK = 2

WIN = {}
_at = 0
for _n, _w in (("fq", FOX * HD), ("fk", FOX * HD), ("fv", FOX * HD), ("ff", FOX), ("sq", SWA * HD),
               ("sk", SWA_KV * HD), ("sv", SWA_KV * HD), ("gq", GLA * GLA_DK), ("gk", GLA * GLA_DK),
               ("gv", GLA * GLA_DV), ("gr", GLA * GLA_DV), ("glr", GLA_RANK)):
    WIN[_n] = _at
    _at += _w

FQ, FK, SQ, SK, GQ, GK, GR = 0, 1024, 2048, 4096, 4608, 5120, 5632
FV, SV, GV, MK, MV = 6656, 7680, 8192, 9216, 10240
WORK = 11264
NTMP = 0
MTMP = 7168
BIAS = 9216
XQ = 4096
GLR_AT = 32
GATES = GLR_AT + GLA_RANK
G_MIX, G_X, G_MEM, G_FFN, B_GATE, G_GLA, NPRM = 0, 16, 32, 48, 64, 66, 67


class Unit:

    def __init__(self, kind, w, k0, nk, c0, nc, first, last, dest=0, scale=1.0, xt="a", half=0, tiles=(), ring=None):
        self.kind, self.w, self.k0, self.nk, self.c0, self.nc = kind, w, k0, nk, c0, nc
        self.first, self.last = first, last
        self.dest, self.scale, self.xt = dest, scale, xt
        self.half, self.tiles, self.ring = half, tiles, ring
        self.banks = []


def plan():
    units, jobs = [], {}

    def job(slot, name, arg=None):
        jobs.setdefault(slot, []).append((name, arg))

    def cols(w, c0, ncols, dest, scale, xt):
        for c in range(0, ncols, 256):
            for half in range(2):
                units.append(Unit("cols", w, 8 * half, 8, c0 + c, 256, half == 0, half == 1,
                                  dest=dest + c * T // P, scale=scale, xt=xt))

    def rows(w, c0, ncols, dest, xt):
        nk = UNIT // ncols
        for k in range(0, KT, nk):
            units.append(Unit("rows", w, k, nk, c0, ncols, k == 0, k + nk == KT, dest=dest, xt=xt))

    def wide(w, order, tiles, ring):
        for half in range(2):
            for i, k in enumerate(order):
                units.append(Unit("wide", w, k, 2, 1024 * half, 1024, i == 0, i == len(order) - 1,
                                  half=half, tiles=tiles, ring=ring))

    cols("w_in", WIN["fk"], 512, FK, 1.0, "a")
    rows("w_in", WIN["fv"], 512, FV, "a")
    cols("w_in", WIN["fq"], 512, FQ, SCALE, "a")
    cols("w_in", WIN["gk"], 256, GK, 1.0, "a")
    cols("w_in", WIN["gq"], 256, GQ, float(GLA_DK) ** -0.5, "a")
    rows("w_in", WIN["gv"], 512, GV, "a")
    cols("w_in", WIN["gr"], 512, GR, 1.0, "a")
    cols("w_in", WIN["sk"], 256, SK, 1.0, "a")
    rows("w_in", WIN["sv"], 256, SV, "a")
    cols("w_in", WIN["sq"], 1024, SQ, SCALE, "a")
    tiles = [FQ + T * h for h in range(FOX)] + [SQ + T * h for h in range(SWA)] + [FK + T * h for h in range(GLA)]
    n_mix = len(units)
    wide("w_mix_out", [0, 2, 12, 14, 4, 6, 8, 10], tiles, "a")
    n_mk = len(units)
    cols("wkv_x", 0, 512, MK, 1.0, "b")
    n_wq = len(units)
    cols("wq_x", 0, 512, XQ, SCALE, "a")
    rows("wkv_x", 512, 512, MV, "b")
    n_wo = len(units)
    wide("wo_x", [0, 2], [XQ + T * h for h in range(XH)], "b")
    n_up = len(units)

    group = 0
    for u, x in enumerate(units):
        if x.kind == "wide":
            x.banks = [4 * x.half + i for i in range(4)]
        if x.first and x.kind != "wide":
            pair = group % 2
            group += 1
        if x.kind != "wide":
            x.banks = [2 * pair, 2 * pair + 1]
        if x.last:
            job(u, "evac_" + x.kind, u)
    job(2, "mem_squares")
    job(2, "tables")
    job(3, "mem_rows")
    job(3, "gates_split")
    job(4, "norm_t", (1, 0, 3))
    job(5, "norm_t", (1, 3, 6))
    job(5, "gates")
    job(6, "norm_t", (1, 6, 8))
    job(7, "fox_gates")
    job(8, "bias_load")
    for h in range(FOX):
        heads(job, ("fox", h, h), 10 + h)
    job(14, "gla_z")
    job(15, "gla_decay")
    job(17, "gla_scale")
    job(18, "gla_scores")
    job(20, "gla_kv")
    job(22, "gla_out")
    job(23, "gla_rms")
    job(24, "gla_norm")
    job(24, "gla_silu")
    job(25, "gla_o")
    for h in range(SWA):
        heads(job, ("swa", h, FOX + h), n_mix - 6 + h)
    job(n_mix + 15, "norm", 2)
    job(n_mix + 17, "norm_t", (2, 0, 4))
    job(n_mix + 18, "norm_t", (2, 4, 8))
    for h, slot in enumerate((n_wq + 2, n_wq + 2, n_wq + 4, n_wq + 4)):
        heads(job, ("x", h, FOX + SWA + h), slot, n_wo - 1)
    job(n_up - 1, "norm", 3)
    job(n_up - 1, "norm_t", (3, 0, 8))
    stages = ["head_o", "head_t", "head_n", "head_s"]
    for some in jobs.values():
        some.sort(key=lambda x: 0 if x[0].startswith("evac") else 1 + stages.index(x[0]) if x[0] in stages else 9)
    early = {}
    for u, some in jobs.items():
        early[u] = [x for x in some if u in (n_wo - 1, n_up - 1) or x[0] in ("evac_cols", "evac_rows")]
    late = {u: [x for x in some if x not in early[u]] for u, some in jobs.items()}
    return units, jobs, early, late, n_mix, n_wo, n_up


def heads(job, head, slot, out_slot=None):
    for i, stage in enumerate(("head_s", "head_n", "head_t")):
        job(slot + i, stage, head)
    job(out_slot or slot + 3, "head_o", head)


def bucket(n):
    half = NBUCKET // 2
    if n < half:
        return n
    big = half + int(np.float32(np.log(np.float32(n) / np.float32(half)))
                     / np.float32(np.log(MAXDIST / half)) * np.float32(NBUCKET - half))
    return min(big, NBUCKET - 1)


def onehot_table():
    t = np.zeros((NBUCKET, P), np.float32)
    for y in range(P):
        t[bucket((-y) % P), y] = 1.0
    return t


def trunk(nc, x, mem, w_in, b_fox_f, swa_sinks, t5_bias, w_gla_gate, b_gla_gate, gla_norm, w_mix_out,
          norm_mix, norm_xattn, norm_mem, wq_x, wkv_x, wo_x, norm_ffn, w_up, conv_w, conv_b, w_down,
          final_norm, t5_onehot, out):
    weights = {"w_in": w_in[0], "w_mix_out": w_mix_out[0], "wkv_x": wkv_x[0], "wq_x": wq_x[0], "wo_x": wo_x[0],
               "w_up": w_up[0], "w_down": w_down[0]}
    units, jobs, early, late, N_MIX, WO0, UP0 = plan()
    UP_ITERS = FT // 2
    DOWN0 = UP0 + 4 * UP_ITERS
    HALF = FT // 2
    GAIN = DOWN0 + 2 * HALF
    assert UP0 % RAW == 0 and DOWN0 % RAW == 0 and HALF % RAW == 2

    ctx = ExitStack()
    with ctx:
        def sb(name, shape, dt=F32):
            return ctx.enter_context(nc.sbuf_tensor("sb_" + name, shape, dt))

        def sem(name):
            return ctx.enter_context(nc.semaphore(name))

        raw = sb("raw", [P, RAW, UNIT])
        wt_hi = sb("wt_hi", [P, 4, SUB], F32R)
        wt_lo = sb("wt_lo", [P, 4, SUB], F32R)
        xt = {"a": sb("xt_a", [P, KT, 2 * T], F32R), "b": sb("xt_b", [P, KT, 2 * T], F32R)}
        h = sb("h", [P, TT, D])
        work = sb("work", [P, WORK])
        att = sb("att", [P, 2560])
        low = sb("low", [P, 2, 2, T])
        ident = sb("ident", [P, P])
        prm = sb("prm", [P, NPRM])
        conv = sb("conv", [P, 4, 2 * FT])
        fox_mask = sb("fox_mask", [P, 3 * P])
        ones = sb("ones", [P, T])
        sumsq = sb("sumsq", [P, TT, 4])
        meansq = sb("meansq", [P, 8])
        rstd = sb("rstd", [P, 8])
        mhalf = sb("mhalf", [P, 8])
        negmax = sb("negmax", [P, 3, 2])
        rowmax = sb("rowmax", [P, 3, 2])
        den = sb("den", [P, 3, 2])
        sink_e = sb("sink_e", [P, 3, 2])
        rden = sb("rden", [P, 3, 2])
        sinks = sb("sinks", [P, SWA])
        b_fox = sb("b_fox", [FOX, 1])
        ps = ctx.enter_context(nc.psum_tensor("ps", [P, 8, 512], F32))
        bias_dram = nc.dram_tensor("bias_rows", [SWA, P * P], F32, kind="Internal").ap()

        def wk(at, *shape):
            n = int(np.prod(shape))
            v = work[:, at:at + n]
            if len(shape) == 2:
                v = v.rearrange("p (a b) -> p a b", b=shape[1])
            if len(shape) == 3:
                v = v.rearrange("p (a b c) -> p a b c", b=shape[1], c=shape[2])
            return v

        probs = att[:, 0:1536].rearrange("p (r n) -> p r n", r=3)
        probs_t = att[:, 1536:2560].rearrange("p (r n) -> p r n", r=2)
        rows_prm = att[0:NPRM, 0:P]
        rows_conv = att[0:2 * FT, P:P + 512].rearrange("p (a b) -> p a b", a=4)
        t5_sb = att[0:NBUCKET, 640:640 + SWA]
        onehot_sb = att[0:NBUCKET, 656:656 + P]
        bias_row = att[0:SWA, 784:784 + P]
        gate_w_in = att[:, 1024:1024 + KT * GATES].rearrange("p (k n) -> p k n", n=GATES)
        gate_parts = xt["b"][:, KT - 3:KT, :].rearrange("p a b -> p (a b)").rearrange("p (i k n) -> p i k n", i=2, n=GATES)
        glr_rows = slice(GLR_AT, GLR_AT + GLA_RANK)
        gla_w = work[glr_rows, SK:SK + GLA * GLA_DK]
        sel = work[0:FOX, GR:GR + 512].rearrange("p (h n) -> p h n", h=FOX)
        glr_t = work[glr_rows, GR + 512:GR + 768]
        c_sel = work[0:FOX, SQ:SQ + 1024].rearrange("p (h n) -> p h n", h=FOX)
        neg_c = work[0:FOX, SQ + 1024:SQ + 1280]
        f_z = work[0:FOX, SQ + 1280:SQ + 1536]
        f_m = work[0:FOX, SQ + 1536:SQ + 1792]
        f_e = work[0:FOX, SQ + 1792:SQ + 2048]
        g_z = wk(SV, 512)
        g_m = wk(SK, 512)
        g_b = wk(SQ + 1536, 512)
        g_e = wk(GR, 512)
        g_kend_t = probs_t[:, 0, :]
        g_kend = probs_t[:, 1, :].rearrange("p (t n) -> p t n", t=TT)
        g_at = wk(FV, GLA, NCH, CHUNK)
        g_s = wk(SQ, GLA, NCH - 1, GLA_DV)
        g_o = att[:, 0:1024].rearrange("p (t n) -> p t n", t=TT)
        g_sq = att[:, 1536:2560].rearrange("p (t n) -> p t n", t=TT)
        bias_m = work[:, BIAS:BIAS + 2048].rearrange("p (h m k) -> p h m k", h=SWA, m=2)
        junk = att[:, 1024:1536]
        u_pad = att[:, 0:4 * (T + 2)].rearrange("p (i n) -> p i n", i=4)
        cv = att[:, 1032:1032 + 4 * T].rearrange("p (i n) -> p i n", i=4)
        act_t = work[:, :]

        raw_in = [sem(f"raw_in{i}") for i in range(RAW)]
        hi_done = sem("hi_done")
        lo_done = sem("lo_done")
        sub_used = sem("sub_used")
        stat_hi = sem("stat_hi")
        stat_lo = sem("stat_lo")
        bank_full = {b: sem(f"bank_full{b}") for b in range(4, 8)}
        low_ready = sem("low_ready")
        proj_done = sem("proj_done")
        x_in = [sem(f"x_in{t}") for t in range(TT)]
        mem_in = sem("mem_in")
        prm_in = sem("prm_in")
        small_in = sem("small_in")
        c_ready = sem("c_ready")
        pool_step = sem("pool_step")
        dve_step = sem("dve_step")
        act_step = sem("act_step")
        prm_ready = sem("prm_ready")
        bias_out = sem("bias_out")
        bias_in = sem("bias_in")
        bias_done = sem("bias_done")
        stats_a = sem("stats_a")
        stats_d = sem("stats_d")
        h_added = sem("h_added")
        meansq_ready = sem("meansq_ready")
        rstd_ready = sem("rstd_ready")
        xn_a = sem("xn_a")
        xn_d = sem("xn_d")
        xt_hi = sem("xt_hi")
        xt_ready = sem("xt_ready")
        scored = sem("scored")
        exped = sem("exped")
        normed = sem("normed")
        pt_ready = sem("pt_ready")
        o_ready = sem("o_ready")
        gate_zero = sem("gate_zero")
        gate_split = sem("gate_split")
        gate_t_ready = sem("gate_t_ready")
        gate_a = sem("gate_a")
        fox_ready = sem("fox_ready")
        gla_d = sem("gla_d")
        gla_a = sem("gla_a")
        gla_p = sem("gla_p")
        gla_done = sem("gla_done")
        u_ready = sem("u_ready")
        cv_init = sem("cv_init")
        cv_tap = sem("cv_tap")
        cv_done = sem("cv_done")
        silu_done = sem("silu_done")
        act_done = sem("act_done")
        out_ready = sem("out_ready")
        out_written = sem("out_written")

        STAT0 = sum(2 for w in units if w.kind == "wide")
        wides = [u for u, w in enumerate(units) if w.kind == "wide"]
        groups = [u for u, w in enumerate(units) if w.last and w.kind != "wide"]
        cols_groups = [u for u in groups if units[u].kind == "cols"]
        n_proj, n_low = len(groups), len(cols_groups)
        PROJ = {"fv": 3, "fq": 5, "gk": 6, "gq": 7, "gv": 8, "gr": 10, "sv": 12, "sq": 16, "xq": 20, "mv": 21}
        assert n_proj == PROJ["mv"]
        reader = {4: (prm_ready, 1)}
        free = {}
        full = {}
        fills = {b: 0 for b in range(4, 8)}
        fills[4] = 1

        def score_bank(head):
            return 7 if head[0] == "x" and head[1] % 2 else 4

        def probs_bank(head):
            return 6 if head[0] == "x" and head[1] % 2 else 5

        def out_bank(head):
            return 7 if head[0] == "x" and head[1] % 2 else 6

        def head_probs_t(head):
            kind, i, a = head
            return wk(NTMP + 2 * T * i, 2 * T) if kind == "x" else probs_t[:, a % 2, :]

        def wide_bank(i):
            return 2 * (i % TT) + i // TT

        def take(key, b, semaphore, count):
            free[key, b] = reader.get(b)
            reader[b] = (semaphore, count)
            if b >= 4:
                fills[b] += 1
                full[key, b] = fills[b]

        for m in range(8):
            take(("norm_t", 0, m), 4 + m % 4, xt_ready, m + 1)
        chunks = 0
        chunk0 = {}
        for u, w in enumerate(units):
            if w.first and w.kind == "wide":
                for i in range(4):
                    b = w.banks[0] + wide_bank(i)
                    free["unit", u, b] = reader.get(b)
                    reader[b] = (h_added, chunks + i + 1)
                last = next(v for v in range(u, len(units)) if units[v].last)
                chunk0[last] = chunks
                chunks += 4
            elif w.first:
                last = next(v for v in range(u, len(units)) if units[v].last)
                for b in w.banks:
                    free["unit", u, b] = reader.get(b)
                    reader[b] = (proj_done, groups.index(last) + 1)
            for name, arg in jobs.get(u, []):
                if name == "norm_t":
                    for m in range(arg[1], arg[2]):
                        take((name, arg[0], m), 4 + m % 4, xt_ready, 8 * arg[0] + m + 1)
                elif name == "tables":
                    take(name, 4, prm_ready, 2)
                    take(name, 5, prm_ready, 3)
                elif name == "gates":
                    take(name, 7, gate_t_ready, 2)
                elif name == "gla_z":
                    take(name, 7, gla_d, 1)
                elif name == "gla_scores":
                    take(name, 7, gla_d, 5)
                    take(name, 4, gla_a, 5)
                    take(name, 6, gla_a, 5)
                elif name == "gla_kv":
                    take(name, 4, gla_d, 6)
                    take(name, 7, gla_d, 6)
                elif name == "gla_out":
                    take(name, 6, gla_d, 7)
                    take(name, 7, gla_d, 7)
                elif name == "gla_o":
                    take(name, 6, gla_done, 1)
                    take(name, 7, gla_done, 1)
                elif name == "head_s":
                    take((name, arg[2]), score_bank(arg), exped if arg[0] == "x" else scored, arg[2] + 1)
                elif name == "head_t":
                    take((name, arg[2]), probs_bank(arg), pt_ready, arg[2] + 1)
                elif name == "head_o":
                    take((name, arg[2]), out_bank(arg), o_ready, arg[2] + 1)
        down_free = {b: reader[b] for b in range(4, 8)}
        up_free = {b: reader[b] for b in range(4)}
        DOWN_CHUNK0 = chunks

        def stationary_of(u):
            if u == WO0 - 1:
                return [WO0, WO0 + 1]
            return [v for v in [u + LOOK] if v < len(units) and units[v].kind == "wide" and v != WO0]

        def head_sources(head):
            kind, i, _ = head
            if kind == "fox":
                v = wk(FV, TT, 512)[:, :, HD * i:HD * i + HD]
                return FQ + T * i, FK + T * i, v, PROJ["fq"] - 1 + i // 2, PROJ["fv"]
            if kind == "swa":
                g = i // (SWA // SWA_KV)
                v = wk(SV, TT, 256)[:, :, HD * g:HD * g + HD]
                return SQ + T * i, SK + T * g, v, PROJ["sq"] - 3 + i // 2, PROJ["sv"]
            v = wk(MV, TT, 512)[:, :, HD * i:HD * i + HD]
            return XQ + T * i, MK + T * i, v, PROJ["xq"] - 1 + i // 2, PROJ["mv"]

        XN_AT = [NTMP, MTMP, NTMP, NTMP]
        GAIN_ROW = [G_MIX, G_MEM, G_X, G_FFN]
        XT_OF = [xt["a"], xt["b"], xt["a"], xt["a"]]

        def norm_source(k, t):
            return work[:, MTMP + D * t:MTMP + D * t + D] if k == 1 else h[:, t, :]

        prm_loads = (
            (rows_prm[G_MIX:G_MIX + 16], norm_mix[0].rearrange("(k p) -> k p", p=P)),
            (rows_prm[G_X:G_X + 16], norm_xattn[0].rearrange("(k p) -> k p", p=P)),
            (rows_prm[G_MEM:G_MEM + 16], norm_mem[0].rearrange("(k p) -> k p", p=P)),
            (rows_prm[G_FFN:G_FFN + 16], norm_ffn[0].rearrange("(k p) -> k p", p=P)),
            (rows_prm[B_GATE:B_GATE + 2], b_gla_gate[0].rearrange("(k p) -> k p", p=P)),
            (rows_prm[G_GLA:G_GLA + 1], gla_norm),
        )
        small_loads = (
            (rows_conv[:, 0:3, :], conv_w[0].rearrange("j (k p) -> k j p", p=P)),
            (rows_conv[:, 3, :], conv_b[0].rearrange("(k p) -> k p", p=P)),
            (t5_sb, t5_bias),
            (onehot_sb, t5_onehot),
            (sinks[:], bass.AP(tensor=swa_sinks.tensor, offset=0, ap=[[0, P], [1, SWA]])),
            (b_fox[:], bass.AP(tensor=b_fox_f.tensor, offset=0, ap=[[1, FOX], [1, 1]])),
            (gla_w, w_gla_gate[0]),
            (gate_w_in[:, :, 0:FOX],
             weights["w_in"].rearrange("(k p) c -> p k c", p=P)[:, :, WIN["ff"]:WIN["ff"] + FOX]),
            (gate_w_in[:, :, GLR_AT:GATES],
             weights["w_in"].rearrange("(k p) c -> p k c", p=P)[:, :, WIN["glr"]:WIN["glr"] + GLA_RANK]),
        )
        N_PRM, N_SMALL = len(prm_loads), len(small_loads)

        block = ctx.enter_context(nc.Block())


        @block.sync
        def _(sp):
            def load(j, c, src):
                if c >= RAW:
                    sp.wait_ge(lo_done, 8 * j + (2 * c - 2 * RAW + 2))
                i = c % RAW
                sp.dma_start(raw[:, i, :].rearrange("p (k n) -> p k n", k=src.shape[1]), src).then_inc(raw_in[i], 16)

            def up_source(j, i):
                wt = weights["w_up"].rearrange("(k p) c -> p k c", p=P)
                return wt[:, 8 * (i % 2):8 * (i % 2) + 8, bass.ds(j * 256 + (i // 2) * D_FF, 256)]

            def down_source(i, half):
                wt = weights["w_down"].rearrange("(k p) c -> p k c", p=P)
                return wt[:, bass.ds(i * 2, 2), 1024 * half:1024 * half + 1024]

            for t in range(TT):
                sp.dma_start(h[:, t, :], x[0, P * t:P * t + P, :]).then_inc(x_in[t], 16)
            sp.wait_ge(prm_in, 16 * N_PRM)
            for u, w in enumerate(units):
                wt = weights[w.w].rearrange("(k p) c -> p k c", p=P)
                load(0, u, wt[:, w.k0:w.k0 + w.nk, w.c0:w.c0 + w.nc])
                if u == 3:
                    sp.dma_start(wk(MTMP, TT, D), mem[0].rearrange("(t p) d -> p t d", p=P)).then_inc(mem_in, 16)
                if u == 2:
                    sp.wait_ge(gate_zero, 1)
                    for dst, src in small_loads:
                        sp.dma_start(dst, src).then_inc(small_in, 16)
            with sp.Fori(0, UP_ITERS) as j:
                for i in range(4):
                    load(j, UP0 + i, up_source(j, i))
            with sp.Fori(0, HALF // 4) as j:
                for i in range(4):
                    load(j, DOWN0 + i, down_source(4 * j + i, 0))
            for i in range(4 * (HALF // 4), HALF):
                load(0, DOWN0 + i, down_source(i, 0))
            for i in range(HALF % 4):
                load(0, DOWN0 + HALF + i, down_source(i, 1))
            with sp.Fori(0, HALF // 4) as j:
                for i in range(HALF % 4, HALF % 4 + 4):
                    load(j, DOWN0 + HALF + i, down_source(4 * j + i, 1))
            sp.wait_ge(lo_done, 2 * GAIN - 2 * RAW + 2)
            gain = bass.AP(tensor=final_norm.tensor, offset=0, ap=[[0, P], [1, D]])
            sp.dma_start(raw[:, GAIN % RAW, :], gain).then_inc(raw_in[GAIN % RAW], 16)
            for i in range(4 * TT):
                c, t = i // TT, i % TT
                sp.wait_ge(out_ready, i + 1)
                sp.dma_start(out[0, P * t:P * t + P, 512 * c:512 * c + 512],
                             h[:, t, 512 * c:512 * c + 512]).then_inc(out_written, 16)
            sp.wait_ge(out_written, 16 * 4 * TT)

        @block.gpsimd
        def _(pool):
            G = nc.gpsimd
            n = [0]

            def step(ins):
                n[0] += 1
                ins.then_inc(pool_step, 1)
                pool.wait_ge(pool_step, n[0])

            step(G.memset(ident[:], 0.0))
            G.affine_select(out=ident[:], in_=ident[:], compare_op=ALU.not_equal, fill=1.0, base=0,
                            pattern=[[-1, P]], channel_multiplier=1).then_inc(c_ready, 1)
            G.memset(att[:, 1024:1024 + KT * GATES], 0.0).then_inc(gate_zero, 1)
            step(G.memset(mhalf[:], -0.5))
            step(G.memset(ones[:], 1.0))
            step(G.memset(fox_mask[:], 0.0))
            step(G.memset(work[0:FOX, GR:GR + 512], 0.0))

            def rms(k, cols=TT):
                pool.wait_ge(meansq_ready, k + 1)
                step(G.tensor_scalar(meansq[:, 0:cols], meansq[:, 0:cols], EPS, None, ALU.add))
                G.tensor_tensor(rstd[:, 0:cols], meansq[:, 0:cols], mhalf[:, 0:cols], ALU.pow).then_inc(rstd_ready, 1)

            rms(0)
            for c in (0, 2):
                m = fox_mask[:, P * c:P * c + P]
                G.affine_select(out=m, in_=m, compare_op=ALU.is_ge, fill=NEG, base=0,
                                pattern=[[-1, P]], channel_multiplier=1).then_inc(c_ready, 1)
            G.affine_select(out=sel, in_=sel, compare_op=ALU.not_equal, fill=1.0, base=0,
                            pattern=[[-1, FOX], [0, P]], channel_multiplier=1).then_inc(c_ready, 1)
            pool.wait_ge(xn_a, 4)
            pool.wait_ge(xn_d, 4)
            rms(1)
            pool.wait_ge(bias_in, 16)
            G.affine_select(out=bias_m[:, :, 0, :], in_=bias_m[:, :, 1, :], compare_op=ALU.is_ge, fill=NEG,
                            base=0, pattern=[[0, SWA], [-1, P]], channel_multiplier=1).then_inc(bias_done, 1)
            pool.wait_ge(bias_done, 1)
            G.affine_select(out=bias_m[:, :, 1, :], in_=bias_m[:, :, 1, :], compare_op=ALU.is_gt, fill=NEG,
                            base=0, pattern=[[0, SWA], [1, P]], channel_multiplier=-1).then_inc(bias_done, 1)
            pool.wait_ge(bank_full[6], full[("head_o", FOX - 1), 6])
            G.memset(wk(FV, 1024), 0.0).then_inc(gla_p, 1)
            G.memset(wk(SQ, 1536), 0.0).then_inc(gla_p, 1)
            pool.wait_ge(gla_p, 2)
            pool.wait_ge(gla_a, 5)
            for half in range(2):
                for hh in range(GLA):
                    m = g_at[64 * half:64 * half + 64, hh, half::2, :]
                    ins = G.affine_select(out=m, in_=m, compare_op=ALU.is_ge, fill=0.0, base=0,
                                          pattern=[[0, NCH // 2], [1, CHUNK]], channel_multiplier=-1)
            ins.then_inc(gla_p, 1)
            pool.wait_ge(xn_a, 8)
            pool.wait_ge(xn_d, 8)
            rms(2, 8)
            pool.wait_ge(gla_d, 8)
            rms(3)
            for k in (4, 5):
                pool.wait_ge(xn_a, 4 * k - 4)
                pool.wait_ge(xn_d, 4 * k - 4)
                rms(k)

        @block.scalar
        def _(act):
            n = [0]

            def step(ins):
                n[0] += 1
                ins.then_inc(act_step, 1)
                act.wait_ge(act_step, n[0])

            def A(out_, in_, f=ACT.Copy, **kw):
                return nc.scalar.activation(out_, in_, f, **kw)

            def split_hi(j, c, subs=(0, 1)):
                if 0 in subs:
                    act.wait_ge(raw_in[c % RAW], 16 * j + 16 * (c // RAW + 1))
                for s in subs:
                    if 2 * c + s >= 4:
                        act.wait_ge(sub_used, 8 * j + (2 * c + s - 3))
                    A(wt_hi[:, (2 * c + s) % 4, :], raw[:, c % RAW, SUB * s:SUB * s + SUB]).then_inc(hi_done, 1)

            def norm_rows(k, c):
                A(work[:, XN_AT[k] + 512 * c:XN_AT[k] + 512 * c + 512],
                  norm_source(k, 0)[:, 512 * c:512 * c + 512], scale=rstd[:, 0:1]).then_inc(xn_a, 1)

            def norm_hi(k, m):
                b = 4 + m % 4
                act.wait_ge(bank_full[b], full[("norm_t", k, m), b])
                for i in range(2):
                    kk = 2 * m + i
                    ins = A(XT_OF[k][:, kk, 0:T], ps[:, b, T * i:T * i + T],
                            scale=prm[:, GAIN_ROW[k] + kk:GAIN_ROW[k] + kk + 1])
                ins.then_inc(xt_hi, 1)

            for dst, src in prm_loads:
                act.dma_start(dst, src).then_inc(prm_in, 16)
            nc.scalar.preload_act_table_set("natural_log_exp_and_others")
            act.wait_ge(x_in[0], 16)
            A(work[:, NTMP:NTMP + D], h[:, 0, :], ACT.Square, accum_out=sumsq[:, 0, 0:1]).then_inc(stats_a, 1)
            act.wait_ge(rstd_ready, 1)
            for c in range(4):
                norm_rows(0, c)
            split_hi(0, 0, [0])
            act.wait_ge(prm_ready, 1)
            for s in range(2):
                if s:
                    split_hi(0, 0, [1])
                for m in range(4 * s, 4 * s + 4):
                    norm_hi(0, m)
            split_hi(0, 1)

            def wide_squares(base, half, nth):
                if half == 0 and nth > 4:
                    act.wait_ge(meansq_ready, (nth + 2) // 2)
                act.wait_ge(stats_a, nth - 1)
                for i in range(4):
                    c, t = i // TT, i % TT
                    col = 1024 * half + 512 * c
                    act.wait_ge(h_added, base + i + 1)
                    ins = A(junk, h[:, t, col:col + 512], ACT.Square, accum_out=sumsq[:, t, 2 * half + c:2 * half + c + 1])
                    if i < 3:
                        step(ins)
                ins.then_inc(stats_a, 1)

            def do(name, arg):
                if name == "evac_cols":
                    w, g = units[arg], cols_groups.index(arg)
                    act.wait_ge(sub_used, 2 * arg + 2)
                    if g >= 2:
                        act.wait_ge(proj_done, groups.index(cols_groups[g - 2]) + 1)
                    A(low[:, g % 2, :, :], ps[:, w.banks[0]:w.banks[0] + 2, T:2 * T], scale=w.scale).then_inc(low_ready, 1)
                elif name == "evac_wide":
                    wide_squares(chunk0[arg], units[arg].half, 4 + sorted(chunk0).index(arg))
                elif name == "mem_squares":
                    act.wait_ge(mem_in, 16)
                    for t in range(TT):
                        A(xt["b"][:, 4 * t:4 * t + 4, :].rearrange("p a b -> p (a b)"), norm_source(1, t),
                          ACT.Square, accum_out=sumsq[:, t, 1:2]).then_inc(stats_a, 1)
                elif name == "mem_rows":
                    act.wait_ge(rstd_ready, 2)
                    act.wait_ge(stats_a, 3)
                    for c in range(4):
                        norm_rows(1, c)
                elif name == "tables":
                    act.wait_ge(prm_ready, 2)
                    repeated = bass.AP(tensor=bias_row.tensor, offset=bias_row.offset,
                                       ap=[list(bias_row.ap[0]), [0, P], [1, P]])
                    act.dma_start(bias_dram.rearrange("h (r y) -> h r y", y=P), repeated).then_inc(bias_out, 16)
                elif name == "norm":
                    act.wait_ge(rstd_ready, arg + 2)
                    for c in range(4):
                        norm_rows(arg, c)
                elif name == "norm_t":
                    for m in range(arg[1], arg[2]):
                        norm_hi(arg[0], m)
                elif name == "bias_load":
                    act.wait_ge(bias_out, 16)
                    src = bass.AP(tensor=bias_dram.tensor, offset=0, ap=[[P - 1, P], [P * P, SWA], [1, P]])
                    act.dma_start(bias_m[:, :, 1, :], src).then_inc(bias_in, 16)
                elif name == "gates_split":
                    act.wait_ge(small_in, 16 * N_SMALL)
                    A(gate_parts[:, 0], gate_w_in).then_inc(gate_split, 1)
                elif name == "gates":
                    act.wait_ge(gate_t_ready, 3)
                    step(A(f_e, f_e, ACT.Exp))
                    A(f_e, f_e, ACT.Ln, bias=1.0).then_inc(gate_a, 1)
                elif name == "head_s":
                    kind, i, a = arg
                    r = a % 3
                    act.wait_ge(scored, a + 1)
                    w0, w1 = (T, 2 * T) if kind == "x" else (P, 3 * P)
                    src = ps[:, score_bank(arg), :] if kind == "x" else probs[:, r, :]
                    if kind == "swa":
                        A(sink_e[:, r, :], negmax[:, r, :], ACT.Exp, bias=sinks[:, i:i + 1])
                    A(probs[:, r, 0:w0], src[:, 0:w0], ACT.Exp, bias=negmax[:, r, 0:1], accum_out=den[:, r, 0:1])
                    A(probs[:, r, w0:w1], src[:, w0:w1], ACT.Exp, bias=negmax[:, r, 1:2],
                      accum_out=den[:, r, 1:2]).then_inc(exped, 1)
                elif name == "head_t":
                    kind, i, a = arg
                    b = probs_bank(arg)
                    act.wait_ge(bank_full[b], full[(name, a), b])
                    if a >= 2 and kind != "x":
                        act.wait_ge(bank_full[6], full[("head_o", a - 2), 6])
                    w = 2 * T if kind == "x" else 3 * P
                    A(head_probs_t(arg)[:, 0:w], ps[:, b, 0:w]).then_inc(pt_ready, 1)
                elif name == "head_o":
                    kind, i, a = arg
                    b = out_bank(arg)
                    act.wait_ge(bank_full[b], full[(name, a), b])
                    q = head_sources(arg)[0]
                    A(work[:, q:q + T], ps[:, b, 0:T]).then_inc(o_ready, 1)
                elif name == "gla_z":
                    act.wait_ge(gla_d, 1)
                    step(A(g_e, g_e, ACT.Exp))
                    A(g_e, g_e, ACT.Ln, bias=1.0).then_inc(gla_a, 1)
                elif name == "gla_decay":
                    act.wait_ge(gla_d, 2)
                    A(g_z, g_b, ACT.Exp).then_inc(gla_a, 1)
                    A(g_m, g_b, ACT.Exp, scale=-1.0).then_inc(gla_a, 1)
                elif name == "gla_scale":
                    act.wait_ge(gla_d, 3)
                    A(g_kend_t, g_kend_t, ACT.Exp).then_inc(gla_a, 1)
                elif name == "gla_scores":
                    act.wait_ge(gla_p, 1)
                    for par, b in ((0, 4), (1, 6)):
                        act.wait_ge(bank_full[b], full[name, b])
                        for half in range(2):
                            q = slice(64 * half, 64 * half + 64)
                            ins = A(g_at[q, par::2, half::2, :],
                                    ps[q, b, 0:256].rearrange("p (h m c) -> p h m c", h=2, m=2))
                    ins.then_inc(gla_a, 1)
                elif name == "gla_silu":
                    act.wait_ge(proj_done, PROJ["gr"])
                    nc.scalar.preload_act_table(ACT.Silu)
                    A(wk(GR, 1024), wk(GR, 1024), ACT.Silu).then_inc(gla_a, 1)
                    nc.scalar.preload_act_table_set("natural_log_exp_and_others")

            def stationary_hi(v):
                w = units[v]
                for s in range(2):
                    k = 2 * wides.index(v) + s
                    tile = w.k0 + s
                    if w.w == "w_mix_out" and tile >= FOX + SWA:
                        act.wait_ge(gla_done, 1)
                    else:
                        act.wait_ge(o_ready, tile + 1 + (FOX + SWA if w.w == "wo_x" else 0))
                    act.wait_ge(sub_used, 2 * v + s - 3)
                    A(xt[w.ring][:, k % 4, 0:T], work[:, w.tiles[tile]:w.tiles[tile] + T]).then_inc(stat_hi, 1)

            for u in range(len(units)):
                split_hi(0, u + LOOK, [0])
                for name, arg in early.get(u, []):
                    do(name, arg)
                if u == WO0 - 1:
                    for v in stationary_of(u):
                        stationary_hi(v)
                split_hi(0, u + LOOK, [1])
                if u != WO0 - 1:
                    for v in stationary_of(u):
                        stationary_hi(v)
                for name, arg in late.get(u, []):
                    do(name, arg)

            nc.scalar.preload_act_table(ACT.Silu)

            def down_stat(j, c, k):
                for s in range(2):
                    act.wait_ge(sub_used, 8 * j + (2 * c + s - 3))
                    A(xt["b"][:, (2 * c + s) % 4, 0:T], act_t[:, bass.ds(j * (8 * T) + (k + s) * T, T)]).then_inc(stat_hi, 1)

            def up(j, last=False):
                for i in range(4):
                    split_hi(j, UP0 + i + LOOK)
                    if last and i >= 2:
                        act.wait_ge(act_done, 3)
                        down_stat(0, DOWN0 + i - 2, 2 * (i - 2))
                    if i % 2 == 0:
                        continue
                    side = i // 2
                    act.wait_ge(sub_used, 8 * j + (2 * (UP0 + i) + 2))
                    act.wait_ge(u_ready, 2 * j + (side + 1))
                    A(low[:, side, :, :], ps[:, 2 * side:2 * side + 2, T:2 * T]).then_inc(low_ready, 1)
                    act.wait_ge(u_ready, 2 * j + (side + 3))
                    act.wait_ge(act_done, j + 1)
                    for c in range(2):
                        ct = 2 * j + (FT * side + c)
                        ins = A(cv[:, 2 * side + c, :], u_pad[:, 2 * side + c, 2:2 + T], ACT.Identity,
                                scale=conv[:, 2, bass.ds(ct, 1)], bias=conv[:, 3, bass.ds(ct, 1)])
                    ins.then_inc(cv_init, 1)
                    if side == 1:
                        act.wait_ge(cv_done, 2 * j + 1)
                        A(cv[:, 0:2, :], cv[:, 0:2, :], ACT.Silu).then_inc(silu_done, 1)

            with act.Fori(0, UP_ITERS - 1) as j:
                up(j)
            up(UP_ITERS - 1, last=True)

            def down(j, x):
                for i in range(4):
                    split_hi(j, DOWN0 + x + i)
                    down_stat(j, DOWN0 + x + i, 2 * ((x + i) % HALF))

            with act.Fori(0, HALF // 4) as j:
                down(j, LOOK)
            for i in range(LOOK):
                split_hi(0, DOWN0 + HALF + i)
                down_stat(0, DOWN0 + HALF + i, 2 * i)
            wide_squares(DOWN_CHUNK0, 0, 8)
            with act.Fori(0, HALF // 4) as j:
                down(j, HALF + LOOK)
            wide_squares(DOWN_CHUNK0 + 4, 1, 9)

        @block.tensor
        def _(pe):
            n_stat = [0]

            def mm(out_, a, b, start, stop):
                return nc.tensor.matmul(out_, a, b, start=start, stop=stop, skip_group_check=True)

            def wait_bank(key, b):
                if free[key, b]:
                    pe.wait_ge(*free[key, b])

            def cols_sub(slot, k0, nk, first, last, banks, X):
                for kk in range(nk):
                    for c in range(2):
                        at, b, k = 256 * kk + P * c, banks[c], k0 + kk
                        hi, lo = wt_hi[:, slot, at:at + P], wt_lo[:, slot, at:at + P]
                        if last and kk == nk - 1:
                            mm(ps[:, b, T:2 * T], lo, X[:, k, 0:T], False, False)
                            ins = mm(ps[:, b, :], hi, X[:, k, :], False, True)
                        else:
                            mm(ps[:, b, :], hi, X[:, k, :], first and kk == 0, False)
                            ins = mm(ps[:, b, T:2 * T], lo, X[:, k, 0:T], False, False)
                ins.then_inc(sub_used, 1)

            def rows_sub(slot, k0, nk, ncols, first, last, banks, X):
                for kk in range(nk):
                    hi = wt_hi[:, slot, ncols * kk:ncols * kk + ncols]
                    lo = wt_lo[:, slot, ncols * kk:ncols * kk + ncols]
                    for t in range(TT):
                        x_hi, x_lo = X[:, k0 + kk, P * t:P * t + P], X[:, k0 + kk, T + P * t:T + P * t + P]
                        o = ps[:, banks[t], 0:ncols]
                        mm(o, x_hi, hi, first and kk == 0, False)
                        mm(o, x_hi, lo, False, False)
                        ins = mm(o, x_lo, hi, False, last and kk == nk - 1)
                ins.then_inc(sub_used, 1)

            def wide_sub(slot, xs, first, last, base, X, waits={}):
                for t in range(TT):
                    for c in range(2):
                        if waits.get(base + 2 * t + c):
                            pe.wait_ge(*waits[base + 2 * t + c])
                    x_hi, x_lo = X[:, xs, P * t:P * t + P], X[:, xs, T + P * t:T + P * t + P]
                    o = [ps[:, base + 2 * t + c, :] for c in range(2)]
                    hi = [wt_hi[:, slot, 512 * c:512 * c + 512] for c in range(2)]
                    lo = [wt_lo[:, slot, 512 * c:512 * c + 512] for c in range(2)]
                    for c in range(2):
                        mm(o[c], x_hi, hi[c], first, False)
                    for c in range(2):
                        mm(o[c], x_hi, lo[c], False, False)
                    for c in range(2):
                        ins = mm(o[c], x_lo, hi[c], False, last)
                ins.then_inc(sub_used, 1)

            def transpose_rows(k, m):
                b = 4 + m % 4
                pe.wait_ge(xn_a, 4 * k + m // 2 + 1)
                pe.wait_ge(xn_d, 4 * k + m // 2 + 1)
                wait_bank(("norm_t", k, m), b)
                for i in range(2):
                    for t in range(TT):
                        at = XN_AT[k] + D * t + P * (2 * m + i)
                        ins = nc.tensor.transpose(ps[:, b, T * i + P * t:T * i + P * t + P], work[:, at:at + P], ident[:])
                ins.then_inc(bank_full[b], 1)

            def rest_of_norm(k, s):
                for m in (4 + 2 * s, 5 + 2 * s):
                    transpose_rows(k, m)

            def do_unit(u):
                w = units[u]
                waits = {b: free["unit", u, b] for b in w.banks} if w.first else {}
                if w.kind != "wide":
                    for b in waits:
                        if waits[b]:
                            pe.wait_ge(*waits[b])
                for s in range(2):
                    pe.wait_ge(lo_done, 2 * u + s + 1)
                    slot, nk = (2 * u + s) % 4, w.nk // 2
                    first, last = w.first and s == 0, w.last and s == 1
                    if w.kind == "wide":
                        n_stat[0] += 1
                        pe.wait_ge(stat_lo, n_stat[0])
                        wide_sub(slot, (n_stat[0] - 1) % 4, first, last, w.banks[0], xt[w.ring], {} if s else waits)
                        continue
                    k0 = w.k0 + nk * s
                    before = 8 if w.xt == "b" else 0 if u < N_MIX else 16
                    pe.wait_ge(xt_ready, before + (k0 + nk) // 2)
                    if w.kind == "cols":
                        cols_sub(slot, k0, nk, first, last, w.banks, xt[w.xt])
                    else:
                        rows_sub(slot, k0, nk, w.nc, first, last, w.banks, xt[w.xt])
                    if u == 0:
                        rest_of_norm(0, s)

            def do(name, arg):
                if name == "norm_t":
                    for m in range(arg[1], 4 if arg[0] == 3 else arg[2]):
                        transpose_rows(arg[0], m)
                elif name == "tables":
                    pe.wait_ge(small_in, 16 * N_SMALL)
                    wait_bank(name, 4)
                    mm(ps[0:SWA, 4, 0:P], t5_sb, onehot_sb, True, True).then_inc(bank_full[4], 1)
                    wait_bank(name, 5)
                    for i in range(4):
                        ins = nc.tensor.transpose(ps[:, 5, 2 * FT * i:2 * FT * i + 2 * FT], rows_conv[:, i, :],
                                                  ident[0:2 * FT, 0:2 * FT])
                    ins.then_inc(bank_full[5], 1)
                elif name == "gates":
                    pe.wait_ge(gate_split, 2)
                    wait_bank(name, 7)
                    gates = ps[0:GATES, 7, 0:T]
                    for k in range(KT):
                        x_hi, x_lo = xt["a"][:, k, 0:T], xt["a"][:, k, T:2 * T]
                        mm(gates, gate_parts[:, 0, k, :], x_hi, k == 0, False)
                        mm(gates, gate_parts[:, 0, k, :], x_lo, False, False)
                        ins = mm(gates, gate_parts[:, 1, k, :], x_hi, False, k == KT - 1)
                    ins.then_inc(bank_full[7], 1)
                elif name == "head_s":
                    kind, i, a = arg
                    q, k, _, need, _ = head_sources(arg)
                    pe.wait_ge(proj_done, need)
                    if kind == "fox":
                        pe.wait_ge(fox_ready, 1)
                    b = score_bank(arg)
                    wait_bank((name, a), b)
                    for qb, o, w in ((0, 0, T), (1, T, T)) if kind == "x" else ((0, 0, P), (1, P, T)):
                        dst = ps[:, b, o:o + w]
                        ins = mm(dst, work[:, q + P * qb:q + P * qb + P], work[:, k:k + w], True, kind != "fox")
                        if kind == "fox":
                            mm(dst, c_sel[:, i, P * qb:P * qb + P], ones[0:FOX, 0:w], False, False)
                            ins = mm(dst, sel[:, i, :], neg_c[:, 0:w], False, True)
                    ins.then_inc(bank_full[b], 1)
                elif name == "head_t":
                    kind, i, a = arg
                    pe.wait_ge(normed, a + 1)
                    b = probs_bank(arg)
                    wait_bank((name, a), b)
                    if kind == "x":
                        moves = [(T * qb + P * kb, T * kb + P * qb) for qb in range(2) for kb in range(2)]
                    else:
                        moves = [(P * c, P * c) for c in range(3)]
                    for src, dst in moves:
                        ins = nc.tensor.transpose(ps[:, b, dst:dst + P], probs[:, a % 3, src:src + P], ident[:])
                    ins.then_inc(bank_full[b], 1)
                elif name == "head_o":
                    kind, i, a = arg
                    _, _, v, _, need = head_sources(arg)
                    pe.wait_ge(pt_ready, a + 1)
                    pe.wait_ge(proj_done, need)
                    b, pt = out_bank(arg), head_probs_t(arg)
                    wait_bank((name, a), b)
                    mm(ps[:, b, 0:T], v[:, 0, :], pt[:, 0:T], True, False)
                    if kind == "x":
                        ins = mm(ps[:, b, 0:T], v[:, 1, :], pt[:, T:2 * T], False, True)
                    else:
                        ins = mm(ps[:, b, P:T], v[:, 1, :], pt[:, T:3 * P], False, True)
                    ins.then_inc(bank_full[b], 1)
                elif name == "gla_z":
                    wait_bank(name, 7)
                    for c in range(2):
                        ins = mm(ps[:, 7, T * c:T * c + T], gla_w[:, P * c:P * c + P], glr_t, True, True)
                    ins.then_inc(bank_full[7], 1)
                elif name == "gla_scores":
                    pe.wait_ge(gla_d, 4)
                    wait_bank(name, 7)
                    for t in range(TT):
                        for c in range(2):
                            ins = nc.tensor.transpose(ps[:, 7, T * t + P * c:T * t + P * c + P],
                                                      g_kend_t[:, T * c + P * t:T * c + P * t + P], ident[:])
                    ins.then_inc(bank_full[7], 1)
                    for par, b in ((0, 4), (1, 6)):
                        wait_bank(name, b)
                        rows = slice(64 * par, 64 * par + 64)
                        for hh in range(par, GLA, 2):
                            for c in range(NCH):
                                tok = T * (hh // 2) + CHUNK * c
                                col = 128 * (hh // 2) + 64 * (c // 2)
                                ins = mm(ps[64 * (c % 2):64 * (c % 2) + 64, b, col:col + 64],
                                         work[rows, GK + tok:GK + tok + 64], work[rows, GQ + tok:GQ + tok + 64],
                                         True, True)
                        ins.then_inc(bank_full[b], 1)
                elif name == "gla_kv":
                    pe.wait_ge(gla_d, 5)
                    pe.wait_ge(proj_done, PROJ["gv"])
                    gv = wk(GV, TT, 512)
                    for b, some in ((4, (0, 2)), (7, (1,))):
                        wait_bank(name, b)
                        for c in some:
                            tok = slice(64 * (c % 2), 64 * (c % 2) + 64)
                            for hh in range(GLA):
                                col = T * (c // 2) + P * (hh // 2)
                                ins = mm(ps[64 * (hh % 2):64 * (hh % 2) + 64, b, col:col + P],
                                         g_kend[tok, c // 2, 64 * hh:64 * hh + 64],
                                         gv[tok, c // 2, P * hh:P * hh + P], True, True)
                        ins.then_inc(bank_full[b], 1)
                elif name == "gla_out":
                    pe.wait_ge(gla_d, 6)
                    pe.wait_ge(gla_p, 3)
                    gv = wk(GV, TT, 512)
                    for t, b in ((0, 6), (1, 7)):
                        wait_bank(name, b)
                        for c in (2 * t, 2 * t + 1):
                            half = 64 * (c % 2)
                            for hh in range(GLA):
                                o = ps[half:half + 64, b, P * hh:P * hh + P]
                                ins = mm(o, g_at[:, hh, c, :], gv[:, t, P * hh:P * hh + P], True, c == 0)
                                if c:
                                    tok = GQ + T * (hh // 2) + CHUNK * c
                                    ins = mm(o, work[:, tok:tok + 64], g_s[:, hh, c - 1, :], False, True)
                        ins.then_inc(bank_full[b], 1)
                elif name == "gla_o":
                    pe.wait_ge(gla_d, 8)
                    for b in (6, 7):
                        wait_bank(name, b)
                        for i in range(2):
                            hh = 2 * (b - 6) + i
                            for t in range(TT):
                                ins = nc.tensor.transpose(ps[:, b, T * i + P * t:T * i + P * t + P],
                                                          g_o[:, t, P * hh:P * hh + P], ident[:])
                        ins.then_inc(bank_full[b], 1)

            pe.wait_ge(prm_in, 16 * N_PRM)
            pe.wait_ge(c_ready, 1)
            nc.tensor.transpose(ps[:, 4, 0:NPRM], rows_prm, ident[0:NPRM, 0:NPRM]).then_inc(bank_full[4], 1)
            for m in range(4):
                transpose_rows(0, m)
            for u in range(len(units)):
                do_unit(u)
                for name, arg in jobs.get(u, []):
                    do(name, arg)

            def up(j, first=False):
                for i in range(4):
                    if i % 2 == 0:
                        if first:
                            for b in (i, i + 1):
                                pe.wait_ge(*up_free[b])
                        else:
                            pe.wait_ge(u_ready, 2 * j + (i // 2 + 1))
                    for s in range(2):
                        pe.wait_ge(lo_done, 8 * j + (2 * (UP0 + i) + s + 1))
                        if first:
                            pe.wait_ge(xt_ready, 24 + 4 * (i % 2) + 2 * s + 2)
                        cols_sub((2 * i + s) % 4, 8 * (i % 2) + 4 * s, 4, i % 2 == 0 and s == 0,
                                 i % 2 == 1 and s == 1, [i // 2 * 2, i // 2 * 2 + 1], xt["a"])
                        if first and i == 0:
                            rest_of_norm(3, s)

            up(0, first=True)
            with pe.Fori(1, UP_ITERS) as j:
                up(j)

            def down(j, x, n, first=False, last=False):
                for i in range(n):
                    for s in range(2):
                        pe.wait_ge(lo_done, 8 * j + (2 * (DOWN0 + x + i) + s + 1))
                        pe.wait_ge(stat_lo, 8 * j + (STAT0 + 2 * (x + i) + s + 1))
                        slot = (2 * (x + i) + s) % 4
                        wide_sub(slot, slot, first and i == 0 and s == 0, last and i == n - 1 and s == 1,
                                 4 * (1 - x // HALF), xt["b"])

            for b in range(4, 8):
                pe.wait_ge(*down_free[b])
            down(0, 0, 4, first=True)
            with pe.Fori(1, HALF // 4) as j:
                down(j, 0, 4)
            down(0, 4 * (HALF // 4), HALF % 4, last=True)
            pe.wait_ge(u_ready, 2 + 2 * UP_ITERS)
            down(0, HALF, HALF % 4, first=True)
            with pe.Fori(0, HALF // 4 - 1) as j:
                down(j, HALF + HALF % 4, 4)
            down(HALF // 4 - 1, HALF + HALF % 4, 4, last=True)

        @block.vector
        def _(dve):
            V = nc.vector
            n = [0]

            def step(ins):
                n[0] += 1
                ins.then_inc(dve_step, 1)
                dve.wait_ge(dve_step, n[0])

            def split_lo(j, c, subs=(0, 1)):
                for s in subs:
                    dve.wait_ge(hi_done, 8 * j + (2 * c + s + 1))
                    V.tensor_tensor(wt_lo[:, (2 * c + s) % 4, :], raw[:, c % RAW, SUB * s:SUB * s + SUB],
                                    wt_hi[:, (2 * c + s) % 4, :].bitcast(F32), ALU.subtract).then_inc(lo_done, 1)

            def norm_rows(k, c):
                at = XN_AT[k] + D + 512 * c
                V.tensor_scalar(work[:, at:at + 512], norm_source(k, 1)[:, 512 * c:512 * c + 512], rstd[:, 1:2],
                                None, ALU.mult).then_inc(xn_d, 1)

            def norm_lo(k, m):
                b, X = 4 + m % 4, XT_OF[k]
                dve.wait_ge(xt_hi, 8 * k + m + 1)
                for i in range(2):
                    kk = 2 * m + i
                    ins = V.scalar_tensor_tensor(X[:, kk, T:2 * T], ps[:, b, T * i:T * i + T],
                                                 prm[:, GAIN_ROW[k] + kk:GAIN_ROW[k] + kk + 1],
                                                 X[:, kk, 0:T].bitcast(F32), ALU.mult, ALU.subtract)
                ins.then_inc(xt_ready, 1)

            def mean_squares(n_norm):
                step(V.tensor_reduce(meansq[:, 0:TT], sumsq[:], AX.X, ALU.add))
                V.tensor_scalar(meansq[:, 0:TT], meansq[:, 0:TT], 1.0 / D, None, ALU.mult).then_inc(meansq_ready, 1)
                dve.wait_ge(rstd_ready, n_norm + 1)

            def wide_add(bank, half, subs):
                dve.wait_ge(sub_used, subs)
                for i in range(4):
                    c, t = i // TT, i % TT
                    col = 1024 * half + 512 * c
                    V.tensor_tensor(h[:, t, col:col + 512], h[:, t, col:col + 512], ps[:, bank + wide_bank(i), :],
                                    ALU.add).then_inc(h_added, 1)

            dve.wait_ge(x_in[1], 16)
            V.tensor_tensor_reduce(out=work[:, NTMP + D:NTMP + 2 * D], in0=h[:, 1, :], in1=h[:, 1, :], scale=1.0,
                                   scalar=0.0, op0=ALU.mult, op1=ALU.add, accum_out=sumsq[:, 1, 0:1]).then_inc(stats_d, 1)
            dve.wait_ge(stats_d, 1)
            dve.wait_ge(stats_a, 1)
            V.tensor_scalar(meansq[:, 0:TT], sumsq[:, :, 0], 1.0 / D, None, ALU.mult).then_inc(meansq_ready, 1)
            dve.wait_ge(rstd_ready, 1)
            for c in range(4):
                norm_rows(0, c)
            dve.wait_ge(bank_full[4], 1)
            V.tensor_copy(prm[:], ps[:, 4, 0:NPRM]).then_inc(prm_ready, 1)
            for s in range(2):
                split_lo(0, 0, [s])
                for m in range(4 * s, 4 * s + 4):
                    norm_lo(0, m)
            split_lo(0, 1)

            def do(name, arg):
                if name == "evac_cols":
                    w, g = units[arg], cols_groups.index(arg)
                    b = w.banks[0]
                    dve.wait_ge(low_ready, g + 1)
                    V.scalar_tensor_tensor(wk(w.dest, 2, T), ps[:, b:b + 2, 0:T], w.scale, low[:, g % 2, :, :],
                                           ALU.mult, ALU.add).then_inc(proj_done, 1)
                elif name == "evac_rows":
                    w = units[arg]
                    b = w.banks[0]
                    dve.wait_ge(sub_used, 2 * arg + 2)
                    V.tensor_copy(wk(w.dest, TT, w.nc), ps[:, b:b + 2, 0:w.nc]).then_inc(proj_done, 1)
                elif name == "evac_wide":
                    wide_add(units[arg].banks[0], units[arg].half, 2 * arg + 2)
                elif name == "mem_squares":
                    dve.wait_ge(stats_a, 3)
                    V.tensor_scalar(meansq[:, 0:TT], sumsq[:, :, 1], 1.0 / D, None, ALU.mult).then_inc(meansq_ready, 1)
                elif name == "mem_rows":
                    dve.wait_ge(rstd_ready, 2)
                    for c in range(4):
                        norm_rows(1, c)
                elif name == "tables":
                    dve.wait_ge(small_in, 16 * N_SMALL)
                    dve.wait_ge(bank_full[4], full[name, 4])
                    V.tensor_copy(bias_row, ps[0:SWA, 4, 0:P]).then_inc(prm_ready, 1)
                    dve.wait_ge(bank_full[5], full[name, 5])
                    V.tensor_copy(conv[:].rearrange("p a b -> p (a b)"), ps[:, 5, 0:8 * FT]).then_inc(prm_ready, 1)
                elif name == "norm":
                    dve.wait_ge(stats_a, 2 * arg + 1)
                    mean_squares(arg + 1)
                    for c in range(4):
                        norm_rows(arg, c)
                elif name == "norm_t":
                    for m in range(arg[1], arg[2]):
                        norm_lo(arg[0], m)
                elif name == "gates_split":
                    dve.wait_ge(gate_split, 1)
                    V.tensor_tensor(gate_parts[:, 1], gate_w_in, gate_parts[:, 0].bitcast(F32), ALU.subtract).then_inc(gate_split, 1)
                elif name == "gates":
                    dve.wait_ge(bank_full[7], full[name, 7])
                    V.tensor_copy(glr_t, ps[glr_rows, 7, 0:T]).then_inc(gate_t_ready, 1)
                    V.tensor_scalar(f_z, ps[0:FOX, 7, 0:T], b_fox[:], None, ALU.add).then_inc(gate_t_ready, 1)
                    dve.wait_ge(gate_t_ready, 2)
                    step(V.tensor_scalar(f_m, f_z, 0.0, None, ALU.min))
                    V.scalar_tensor_tensor(f_e, f_m, 2.0, f_z, ALU.mult, ALU.subtract).then_inc(gate_t_ready, 1)
                elif name == "fox_gates":
                    dve.wait_ge(gate_a, 1)
                    dve.wait_ge(c_ready, 4)
                    step(V.tensor_tensor(f_m, f_m, f_e, ALU.subtract))
                    step(V.tensor_tensor_scan(f_z, ones[0:FOX, :], f_m, 0.0, ALU.mult, ALU.add))
                    V.tensor_scalar(neg_c, f_z, -1.0, None, ALU.mult)
                    for i in range(FOX):
                        ins = V.tensor_scalar(c_sel[:, i, :], f_z, sel[:, i, 0:1], None, ALU.mult)
                    ins.then_inc(fox_ready, 1)
                elif name == "head_s":
                    kind, i, a = arg
                    r = a % 3
                    b = score_bank(arg)
                    dve.wait_ge(bank_full[b], full[(name, a), b])
                    if a == 0:
                        dve.wait_ge(bias_out, 16)
                    if a >= 3:
                        b = 6 if a - 3 == FOX + SWA + 1 else 5
                        dve.wait_ge(bank_full[b], full[("head_t", a - 3), b])
                    w0, w1 = (T, 2 * T) if kind == "x" else (P, 3 * P)
                    src = ps[:, score_bank(arg), :] if kind == "x" else probs[:, r, :]
                    if kind == "fox":
                        step(V.tensor_tensor(probs[:, r, 0:w1], ps[:, 4, 0:w1], fox_mask[:], ALU.add))
                    if kind == "swa":
                        dve.wait_ge(bias_done, 2)
                        V.tensor_tensor(probs[:, r, 0:T], ps[:, 4, 0:T], bias_m[:, i, :, :].rearrange("p m k -> p (m k)"),
                                        ALU.add)
                        step(V.tensor_tensor(probs[:, r, T:w1], ps[:, 4, T:w1], bias_m[:, i, 0, :], ALU.add))
                    V.tensor_reduce(rowmax[:, r, 0:1], src[:, 0:w0], AX.X, ALU.max)
                    step(V.tensor_reduce(rowmax[:, r, 1:2], src[:, w0:w1], AX.X, ALU.max))
                    if kind == "swa":
                        V.tensor_scalar(negmax[:, r, :], rowmax[:, r, :], sinks[:, i:i + 1], -1.0, ALU.max,
                                        ALU.mult).then_inc(scored, 1)
                    else:
                        V.tensor_scalar(negmax[:, r, :], rowmax[:, r, :], -1.0, None, ALU.mult).then_inc(scored, 1)
                elif name == "head_n":
                    kind, i, a = arg
                    r = a % 3
                    dve.wait_ge(exped, a + 1)
                    w0, w1 = (T, 2 * T) if kind == "x" else (P, 3 * P)
                    if kind == "swa":
                        step(V.tensor_tensor(den[:, r, :], den[:, r, :], sink_e[:, r, :], ALU.add))
                    step(V.reciprocal(rden[:, r, :], den[:, r, :]))
                    V.tensor_scalar(probs[:, r, 0:w0], probs[:, r, 0:w0], rden[:, r, 0:1], None, ALU.mult)
                    V.tensor_scalar(probs[:, r, w0:w1], probs[:, r, w0:w1], rden[:, r, 1:2], None,
                                    ALU.mult).then_inc(normed, 1)
                elif name == "gla_z":
                    dve.wait_ge(bank_full[7], full[name, 7])
                    dve.wait_ge(bank_full[4], full[("head_s", FOX - 1), 4])
                    for c in range(2):
                        ins = V.tensor_scalar(g_z[:, T * c:T * c + T], ps[:, 7, T * c:T * c + T],
                                              prm[:, B_GATE + c:B_GATE + c + 1], None, ALU.add)
                    step(ins)
                    step(V.tensor_scalar(g_m, g_z, 0.0, None, ALU.min))
                    V.scalar_tensor_tensor(g_e, g_m, 2.0, g_z, ALU.mult, ALU.subtract).then_inc(gla_d, 1)
                elif name == "gla_decay":
                    dve.wait_ge(gla_a, 1)
                    step(V.tensor_tensor(g_m, g_m, g_e, ALU.subtract))
                    step(V.tensor_scalar(g_m, g_m, 1.0 / 16.0, None, ALU.mult))
                    for c in range(2 * NCH):
                        at = slice(CHUNK * c, CHUNK * c + CHUNK)
                        ins = V.tensor_tensor_scan(g_b[:, at], ones[:, 0:CHUNK], g_m[:, at], 0.0, ALU.mult, ALU.add)
                    ins.then_inc(gla_d, 1)
                elif name == "gla_scale":
                    dve.wait_ge(bank_full[6], full[("head_o", FOX - 1), 6])
                    dve.wait_ge(gla_d, 2)
                    b4 = g_b.rearrange("p (n c) -> p n c", c=CHUNK)
                    V.tensor_tensor(g_kend_t.rearrange("p (n c) -> p n c", c=CHUNK),
                                    b4[:, :, CHUNK - 1:CHUNK].broadcast_to([P, 2 * NCH, CHUNK]), b4,
                                    ALU.subtract).then_inc(gla_d, 1)
                    dve.wait_ge(gla_a, 4)
                    dve.wait_ge(proj_done, PROJ["gq"])
                    step(V.tensor_tensor(g_kend_t, g_kend_t, wk(GK, 512), ALU.mult))
                    V.tensor_tensor(wk(GK, 512), wk(GK, 512), g_m, ALU.mult)
                    V.tensor_tensor(wk(GQ, 512), wk(GQ, 512), g_z, ALU.mult).then_inc(gla_d, 1)
                elif name == "gla_scores":
                    dve.wait_ge(bank_full[7], full[name, 7])
                    V.tensor_copy(g_kend, ps[:, 7, :].rearrange("p (t n) -> p t n", t=TT)).then_inc(gla_d, 1)
                elif name == "gla_kv":
                    dve.wait_ge(gla_p, 2)
                    dve.wait_ge(bank_full[4], full[name, 4])
                    dve.wait_ge(bank_full[7], full[name, 7])
                    for par in range(2):
                        rows = slice(64 * par, 64 * par + 64)
                        ins = V.tensor_copy(g_s[rows, par::2, 0, :], ps[rows, 4, 0:T].rearrange("p (h n) -> p h n", h=2))
                    step(ins)
                    for c, b, at in ((1, 7, 0), (2, 4, T)):
                        for par in range(2):
                            rows = slice(64 * par, 64 * par + 64)
                            for i in range(2):
                                last = T * i + CHUNK * c + CHUNK - 1
                                ins = V.scalar_tensor_tensor(g_s[rows, 2 * i + par, c, :], g_s[rows, 2 * i + par, c - 1, :],
                                                             g_z[rows, last:last + 1],
                                                             ps[rows, b, at + P * i:at + P * i + P], ALU.mult, ALU.add)
                        if c == 1:
                            step(ins)
                    ins.then_inc(gla_d, 1)
                elif name == "gla_out":
                    dve.wait_ge(bank_full[6], full[name, 6])
                    dve.wait_ge(bank_full[7], full[name, 7])
                    V.tensor_copy(g_o, ps[:, 6:8, :]).then_inc(gla_d, 1)
                elif name == "gla_rms":
                    dve.wait_ge(gla_d, 7)
                    step(V.tensor_tensor(g_sq, g_o, g_o, ALU.mult))
                    step(V.tensor_reduce(meansq[:, 0:8], g_sq.rearrange("p t (h n) -> p (t h) n", n=GLA_DV), AX.X, ALU.add))
                    V.tensor_scalar(meansq[:, 0:8], meansq[:, 0:8], 1.0 / GLA_DV, None, ALU.mult).then_inc(meansq_ready, 1)
                elif name == "gla_norm":
                    dve.wait_ge(rstd_ready, 3)
                    o8 = g_o.rearrange("p t (h n) -> p (t h) n", n=GLA_DV)
                    V.tensor_tensor(o8, o8, rstd[:, 0:8].unsqueeze(2).broadcast_to([P, 8, GLA_DV]),
                                    ALU.mult).then_inc(gla_d, 1)
                elif name == "gla_o":
                    dve.wait_ge(gla_a, 6)
                    for b in (6, 7):
                        dve.wait_ge(bank_full[b], full[name, b])
                        at = 512 * (b - 6)
                        ins = V.scalar_tensor_tensor(wk(FK + at, 512), ps[:, b, :], prm[:, G_GLA:G_GLA + 1],
                                                     wk(GR + at, 512), ALU.mult, ALU.mult)
                    ins.then_inc(gla_done, 1)

            def stationary_lo(v):
                w = units[v]
                for s in range(2):
                    k, at = 2 * wides.index(v) + s, w.tiles[w.k0 + s]
                    dve.wait_ge(stat_hi, k + 1)
                    V.tensor_tensor(xt[w.ring][:, k % 4, T:2 * T], work[:, at:at + T],
                                    xt[w.ring][:, k % 4, 0:T].bitcast(F32), ALU.subtract).then_inc(stat_lo, 1)

            for u in range(len(units)):
                split_lo(0, u + LOOK, [0])
                for name, arg in early.get(u, []):
                    do(name, arg)
                if u == WO0 - 1:
                    for v in stationary_of(u):
                        stationary_lo(v)
                split_lo(0, u + LOOK, [1])
                if u != WO0 - 1:
                    for v in stationary_of(u):
                        stationary_lo(v)
                for name, arg in late.get(u, []):
                    do(name, arg)

            def down_stat(j, c, k):
                for s in range(2):
                    dve.wait_ge(stat_hi, 8 * j + (STAT0 + 2 * (c - DOWN0) + s + 1))
                    X = xt["b"][:, (2 * c + s) % 4, :]
                    V.tensor_tensor(X[:, T:2 * T], act_t[:, bass.ds(j * (8 * T) + (k + s) * T, T)],
                                    X[:, 0:T].bitcast(F32), ALU.subtract).then_inc(stat_lo, 1)

            V.memset(u_pad[:, :, 0:2], 0.0).then_inc(act_done, 1)
            dve.wait_ge(act_done, 1)
            V.tensor_copy(rden[:, 0, :], rstd[:, 0:2]).then_inc(u_ready, 1)
            V.tensor_copy(rden[:, 1, :], rstd[:, 0:2]).then_inc(u_ready, 1)

            def up(j, last=False):
                for i in range(4):
                    split_lo(j, UP0 + i + LOOK)
                    if last and i >= 2:
                        down_stat(0, DOWN0 + i - 2, 2 * (i - 2))
                    if i % 2 == 0:
                        continue
                    side = i // 2
                    mine = slice(2 * side, 2 * side + 2)
                    dve.wait_ge(low_ready, 2 * j + (n_low + side + 1))
                    V.tensor_tensor(u_pad[:, mine, 2:2 + T], ps[:, mine, 0:T], low[:, side, :, :], ALU.add).then_inc(u_ready, 1)
                    dve.wait_ge(cv_init, 2 * j + (side + 1))
                    for tap, done in ((1, cv_tap), (0, cv_done)):
                        for c in range(2):
                            x2 = 2 * side + c
                            ct = 2 * j + (FT * side + c)
                            ins = V.scalar_tensor_tensor(cv[:, x2, :], u_pad[:, x2, tap:tap + T],
                                                         conv[:, tap, bass.ds(ct, 1)], cv[:, x2, :], ALU.mult, ALU.add)
                        ins.then_inc(done, 1)
                        dve.wait_ge(done, 2 * j + (side + 1))
                dve.wait_ge(silu_done, j + 1)
                V.tensor_tensor(act_t[:, bass.ds(j * (2 * T), 2 * T)].rearrange("p (a b) -> p a b", a=2), cv[:, 0:2, :],
                                cv[:, 2:4, :], ALU.mult).then_inc(act_done, 1)

            with dve.Fori(0, UP_ITERS - 1) as j:
                up(j)
            up(UP_ITERS - 1, last=True)

            def down(j, x):
                for i in range(4):
                    split_lo(j, DOWN0 + x + i)
                    down_stat(j, DOWN0 + x + i, 2 * ((x + i) % HALF))

            with dve.Fori(0, HALF // 4) as j:
                down(j, LOOK)
            for i in range(LOOK):
                split_lo(0, DOWN0 + HALF + i)
                down_stat(0, DOWN0 + HALF + i, 2 * i)
            wide_add(4, 0, 2 * (DOWN0 + HALF))
            with dve.Fori(0, HALF // 4) as j:
                down(j, HALF + LOOK)
            wide_add(0, 1, 2 * (DOWN0 + 2 * HALF))
            dve.wait_ge(stats_a, 9)
            mean_squares(5)
            dve.wait_ge(raw_in[GAIN % RAW], 16 * (GAIN // RAW + 1))
            for c in range(4):
                for t in range(TT):
                    y = h[:, t, 512 * c:512 * c + 512]
                    V.scalar_tensor_tensor(y, y, rstd[:, t:t + 1], raw[:, GAIN % RAW, 512 * c:512 * c + 512],
                                           ALU.mult, ALU.mult).then_inc(out_ready, 1)


_INS = ["x", "mem", "w_in", "b_fox_f", "swa_sinks", "t5_bias", "w_gla_gate", "b_gla_gate", "gla_norm", "w_mix_out",
        "norm_mix", "norm_xattn", "norm_mem", "wq_x", "wkv_x", "wo_x", "norm_ffn", "w_up", "conv_w", "conv_b",
        "w_down", "final_norm"]


def kernel(**inputs):
    import concourse.bacc as bacc
    from concourse.bass_utils import run_bass_kernel_spmd

    nc = bacc.Bacc("TRN2", target_bir_lowering=False, num_devices=1)
    arrays, args = {}, []
    for name in _INS + ["t5_onehot"]:
        a = onehot_table() if name == "t5_onehot" else np.ascontiguousarray(inputs[name])
        arrays[f"in_{name}"] = a
        args.append(nc.dram_tensor(f"in_{name}", a.shape, mybir.dt.from_np(a.dtype), kind="ExternalInput").ap())
    out = nc.dram_tensor("out_y", inputs["x"].shape, F32, kind="ExternalOutput").ap()
    trunk(nc, *args, out)
    r = run_bass_kernel_spmd(nc, [arrays], core_ids=[0])
    return r.results[0]["out_y"]
```

```python
from contextlib import ExitStack

import numpy as np

import concourse.bass as bass
from concourse import mybir

F32 = mybir.dt.float32
F32R = mybir.dt.float32r
ACT = mybir.ActivationFunctionType
ALU = mybir.AluOpType
AX = mybir.AxisListType

P = 128
D = 2048
T = 256
TT = T // P
KT = D // P
HD = 128
FOX, SWA, SWA_KV, GLA, XH = 4, 8, 2, 4, 4
GLA_DK, GLA_DV, GLA_RANK, CHUNK = 64, 128, 16, 64
NCH = T // CHUNK
D_FF = 5632
FT = D_FF // P
NBUCKET, MAXDIST = 32, 128
EPS = 1e-6
SCALE = float(HD) ** -0.5
NEG = -1.0e30
UNIT = 2048
SUB = UNIT // 2
RAW = 4
LOOK = 2

WIN = {}
_at = 0
for _n, _w in (("fq", FOX * HD), ("fk", FOX * HD), ("fv", FOX * HD), ("ff", FOX), ("sq", SWA * HD),
               ("sk", SWA_KV * HD), ("sv", SWA_KV * HD), ("gq", GLA * GLA_DK), ("gk", GLA * GLA_DK),
               ("gv", GLA * GLA_DV), ("gr", GLA * GLA_DV), ("glr", GLA_RANK)):
    WIN[_n] = _at
    _at += _w

FQ, FK, SQ, SK, GQ, GK, GR = 0, 1024, 2048, 4096, 4608, 5120, 5632
FV, SV, GV, MK, MV = 6656, 7680, 8192, 9216, 10240
WORK = 11264
MEM_AT = 7168
XPT = 0
BIAS = 9216
XQ = 4096
GLR_AT = 32
GATES = GLR_AT + GLA_RANK
G_MIX, G_X, G_MEM, G_FFN, B_GATE, G_GLA, NPRM = 0, 16, 32, 48, 64, 66, 67


class Unit:

    def __init__(self, kind, w, k0, nk, c0, nc, first, last, dest=0, scale=1.0, xt="a", half=0, tiles=(), ring=None):
        self.kind, self.w, self.k0, self.nk, self.c0, self.nc = kind, w, k0, nk, c0, nc
        self.first, self.last = first, last
        self.dest, self.scale, self.xt = dest, scale, xt
        self.half, self.tiles, self.ring = half, tiles, ring
        self.banks = []


def plan():
    units, jobs = [], {}

    def job(slot, name, arg=None):
        jobs.setdefault(slot, []).append((name, arg))

    def cols(w, c0, ncols, dest, scale, xt):
        for c in range(0, ncols, 256):
            for half in range(2):
                units.append(Unit("cols", w, 8 * half, 8, c0 + c, 256, half == 0, half == 1,
                                  dest=dest + c * T // P, scale=scale, xt=xt))

    def rows(w, c0, ncols, dest, xt):
        nk = UNIT // ncols
        for k in range(0, KT, nk):
            units.append(Unit("rows", w, k, nk, c0, ncols, k == 0, k + nk == KT, dest=dest, xt=xt))

    def wide(w, order, tiles, ring):
        for half in range(2):
            for i, k in enumerate(order):
                units.append(Unit("wide", w, k, 2, 1024 * half, 1024, i == 0, i == len(order) - 1,
                                  half=half, tiles=tiles, ring=ring))

    cols("w_in", WIN["fk"], 512, FK, 1.0, "a")
    rows("w_in", WIN["fv"], 512, FV, "a")
    cols("w_in", WIN["fq"], 512, FQ, SCALE, "a")
    cols("w_in", WIN["gk"], 256, GK, 1.0, "a")
    cols("w_in", WIN["gq"], 256, GQ, float(GLA_DK) ** -0.5, "a")
    rows("w_in", WIN["gv"], 512, GV, "a")
    cols("w_in", WIN["gr"], 512, GR, 1.0, "a")
    cols("w_in", WIN["sk"], 256, SK, 1.0, "a")
    rows("w_in", WIN["sv"], 256, SV, "a")
    cols("w_in", WIN["sq"], 1024, SQ, SCALE, "a")
    tiles = [FQ + T * h for h in range(FOX)] + [SQ + T * h for h in range(SWA)] + [FK + T * h for h in range(GLA)]
    n_mix = len(units)
    wide("w_mix_out", [0, 2, 12, 14, 4, 6, 8, 10], tiles, "a")
    n_mk = len(units)
    cols("wkv_x", 0, 512, MK, 1.0, "b")
    n_wq = len(units)
    cols("wq_x", 0, 512, XQ, SCALE, "a")
    for pair in range(2):
        rows("wkv_x", XH * HD + T * pair, 2 * HD, MV + 2 * T * pair, "b")
    n_wo = len(units)
    wide("wo_x", [0, 2], [XQ + T * h for h in range(XH)], "b")
    n_up = len(units)

    group = 0
    for u, x in enumerate(units):
        if x.kind == "wide":
            x.banks = [4 * x.half + i for i in range(4)]
        if x.first and x.kind != "wide":
            pair = group % 2
            group += 1
        if x.kind != "wide":
            x.banks = [2 * pair, 2 * pair + 1]
        if x.last:
            job(max(u, 2), "evac_" + x.kind, u)
    job(0, "rms", 0)
    job(0, "diag", 0)
    job(2, "bcast", 0)
    job(2, "rms", 1)
    job(4, "norm_t", (1, 0, 3))
    job(6, "norm_t", (1, 3, 6))
    job(7, "norm_t", (1, 6, 8))
    job(n_mix + 5, "diag", 1)
    job(n_mix + 6, "bcast", 1)
    job(n_mix + 15, "rms", 2)
    job(n_mix + 16, "norm_t", (2, 0, 4))
    job(n_mix + 17, "norm_t", (2, 4, 8))
    job(n_mix + 17, "diag", 2)
    job(n_mix + 18, "bcast", 2)
    job(n_up - 2, "norm_t", (3, 0, 4))
    job(n_up - 1, "norm_t", (3, 4, 8))
    job(n_up - 1, "rms", 3)
    job(n_up - 1, "diag", 3)
    job(2, "tables")
    job(3, "gates_split")
    job(5, "gates")
    job(7, "fox_gates")
    job(8, "bias_load")
    for h in range(FOX):
        heads(job, ("fox", h, h), 10 + h)
    job(14, "gla_z")
    job(15, "gla_decay")
    job(17, "gla_scale")
    job(18, "gla_scores")
    job(20, "gla_kv")
    job(22, "gla_out")
    job(23, "gla_rms")
    job(24, "gla_norm")
    job(24, "gla_silu")
    job(25, "gla_o")
    for h in range(SWA):
        heads(job, ("swa", h, FOX + h), n_mix - 6 + h)
    for h in range(XH):
        heads(job, ("x", h, FOX + SWA + h), n_wq + 2 + 2 * (h // 2), n_wo - 2 + 2 * (h // 2))
    stages = ["head_o", "head_t", "head_n", "head_s"]
    for some in jobs.values():
        some.sort(key=lambda x: 0 if x[0].startswith("evac") else 1 + stages.index(x[0]) if x[0] in stages else 9)
    early = {}
    for u, some in jobs.items():
        early[u] = [x for x in some if x[0] in ("evac_cols", "evac_rows") or x == ("bcast", 0) or u == n_wo
                    or u == n_up - 1 and x[0] in ("evac_wide", "norm_t")]
    late = {u: [x for x in some if x not in early[u]] for u, some in jobs.items()}
    return units, jobs, early, late, n_mix, n_wo, n_up


def heads(job, head, slot, out_slot=None):
    for i, stage in enumerate(("head_s", "head_n", "head_t")):
        job(slot + i, stage, head)
    job(out_slot or slot + 3, "head_o", head)


def bucket(n):
    half = NBUCKET // 2
    if n < half:
        return n
    big = half + int(np.float32(np.log(np.float32(n) / np.float32(half)))
                     / np.float32(np.log(MAXDIST / half)) * np.float32(NBUCKET - half))
    return min(big, NBUCKET - 1)


def onehot_table():
    t = np.zeros((NBUCKET, P), np.float32)
    for y in range(P):
        t[bucket((-y) % P), y] = 1.0
    return t


def trunk(nc, x, mem, w_in, b_fox_f, swa_sinks, t5_bias, w_gla_gate, b_gla_gate, gla_norm, w_mix_out,
          norm_mix, norm_xattn, norm_mem, wq_x, wkv_x, wo_x, norm_ffn, w_up, conv_w, conv_b, w_down,
          final_norm, t5_onehot, out):
    weights = {"w_in": w_in[0], "w_mix_out": w_mix_out[0], "wkv_x": wkv_x[0], "wq_x": wq_x[0], "wo_x": wo_x[0],
               "w_up": w_up[0], "w_down": w_down[0]}
    units, jobs, early, late, N_MIX, WO0, UP0 = plan()
    UP_ITERS = FT // 2
    DOWN0 = UP0 + 4 * UP_ITERS
    HALF = FT // 2
    GAIN = DOWN0 + 2 * HALF
    assert UP0 % RAW == 0 and DOWN0 % RAW == 0 and HALF % RAW == 2

    ctx = ExitStack()
    with ctx:
        def sb(name, shape, dt=F32):
            return ctx.enter_context(nc.sbuf_tensor("sb_" + name, shape, dt))

        def sem(name):
            return ctx.enter_context(nc.semaphore(name))

        raw = sb("raw", [P, RAW, UNIT])
        wt_hi = sb("wt_hi", [P, 4, SUB], F32R)
        wt_lo = sb("wt_lo", [P, 4, SUB], F32R)
        xt = {"a": sb("xt_a", [P, KT, 2 * T], F32R), "b": sb("xt_b", [P, KT, 2 * T], F32R)}
        h = sb("h", [P, TT, D])
        work = sb("work", [P, WORK])
        att = sb("att", [P, 2560])
        low = sb("low", [P, 2, 2, T])
        ident = sb("ident", [P, P])
        prm = sb("prm", [P, NPRM])
        conv = sb("conv", [P, 4, 2 * FT])
        fox_mask = sb("fox_mask", [P, 2 * P])
        ones = sb("ones", [P, T])
        sumsq = sb("sumsq", [P, TT, 4])
        meansq = sb("meansq", [P, 8])
        rstd = sb("rstd", [P, 8 + 2 * 5])
        rms_row_0 = sb("rms_row_0", [P, T])
        mhalf = sb("mhalf", [P, 8])
        negmax = sb("negmax", [P, 3, 2])
        rowmax = sb("rowmax", [P, 3, 2])
        den = sb("den", [P, 3, 2])
        sink_e = sb("sink_e", [P, 3, 2])
        rden = sb("rden", [P, 3, 2])
        sinks = sb("sinks", [P, SWA])
        b_fox = sb("b_fox", [FOX, 1])
        ps = ctx.enter_context(nc.psum_tensor("ps", [P, 8, 512], F32))
        bias_dram = nc.dram_tensor("bias_rows", [SWA, P * P], F32, kind="Internal").ap()

        def wk(at, *shape):
            n = int(np.prod(shape))
            v = work[:, at:at + n]
            if len(shape) == 2:
                v = v.rearrange("p (a b) -> p a b", b=shape[1])
            if len(shape) == 3:
                v = v.rearrange("p (a b c) -> p a b c", b=shape[1], c=shape[2])
            return v

        probs = att[:, 0:1536].rearrange("p (r n) -> p r n", r=3)
        probs_t = att[:, 1536:2560].rearrange("p (r n) -> p r n", r=2)
        rows_mix = att[0:G_X, 1792:1792 + P]
        rows_prm = att[0:NPRM - G_X, 0:P]
        diag = att[:, 2048:2048 + T]
        rows_conv = att[0:2 * FT, P:P + 512].rearrange("p (a b) -> p a b", a=4)
        t5_sb = att[0:NBUCKET, 640:640 + SWA]
        onehot_sb = att[0:NBUCKET, 656:656 + P]
        bias_row = att[0:SWA, 784:784 + P]
        gate_w_in = att[:, 1024:1024 + KT * GATES].rearrange("p (k n) -> p k n", n=GATES)
        gate_parts = xt["b"][:, KT - 3:KT, :].rearrange("p a b -> p (a b)").rearrange(
            "p (i k n) -> p i k n", i=2, n=GATES)
        glr_rows = slice(GLR_AT, GLR_AT + GLA_RANK)
        gla_w = work[glr_rows, SK:SK + GLA * GLA_DK]
        sel = work[0:FOX, GR:GR + 512].rearrange("p (h n) -> p h n", h=FOX)
        glr_t = work[glr_rows, GR + 512:GR + 768]
        c_sel = work[0:FOX, SQ:SQ + 1024].rearrange("p (h n) -> p h n", h=FOX)
        neg_c = work[0:FOX, SQ + 1024:SQ + 1280]
        f_z = work[0:FOX, SQ + 1280:SQ + 1536]
        f_m = work[0:FOX, SQ + 1536:SQ + 1792]
        f_e = work[0:FOX, SQ + 1792:SQ + 2048]
        g_z = wk(SV, 512)
        g_m = wk(SK, 512)
        g_b = wk(SQ + 1536, 512)
        g_e = wk(GR, 512)
        g_kend_t = probs_t[:, 0, :]
        g_kend = probs_t[:, 1, :].rearrange("p (t n) -> p t n", t=TT)
        g_at = wk(FV, GLA, NCH, CHUNK)
        g_s = wk(SQ, GLA, NCH - 1, GLA_DV)
        g_o = att[:, 0:1024].rearrange("p (t n) -> p t n", t=TT)
        g_sq = att[:, 1536:2560].rearrange("p (t n) -> p t n", t=TT)
        bias_m = work[:, BIAS:BIAS + 2048].rearrange("p (h m k) -> p h m k", h=SWA, m=2)
        junk = att[:, 1024:1536]
        u_pad = att[:, 0:4 * (T + 2)].rearrange("p (i n) -> p i n", i=4)
        cv = att[:, 1032:1032 + 4 * T].rearrange("p (i n) -> p i n", i=4)
        act_t = work[:, :]

        def rms_col(k):
            return rstd[:, 8 + TT * k:8 + TT * k + TT]

        def rms_row(k):
            return rms_row_0[:] if k % 2 == 0 else fox_mask[:, 0:T]

        raw_in = [sem(f"raw_in{i}") for i in range(RAW)]
        hi_done = sem("hi_done")
        lo_done = sem("lo_done")
        sub_used = sem("sub_used")
        tile0_full = sem("tile0_full")
        stat_hi = sem("stat_hi")
        stat_lo = sem("stat_lo")
        bank_full = [sem(f"bank_full{b}") for b in range(8)]
        low_ready = sem("low_ready")
        proj_done = sem("proj_done")
        x_in = [sem(f"x_in{c}") for c in range(2)]
        mem_in = sem("mem_in")
        prm_in = sem("prm_in")
        small_in = sem("small_in")
        c_ready = sem("c_ready")
        pool_step = sem("pool_step")
        dve_step = sem("dve_step")
        act_step = sem("act_step")
        prm_ready = sem("prm_ready")
        bias_out = sem("bias_out")
        bias_in = sem("bias_in")
        bias_done = sem("bias_done")
        stats_a = sem("stats_a")
        stats_d = sem("stats_d")
        h_added = sem("h_added")
        meansq_ready = sem("meansq_ready")
        rstd_ready = sem("rstd_ready")
        diag_ready = sem("diag_ready")
        row_ready = sem("row_ready")
        xt_hi = sem("xt_hi")
        xt_ready = sem("xt_ready")
        scored = sem("scored")
        exped = sem("exped")
        normed = sem("normed")
        pt_ready = sem("pt_ready")
        o_ready = sem("o_ready")
        gate_zero = sem("gate_zero")
        gate_split = sem("gate_split")
        gate_t_ready = sem("gate_t_ready")
        gate_a = sem("gate_a")
        fox_ready = sem("fox_ready")
        gla_d = sem("gla_d")
        gla_a = sem("gla_a")
        gla_p = sem("gla_p")
        gla_done = sem("gla_done")
        u_sum = sem("u_sum")
        u_ready = sem("u_ready")
        cv_init = sem("cv_init")
        cv_tap = sem("cv_tap")
        cv_done = sem("cv_done")
        silu_done = sem("silu_done")
        act_done = sem("act_done")
        out_ready = sem("out_ready")
        out_written = sem("out_written")

        STAT0 = sum(2 for w in units if w.kind == "wide")
        wides = [u for u, w in enumerate(units) if w.kind == "wide"]
        groups = [u for u, w in enumerate(units) if w.last and w.kind != "wide"]
        cols_groups = [u for u in groups if units[u].kind == "cols"]
        n_proj, n_low = len(groups), len(cols_groups)
        PROJ = {"fv": 3, "fq": 5, "gk": 6, "gq": 7, "gv": 8, "gr": 10, "sv": 12, "sq": 16, "xq": 20, "mv": 22}
        assert n_proj == PROJ["mv"]
        reader = {4: (prm_ready, 1)}
        free = {}
        full = {}
        fills = [0] * 8
        fills[4] = 1

        def score_bank(head):
            return 7 if head[0] == "x" and head[1] % 2 else 4

        def probs_bank(head):
            return 6 if head[0] == "x" and head[1] % 2 else 5

        def out_bank(head):
            return 7 if head[0] == "x" and head[1] % 2 else 6

        def head_probs_t(head):
            kind, i, a = head
            return wk(XPT + 2 * T * i, 2 * T) if kind == "x" else probs_t[:, a % 2, :]

        def norm_bank(k, m):
            return m if k == 3 else 4 + m % 4

        def take(key, b, semaphore, count):
            free[key, b] = reader.get(b)
            reader[b] = (semaphore, count)
            fills[b] += 1
            full[key, b] = fills[b]

        for m in range(8):
            take(("norm_t", 0, m), norm_bank(0, m), xt_ready, m + 1)
        chunks = 0
        chunk0 = {}
        for u, w in enumerate(units):
            if w.first and w.kind == "wide":
                for i in range(4):
                    b = w.banks[0] + i
                    free["unit", u, b] = reader.get(b)
                    reader[b] = (h_added, chunks + i + 1)
                last = next(v for v in range(u, len(units)) if units[v].last)
                chunk0[last] = chunks
                chunks += 4
            elif w.first:
                last = next(v for v in range(u, len(units)) if units[v].last)
                for b in w.banks:
                    free["unit", u, b] = reader.get(b)
                    reader[b] = (proj_done, groups.index(last) + 1)
            for name, arg in jobs.get(u, []):
                if name == "norm_t":
                    for m in range(arg[1], arg[2]):
                        take((name, arg[0], m), norm_bank(arg[0], m), xt_ready, 8 * arg[0] + m + 1)
                elif name == "tables":
                    take(name, 4, prm_ready, 3)
                    take(name, 5, prm_ready, 4)
                elif name == "bcast":
                    take((name, arg), 7, row_ready, arg + 1)
                elif name == "gates":
                    take(name, 7, gate_t_ready, 2)
                elif name == "gla_z":
                    take(name, 7, gla_d, 1)
                elif name == "gla_scores":
                    take(name, 7, gla_d, 5)
                    take(name, 4, gla_a, 5)
                    take(name, 6, gla_a, 5)
                elif name == "gla_kv":
                    take(name, 4, gla_d, 6)
                    take(name, 7, gla_d, 6)
                elif name == "gla_out":
                    take(name, 6, gla_d, 7)
                    take(name, 7, gla_d, 7)
                elif name == "gla_o":
                    take(name, 6, gla_done, 1)
                    take(name, 7, gla_done, 1)
                elif name == "head_s":
                    take((name, arg[2]), score_bank(arg), exped if arg[0] == "x" else scored, arg[2] + 1)
                elif name == "head_t":
                    take((name, arg[2]), probs_bank(arg), pt_ready, arg[2] + 1)
                elif name == "head_o":
                    take((name, arg[2]), out_bank(arg), o_ready, arg[2] + 1)
        take(("bcast", 3), 7, row_ready, 4)
        down_free = {b: reader[b] for b in range(4, 8)}
        up_free = {b: reader[b] for b in range(4)}
        DOWN_CHUNK0 = chunks

        def stationary_of(u):
            v = u + LOOK
            ahead = v < len(units) and units[v].kind == "wide" and v not in (WO0, WO0 + 1)
            return ([WO0 + 1] if u == WO0 else [], [v] if ahead else [], [WO0] if v == WO0 else [])

        def head_sources(head):
            kind, i, _ = head
            if kind == "fox":
                v = wk(FV, TT, 512)[:, :, HD * i:HD * i + HD]
                return FQ + T * i, FK + T * i, v, PROJ["fq"] - 1 + i // 2, PROJ["fv"]
            if kind == "swa":
                g = i // (SWA // SWA_KV)
                v = wk(SV, TT, 256)[:, :, HD * g:HD * g + HD]
                return SQ + T * i, SK + T * g, v, PROJ["sq"] - 3 + i // 2, PROJ["sv"]
            v = wk(MV + 2 * T * (i // 2), TT, 2 * HD)[:, :, HD * (i % 2):HD * (i % 2) + HD]
            return XQ + T * i, MK + T * i, v, PROJ["xq"] - 1 + i // 2, PROJ["mv"] - 1 + i // 2

        GAIN_ROW = [G_MIX, G_MEM, G_X, G_FFN]
        XT_OF = [xt["a"], xt["b"], xt["a"], xt["a"]]

        def norm_source(k, t):
            return work[:, MEM_AT + D * t:MEM_AT + D * t + D] if k == 1 else h[:, t, :]

        def norm_of(w):
            return {"w_in": 0, "wkv_x": 1, "wq_x": 2}[w.w]

        def prm_rows(first, n):
            return rows_prm[first - G_X:first - G_X + n]

        small_loads = (
            (prm_rows(G_X, 16), norm_xattn[0].rearrange("(k p) -> k p", p=P)),
            (prm_rows(G_MEM, 16), norm_mem[0].rearrange("(k p) -> k p", p=P)),
            (prm_rows(G_FFN, 16), norm_ffn[0].rearrange("(k p) -> k p", p=P)),
            (prm_rows(B_GATE, 2), b_gla_gate[0].rearrange("(k p) -> k p", p=P)),
            (prm_rows(G_GLA, 1), gla_norm),
            (rows_conv[:, 0:3, :], conv_w[0].rearrange("j (k p) -> k j p", p=P)),
            (rows_conv[:, 3, :], conv_b[0].rearrange("(k p) -> k p", p=P)),
            (t5_sb, t5_bias),
            (onehot_sb, t5_onehot),
            (sinks[:], bass.AP(tensor=swa_sinks.tensor, offset=0, ap=[[0, P], [1, SWA]])),
            (b_fox[:], bass.AP(tensor=b_fox_f.tensor, offset=0, ap=[[1, FOX], [1, 1]])),
            (gla_w, w_gla_gate[0]),
            (gate_w_in[:, :, 0:FOX],
             weights["w_in"].rearrange("(k p) c -> p k c", p=P)[:, :, WIN["ff"]:WIN["ff"] + FOX]),
            (gate_w_in[:, :, GLR_AT:GATES],
             weights["w_in"].rearrange("(k p) c -> p k c", p=P)[:, :, WIN["glr"]:WIN["glr"] + GLA_RANK]),
        )
        N_SMALL = len(small_loads)

        block = ctx.enter_context(nc.Block())


        @block.sync
        def _(sp):
            def load(j, c, src):
                if c >= RAW:
                    sp.wait_ge(lo_done, 8 * j + (2 * c - 2 * RAW + 2))
                i = c % RAW
                sp.dma_start(raw[:, i, :].rearrange("p (k n) -> p k n", k=src.shape[1]), src).then_inc(raw_in[i], 16)

            def up_source(j, i):
                wt = weights["w_up"].rearrange("(k p) c -> p k c", p=P)
                return wt[:, 8 * (i % 2):8 * (i % 2) + 8, bass.ds(j * 256 + (i // 2) * D_FF, 256)]

            def down_source(i, half):
                wt = weights["w_down"].rearrange("(k p) c -> p k c", p=P)
                return wt[:, bass.ds(i * 2, 2), 1024 * half:1024 * half + 1024]

            def load_x(c):
                cols = slice(D // 2 * c, D // 2 * c + D // 2)
                sp.dma_start(h[:, :, cols], x[0].rearrange("(t p) d -> p t d", p=P)[:, :, cols]).then_inc(x_in[c], 16)

            load_x(0)
            for u, w in enumerate(units):
                wt = weights[w.w].rearrange("(k p) c -> p k c", p=P)
                load(0, u, wt[:, w.k0:w.k0 + w.nk, w.c0:w.c0 + w.nc])
                if u == 0:
                    load_x(1)
                if u == 3:
                    sp.dma_start(wk(MEM_AT, TT, D), mem[0].rearrange("(t p) d -> p t d", p=P)).then_inc(mem_in, 16)
                if u == 2:
                    sp.wait_ge(gate_zero, 1)
                    for dst, src in small_loads:
                        sp.dma_start(dst, src).then_inc(small_in, 16)
            with sp.Fori(0, UP_ITERS) as j:
                for i in range(4):
                    load(j, UP0 + i, up_source(j, i))
            with sp.Fori(0, HALF // 4) as j:
                for i in range(4):
                    load(j, DOWN0 + i, down_source(4 * j + i, 0))
            for i in range(4 * (HALF // 4), HALF):
                load(0, DOWN0 + i, down_source(i, 0))
            for i in range(HALF % 4):
                load(0, DOWN0 + HALF + i, down_source(i, 1))
            with sp.Fori(0, HALF // 4) as j:
                for i in range(HALF % 4, HALF % 4 + 4):
                    load(j, DOWN0 + HALF + i, down_source(4 * j + i, 1))
            sp.wait_ge(lo_done, 2 * GAIN - 2 * RAW + 2)
            gain = bass.AP(tensor=final_norm.tensor, offset=0, ap=[[0, P], [1, D]])
            sp.dma_start(raw[:, GAIN % RAW, :], gain).then_inc(raw_in[GAIN % RAW], 16)
            for i in range(4 * TT):
                c, t = i // TT, i % TT
                sp.wait_ge(out_ready, i + 1)
                sp.dma_start(out[0, P * t:P * t + P, 512 * c:512 * c + 512],
                             h[:, t, 512 * c:512 * c + 512]).then_inc(out_written, 16)
            sp.wait_ge(out_written, 16 * 4 * TT)

        @block.gpsimd
        def _(pool):
            G = nc.gpsimd
            n = [0]

            def step(ins):
                n[0] += 1
                ins.then_inc(pool_step, 1)
                pool.wait_ge(pool_step, n[0])

            step(G.memset(ident[:], 0.0))
            G.affine_select(out=ident[:], in_=ident[:], compare_op=ALU.not_equal, fill=1.0, base=0,
                            pattern=[[-1, P]], channel_multiplier=1).then_inc(c_ready, 1)
            G.memset(att[:, 1024:1024 + KT * GATES], 0.0).then_inc(gate_zero, 1)
            step(G.memset(mhalf[:], -0.5))
            step(G.memset(ones[:], 1.0))
            step(G.memset(fox_mask[:], 0.0))
            step(G.memset(work[0:FOX, GR:GR + 512], 0.0))

            def rms(nth, dst):
                cols = dst.shape[1]
                pool.wait_ge(meansq_ready, nth)
                G.tensor_tensor(dst, meansq[:, 0:cols], mhalf[:, 0:cols], ALU.pow).then_inc(rstd_ready, 1)

            rms(1, rms_col(0))
            m = fox_mask[:, 0:P]
            G.affine_select(out=m, in_=m, compare_op=ALU.is_ge, fill=NEG, base=0,
                            pattern=[[-1, P]], channel_multiplier=1).then_inc(c_ready, 1)
            G.affine_select(out=sel, in_=sel, compare_op=ALU.not_equal, fill=1.0, base=0,
                            pattern=[[-1, FOX], [0, P]], channel_multiplier=1).then_inc(c_ready, 1)
            rms(2, rms_col(1))
            pool.wait_ge(bias_in, 16)
            G.affine_select(out=bias_m[:, :, 0, :], in_=bias_m[:, :, 1, :], compare_op=ALU.is_ge, fill=NEG,
                            base=0, pattern=[[0, SWA], [-1, P]], channel_multiplier=1).then_inc(bias_done, 1)
            pool.wait_ge(bias_done, 1)
            G.affine_select(out=bias_m[:, :, 1, :], in_=bias_m[:, :, 1, :], compare_op=ALU.is_gt, fill=NEG,
                            base=0, pattern=[[0, SWA], [1, P]], channel_multiplier=-1).then_inc(bias_done, 1)
            pool.wait_ge(bank_full[6], full[("head_o", FOX - 1), 6])
            G.memset(wk(FV, 1024), 0.0).then_inc(gla_p, 1)
            G.memset(wk(SQ, 1536), 0.0).then_inc(gla_p, 1)
            pool.wait_ge(gla_p, 2)
            pool.wait_ge(gla_a, 5)
            for half in range(2):
                for hh in range(GLA):
                    m = g_at[64 * half:64 * half + 64, hh, half::2, :]
                    ins = G.affine_select(out=m, in_=m, compare_op=ALU.is_ge, fill=0.0, base=0,
                                          pattern=[[0, NCH // 2], [1, CHUNK]], channel_multiplier=-1)
            ins.then_inc(gla_p, 1)
            rms(3, rstd[:, 0:8])
            for k in (2, 3, 4):
                rms(k + 2, rms_col(k))

        @block.scalar
        def _(act):
            n = [0]

            def step(ins):
                n[0] += 1
                ins.then_inc(act_step, 1)
                act.wait_ge(act_step, n[0])

            def A(out_, in_, f=ACT.Copy, **kw):
                return nc.scalar.activation(out_, in_, f, **kw)

            def split_hi(j, c, subs=(0, 1)):
                if 0 in subs:
                    act.wait_ge(raw_in[c % RAW], 16 * j + 16 * (c // RAW + 1))
                for s in subs:
                    if 2 * c + s >= 4:
                        act.wait_ge(sub_used, 8 * j + (2 * c + s - 3))
                    A(wt_hi[:, (2 * c + s) % 4, :], raw[:, c % RAW, SUB * s:SUB * s + SUB]).then_inc(hi_done, 1)

            def norm_hi(k, m):
                b = norm_bank(k, m)
                act.wait_ge(bank_full[b], full[("norm_t", k, m), b])
                for i in range(2):
                    kk = 2 * m + i
                    ins = A(XT_OF[k][:, kk, 0:T], ps[:, b, T * i:T * i + T],
                            scale=prm[:, GAIN_ROW[k] + kk:GAIN_ROW[k] + kk + 1])
                ins.then_inc(xt_hi, 1)

            act.dma_start(rows_mix, norm_mix[0].rearrange("(k p) -> k p", p=P)).then_inc(prm_in, 16)
            nc.scalar.preload_act_table_set("natural_log_exp_and_others")
            act.wait_ge(prm_ready, 1)
            for s, ms in enumerate((range(4), (4, 5))):
                for m in ms:
                    norm_hi(0, m)
                split_hi(0, 0, [s])
            for m in (6, 7):
                norm_hi(0, m)
            split_hi(0, 1)

            def rms_row_copy(k):
                act.wait_ge(bank_full[7], full[("bcast", k), 7])
                A(rms_row(k), ps[:, 7, 0:T]).then_inc(row_ready, 1)

            def wide_squares(base, half, nth):
                if half == 0 and nth > 4:
                    act.wait_ge(meansq_ready, (nth + 2) // 2)
                act.wait_ge(stats_a, nth - 1)
                for i in range(4):
                    t, c = i // 2, i % 2
                    col = 1024 * half + 512 * c
                    act.wait_ge(h_added, base + i + 1)
                    at = 2 * half + c
                    ins = A(junk, h[:, t, col:col + 512], ACT.Square, accum_out=sumsq[:, t, at:at + 1])
                    if i < 3:
                        step(ins)
                ins.then_inc(stats_a, 1)

            def do(name, arg):
                if name == "evac_cols":
                    w, g = units[arg], cols_groups.index(arg)
                    act.wait_ge(sub_used, 2 * arg + 2)
                    if g >= 2:
                        act.wait_ge(proj_done, groups.index(cols_groups[g - 2]) + 1)
                    A(low[:, g % 2, :, :], ps[:, w.banks[0]:w.banks[0] + 2, T:2 * T],
                      scale=w.scale).then_inc(low_ready, 1)
                elif name == "evac_wide":
                    wide_squares(chunk0[arg], units[arg].half, 4 + sorted(chunk0).index(arg))
                elif name == "rms" and arg == 0:
                    A(work[:, 0:D], h[:, 0, :], ACT.Square, accum_out=sumsq[:, 0, 0:1]).then_inc(stats_a, 1)
                elif name == "rms" and arg == 1:
                    act.wait_ge(mem_in, 16)
                    for t in range(TT):
                        A(xt["b"][:, 4 * t:4 * t + 4, :].rearrange("p a b -> p (a b)"), norm_source(1, t),
                          ACT.Square, accum_out=sumsq[:, t, 1:2]).then_inc(stats_a, 1)
                elif name == "bcast":
                    rms_row_copy(arg)
                elif name == "tables":
                    act.wait_ge(prm_ready, 2)
                    repeated = bass.AP(tensor=bias_row.tensor, offset=bias_row.offset,
                                       ap=[list(bias_row.ap[0]), [0, P], [1, P]])
                    act.dma_start(bias_dram.rearrange("h (r y) -> h r y", y=P), repeated).then_inc(bias_out, 16)
                elif name == "norm_t":
                    for m in range(arg[1], arg[2]):
                        norm_hi(arg[0], m)
                elif name == "bias_load":
                    act.wait_ge(bias_out, 16)
                    src = bass.AP(tensor=bias_dram.tensor, offset=0, ap=[[P - 1, P], [P * P, SWA], [1, P]])
                    act.dma_start(bias_m[:, :, 1, :], src).then_inc(bias_in, 16)
                elif name == "gates_split":
                    act.wait_ge(small_in, 16 * N_SMALL)
                    A(gate_parts[:, 0], gate_w_in).then_inc(gate_split, 1)
                elif name == "gates":
                    act.wait_ge(gate_t_ready, 3)
                    step(A(f_e, f_e, ACT.Exp))
                    A(f_e, f_e, ACT.Ln, bias=1.0).then_inc(gate_a, 1)
                elif name == "head_n":
                    kind, i, a = arg
                    r = a % 3
                    act.wait_ge(scored, a + 1)
                    w0, w1 = (T, 2 * T) if kind == "x" else (P, 3 * P)
                    src = ps[:, score_bank(arg), :] if kind == "x" else probs[:, r, :]
                    if kind == "swa":
                        A(sink_e[:, r, :], negmax[:, r, :], ACT.Exp, bias=sinks[:, i:i + 1])
                    A(probs[:, r, 0:w0], src[:, 0:w0], ACT.Exp, bias=negmax[:, r, 0:1], accum_out=den[:, r, 0:1])
                    A(probs[:, r, w0:w1], src[:, w0:w1], ACT.Exp, bias=negmax[:, r, 1:2],
                      accum_out=den[:, r, 1:2]).then_inc(exped, 1)
                elif name == "head_t":
                    kind, i, a = arg
                    b = probs_bank(arg)
                    act.wait_ge(bank_full[b], full[(name, a), b])
                    if a >= 2 and kind != "x":
                        act.wait_ge(bank_full[6], full[("head_o", a - 2), 6])
                    w = 2 * T if kind == "x" else 3 * P
                    A(head_probs_t(arg)[:, 0:w], ps[:, b, 0:w]).then_inc(pt_ready, 1)
                elif name == "head_o":
                    kind, i, a = arg
                    b = out_bank(arg)
                    act.wait_ge(bank_full[b], full[(name, a), b])
                    q = head_sources(arg)[0]
                    A(work[:, q:q + T], ps[:, b, 0:T]).then_inc(o_ready, 1)
                elif name == "gla_z":
                    act.wait_ge(gla_d, 1)
                    step(A(g_e, g_e, ACT.Exp))
                    A(g_e, g_e, ACT.Ln, bias=1.0).then_inc(gla_a, 1)
                elif name == "gla_decay":
                    act.wait_ge(gla_d, 2)
                    A(g_z, g_b, ACT.Exp).then_inc(gla_a, 1)
                    A(g_m, g_b, ACT.Exp, scale=-1.0).then_inc(gla_a, 1)
                elif name == "gla_scale":
                    act.wait_ge(gla_d, 3)
                    A(g_kend_t, g_kend_t, ACT.Exp).then_inc(gla_a, 1)
                elif name == "gla_scores":
                    act.wait_ge(gla_p, 1)
                    for par, b in ((0, 4), (1, 6)):
                        act.wait_ge(bank_full[b], full[name, b])
                        for half in range(2):
                            q = slice(64 * half, 64 * half + 64)
                            ins = A(g_at[q, par::2, half::2, :],
                                    ps[q, b, 0:256].rearrange("p (h m c) -> p h m c", h=2, m=2))
                    ins.then_inc(gla_a, 1)
                elif name == "gla_silu":
                    act.wait_ge(proj_done, PROJ["gr"])
                    nc.scalar.preload_act_table(ACT.Silu)
                    A(wk(GR, 1024), wk(GR, 1024), ACT.Silu).then_inc(gla_a, 1)
                    nc.scalar.preload_act_table_set("natural_log_exp_and_others")

            def stationary_hi(v):
                w = units[v]
                for s in range(2):
                    k = 2 * wides.index(v) + s
                    tile = w.k0 + s
                    if w.w == "w_mix_out" and tile >= FOX + SWA:
                        act.wait_ge(gla_done, 1)
                    else:
                        act.wait_ge(o_ready, tile + 1 + (FOX + SWA if w.w == "wo_x" else 0))
                    act.wait_ge(sub_used, 2 * v + s - 3)
                    A(xt[w.ring][:, k % 4, 0:T], work[:, w.tiles[tile]:w.tiles[tile] + T]).then_inc(stat_hi, 1)

            for u in range(len(units)):
                split_hi(0, u + LOOK, [0])
                for name, arg in early.get(u, []):
                    do(name, arg)
                before, after, last = stationary_of(u)
                for v in before:
                    stationary_hi(v)
                split_hi(0, u + LOOK, [1])
                for v in after:
                    stationary_hi(v)
                for name, arg in late.get(u, []):
                    do(name, arg)
                for v in last:
                    stationary_hi(v)

            nc.scalar.preload_act_table(ACT.Silu)

            def down_stat(j, c, k):
                for s in range(2):
                    act.wait_ge(sub_used, 8 * j + (2 * c + s - 3))
                    A(xt["b"][:, (2 * c + s) % 4, 0:T],
                      act_t[:, bass.ds(j * (8 * T) + (k + s) * T, T)]).then_inc(stat_hi, 1)

            def up(j, first=False, last=False):
                for i in range(4):
                    split_hi(j, UP0 + i + LOOK)
                    if first and i == 0:
                        rms_row_copy(3)
                    if last and i >= 2:
                        act.wait_ge(act_done, 3)
                        down_stat(0, DOWN0 + i - 2, 2 * (i - 2))
                    if i % 2 == 0:
                        continue
                    side = i // 2
                    act.wait_ge(sub_used, 8 * j + (2 * (UP0 + i) + 2))
                    act.wait_ge(u_ready, 2 * j + (side + 1))
                    A(low[:, side, :, :], ps[:, 2 * side:2 * side + 2, T:2 * T]).then_inc(low_ready, 1)
                    act.wait_ge(u_ready, 2 * j + (side + 3))
                    act.wait_ge(act_done, j + 1)
                    for c in range(2):
                        ct = 2 * j + (FT * side + c)
                        ins = A(cv[:, 2 * side + c, :], u_pad[:, 2 * side + c, 2:2 + T], ACT.Identity,
                                scale=conv[:, 2, bass.ds(ct, 1)], bias=conv[:, 3, bass.ds(ct, 1)])
                    ins.then_inc(cv_init, 1)
                    if side == 1:
                        act.wait_ge(cv_done, 2 * j + 1)
                        A(cv[:, 0:2, :], cv[:, 0:2, :], ACT.Silu).then_inc(silu_done, 1)

            up(0, first=True)
            with act.Fori(1, UP_ITERS - 1) as j:
                up(j)
            up(UP_ITERS - 1, last=True)

            def down(j, x):
                for i in range(4):
                    split_hi(j, DOWN0 + x + i)
                    down_stat(j, DOWN0 + x + i, 2 * ((x + i) % HALF))

            with act.Fori(0, HALF // 4) as j:
                down(j, LOOK)
            for i in range(LOOK):
                split_hi(0, DOWN0 + HALF + i)
                down_stat(0, DOWN0 + HALF + i, 2 * i)
            wide_squares(DOWN_CHUNK0, 0, 8)
            with act.Fori(0, HALF // 4) as j:
                down(j, HALF + LOOK)
            wide_squares(DOWN_CHUNK0 + 4, 1, 9)

        @block.tensor
        def _(pe):
            n_stat = [0]

            def mm(out_, a, b, start, stop):
                return nc.tensor.matmul(out_, a, b, start=start, stop=stop, skip_group_check=True)

            def wait_bank(key, b):
                if free[key, b]:
                    pe.wait_ge(*free[key, b])

            def cols_sub(slot, k0, nk, first, last, banks, X):
                for kk in range(nk):
                    for c in range(2):
                        at, b, k = 256 * kk + P * c, banks[c], k0 + kk
                        hi, lo = wt_hi[:, slot, at:at + P], wt_lo[:, slot, at:at + P]
                        if last and kk == nk - 1:
                            mm(ps[:, b, T:2 * T], lo, X[:, k, 0:T], False, False)
                            ins = mm(ps[:, b, :], hi, X[:, k, :], False, True)
                        else:
                            mm(ps[:, b, :], hi, X[:, k, :], first and kk == 0, False)
                            ins = mm(ps[:, b, T:2 * T], lo, X[:, k, 0:T], False, False)
                ins.then_inc(sub_used, 1)

            def rows_sub(slot, k0, nk, ncols, first, last, banks, X):
                for kk in range(nk):
                    hi = wt_hi[:, slot, ncols * kk:ncols * kk + ncols]
                    lo = wt_lo[:, slot, ncols * kk:ncols * kk + ncols]
                    for t in range(TT):
                        x_hi, x_lo = X[:, k0 + kk, P * t:P * t + P], X[:, k0 + kk, T + P * t:T + P * t + P]
                        o = ps[:, banks[t], 0:ncols]
                        mm(o, x_hi, hi, first and kk == 0, False)
                        mm(o, x_hi, lo, False, False)
                        ins = mm(o, x_lo, hi, False, last and kk == nk - 1)
                ins.then_inc(sub_used, 1)

            def wide_sub(slot, xs, first, last, base, X, waits={}):
                for t in range(TT):
                    for c in range(2):
                        if waits.get(base + 2 * t + c):
                            pe.wait_ge(*waits[base + 2 * t + c])
                    x_hi, x_lo = X[:, xs, P * t:P * t + P], X[:, xs, T + P * t:T + P * t + P]
                    o = [ps[:, base + 2 * t + c, :] for c in range(2)]
                    hi = [wt_hi[:, slot, 512 * c:512 * c + 512] for c in range(2)]
                    lo = [wt_lo[:, slot, 512 * c:512 * c + 512] for c in range(2)]
                    for c in range(2):
                        mm(o[c], x_hi, hi[c], first, False)
                    for c in range(2):
                        mm(o[c], x_hi, lo[c], False, False)
                    for c in range(2):
                        ins = mm(o[c], x_lo, hi[c], False, last)
                    if last and t == 0:
                        ins.then_inc(tile0_full, 1)
                ins.then_inc(sub_used, 1)

            def transpose_rows(k, m):
                b = norm_bank(k, m)
                if k == 0:
                    pe.wait_ge(x_in[m // 4], 16)
                elif k == 1:
                    pe.wait_ge(mem_in, 16)
                else:
                    pe.wait_ge(h_added, 8 * (k - 2) + 4 * (m // 4) + m // 2 % 2 + 3)
                wait_bank(("norm_t", k, m), b)
                for i in range(2):
                    for t in range(TT):
                        at = P * (2 * m + i)
                        ins = nc.tensor.transpose(ps[:, b, T * i + P * t:T * i + P * t + P],
                                                  norm_source(k, t)[:, at:at + P], ident[:])
                ins.then_inc(bank_full[b], 1)

            def broadcast_rms(k):
                pe.wait_ge(diag_ready, k + 1)
                pe.wait_ge(c_ready, 2)
                wait_bank(("bcast", k), 7)
                mm(ps[:, 7, 0:T], ones[:, 0:P], diag, True, True).then_inc(bank_full[7], 1)

            def do_unit(u):
                w = units[u]
                waits = {b: free["unit", u, b] for b in w.banks} if w.first else {}
                if w.kind != "wide":
                    for b in waits:
                        if waits[b]:
                            pe.wait_ge(*waits[b])
                for s in range(2):
                    pe.wait_ge(lo_done, 2 * u + s + 1)
                    slot, nk = (2 * u + s) % 4, w.nk // 2
                    first, last = w.first and s == 0, w.last and s == 1
                    if w.kind == "wide":
                        n_stat[0] += 1
                        pe.wait_ge(stat_lo, n_stat[0])
                        wide_sub(slot, (n_stat[0] - 1) % 4, first, last, w.banks[0], xt[w.ring], {} if s else waits)
                        if u == WO0 and s == 0:
                            for name, arg in jobs[u]:
                                do(name, arg)
                        continue
                    k0 = w.k0 + nk * s
                    before = 8 if w.xt == "b" else 0 if u < N_MIX else 16
                    pe.wait_ge(xt_ready, before + (k0 + nk) // 2)
                    if w.kind == "cols":
                        cols_sub(slot, k0, nk, first, last, w.banks, xt[w.xt])
                    else:
                        rows_sub(slot, k0, nk, w.nc, first, last, w.banks, xt[w.xt])
                    if u == 0 and s == 0:
                        for m in (6, 7):
                            transpose_rows(0, m)

            def do(name, arg):
                if name == "norm_t":
                    if arg != (3, 4, 8):
                        for m in range(arg[1], arg[2]):
                            transpose_rows(arg[0], m)
                elif name == "bcast" and arg < 3:
                    broadcast_rms(arg)
                elif name == "tables":
                    pe.wait_ge(small_in, 16 * N_SMALL)
                    wait_bank(name, 4)
                    nc.tensor.transpose(ps[:, 4, P:P + NPRM - G_X], rows_prm, ident[0:NPRM - G_X, 0:NPRM - G_X])
                    mm(ps[0:SWA, 4, 0:P], t5_sb, onehot_sb, True, True).then_inc(bank_full[4], 1)
                    wait_bank(name, 5)
                    for i in range(4):
                        ins = nc.tensor.transpose(ps[:, 5, 2 * FT * i:2 * FT * i + 2 * FT], rows_conv[:, i, :],
                                                  ident[0:2 * FT, 0:2 * FT])
                    ins.then_inc(bank_full[5], 1)
                elif name == "gates":
                    pe.wait_ge(gate_split, 2)
                    wait_bank(name, 7)
                    gates = ps[0:GATES, 7, 0:T]
                    for k in range(KT):
                        x_hi, x_lo = xt["a"][:, k, 0:T], xt["a"][:, k, T:2 * T]
                        mm(gates, gate_parts[:, 0, k, :], x_hi, k == 0, False)
                        mm(gates, gate_parts[:, 0, k, :], x_lo, False, False)
                        ins = mm(gates, gate_parts[:, 1, k, :], x_hi, False, k == KT - 1)
                    ins.then_inc(bank_full[7], 1)
                elif name == "head_s":
                    kind, i, a = arg
                    q, k, _, need, _ = head_sources(arg)
                    pe.wait_ge(proj_done, need)
                    if kind == "fox":
                        pe.wait_ge(fox_ready, 1)
                    b = score_bank(arg)
                    wait_bank((name, a), b)
                    for qb, o, w in ((0, 0, T), (1, T, T)) if kind == "x" else ((0, 0, P), (1, P, T)):
                        dst = ps[:, b, o:o + w]
                        ins = mm(dst, work[:, q + P * qb:q + P * qb + P], work[:, k:k + w], True, kind != "fox")
                        if kind == "fox":
                            mm(dst, c_sel[:, i, P * qb:P * qb + P], ones[0:FOX, 0:w], False, False)
                            ins = mm(dst, sel[:, i, :], neg_c[:, 0:w], False, True)
                    ins.then_inc(bank_full[b], 1)
                elif name == "head_t":
                    kind, i, a = arg
                    pe.wait_ge(normed, a + 1)
                    b = probs_bank(arg)
                    wait_bank((name, a), b)
                    if kind == "x":
                        moves = [(T * qb + P * kb, T * kb + P * qb) for qb in range(2) for kb in range(2)]
                    else:
                        moves = [(P * c, P * c) for c in range(3)]
                    for src, dst in moves:
                        ins = nc.tensor.transpose(ps[:, b, dst:dst + P], probs[:, a % 3, src:src + P], ident[:])
                    ins.then_inc(bank_full[b], 1)
                elif name == "head_o":
                    kind, i, a = arg
                    _, _, v, _, need = head_sources(arg)
                    pe.wait_ge(pt_ready, a + 1)
                    pe.wait_ge(proj_done, need)
                    b, pt = out_bank(arg), head_probs_t(arg)
                    wait_bank((name, a), b)
                    mm(ps[:, b, 0:T], v[:, 0, :], pt[:, 0:T], True, False)
                    if kind == "x":
                        ins = mm(ps[:, b, 0:T], v[:, 1, :], pt[:, T:2 * T], False, True)
                    else:
                        ins = mm(ps[:, b, P:T], v[:, 1, :], pt[:, T:3 * P], False, True)
                    ins.then_inc(bank_full[b], 1)
                elif name == "gla_z":
                    wait_bank(name, 7)
                    for c in range(2):
                        ins = mm(ps[:, 7, T * c:T * c + T], gla_w[:, P * c:P * c + P], glr_t, True, True)
                    ins.then_inc(bank_full[7], 1)
                elif name == "gla_scores":
                    pe.wait_ge(gla_d, 4)
                    wait_bank(name, 7)
                    for t in range(TT):
                        for c in range(2):
                            ins = nc.tensor.transpose(ps[:, 7, T * t + P * c:T * t + P * c + P],
                                                      g_kend_t[:, T * c + P * t:T * c + P * t + P], ident[:])
                    ins.then_inc(bank_full[7], 1)
                    for par, b in ((0, 4), (1, 6)):
                        wait_bank(name, b)
                        rows = slice(64 * par, 64 * par + 64)
                        for hh in range(par, GLA, 2):
                            for c in range(NCH):
                                tok = T * (hh // 2) + CHUNK * c
                                col = 128 * (hh // 2) + 64 * (c // 2)
                                ins = mm(ps[64 * (c % 2):64 * (c % 2) + 64, b, col:col + 64],
                                         work[rows, GK + tok:GK + tok + 64], work[rows, GQ + tok:GQ + tok + 64],
                                         True, True)
                        ins.then_inc(bank_full[b], 1)
                elif name == "gla_kv":
                    pe.wait_ge(gla_d, 5)
                    pe.wait_ge(proj_done, PROJ["gv"])
                    gv = wk(GV, TT, 512)
                    for b, some in ((4, (0, 2)), (7, (1,))):
                        wait_bank(name, b)
                        for c in some:
                            tok = slice(64 * (c % 2), 64 * (c % 2) + 64)
                            for hh in range(GLA):
                                col = T * (c // 2) + P * (hh // 2)
                                ins = mm(ps[64 * (hh % 2):64 * (hh % 2) + 64, b, col:col + P],
                                         g_kend[tok, c // 2, 64 * hh:64 * hh + 64],
                                         gv[tok, c // 2, P * hh:P * hh + P], True, True)
                        ins.then_inc(bank_full[b], 1)
                elif name == "gla_out":
                    pe.wait_ge(gla_d, 6)
                    pe.wait_ge(gla_p, 3)
                    gv = wk(GV, TT, 512)
                    for t, b in ((0, 6), (1, 7)):
                        wait_bank(name, b)
                        for c in (2 * t, 2 * t + 1):
                            half = 64 * (c % 2)
                            for hh in range(GLA):
                                o = ps[half:half + 64, b, P * hh:P * hh + P]
                                ins = mm(o, g_at[:, hh, c, :], gv[:, t, P * hh:P * hh + P], True, c == 0)
                                if c:
                                    tok = GQ + T * (hh // 2) + CHUNK * c
                                    ins = mm(o, work[:, tok:tok + 64], g_s[:, hh, c - 1, :], False, True)
                        ins.then_inc(bank_full[b], 1)
                elif name == "gla_o":
                    pe.wait_ge(gla_d, 8)
                    for b in (6, 7):
                        wait_bank(name, b)
                        for i in range(2):
                            hh = 2 * (b - 6) + i
                            for t in range(TT):
                                ins = nc.tensor.transpose(ps[:, b, T * i + P * t:T * i + P * t + P],
                                                          g_o[:, t, P * hh:P * hh + P], ident[:])
                        ins.then_inc(bank_full[b], 1)

            pe.wait_ge(prm_in, 16)
            pe.wait_ge(c_ready, 1)
            nc.tensor.transpose(ps[:, 4, 0:G_X], rows_mix, ident[0:G_X, 0:G_X]).then_inc(bank_full[4], 1)
            for m in range(6):
                transpose_rows(0, m)
            for u in range(len(units)):
                do_unit(u)
                for name, arg in jobs.get(u, []) if u != WO0 else []:
                    do(name, arg)

            def up(j, first=False):
                for i in range(4):
                    if i % 2 == 0:
                        if first:
                            for b in (i, i + 1):
                                pe.wait_ge(*up_free[b])
                        else:
                            pe.wait_ge(u_ready, 2 * j + (i // 2 + 1))
                    for s in range(2):
                        pe.wait_ge(lo_done, 8 * j + (2 * (UP0 + i) + s + 1))
                        if first:
                            pe.wait_ge(xt_ready, 24 + 4 * (i % 2) + 2 * s + 2)
                        cols_sub((2 * i + s) % 4, 8 * (i % 2) + 4 * s, 4, i % 2 == 0 and s == 0,
                                 i % 2 == 1 and s == 1, [i // 2 * 2, i // 2 * 2 + 1], xt["a"])
                        if first and i == 0:
                            for m in (4 + 2 * s, 5 + 2 * s):
                                transpose_rows(3, m)
                    if first and i == 1:
                        broadcast_rms(3)

            up(0, first=True)
            with pe.Fori(1, UP_ITERS) as j:
                up(j)

            def down(j, x, n, first=False, last=False):
                for i in range(n):
                    for s in range(2):
                        pe.wait_ge(lo_done, 8 * j + (2 * (DOWN0 + x + i) + s + 1))
                        pe.wait_ge(stat_lo, 8 * j + (STAT0 + 2 * (x + i) + s + 1))
                        slot = (2 * (x + i) + s) % 4
                        wide_sub(slot, slot, first and i == 0 and s == 0, last and i == n - 1 and s == 1,
                                 4 * (1 - x // HALF), xt["b"])

            for b in range(4, 8):
                pe.wait_ge(*down_free[b])
            down(0, 0, 4, first=True)
            with pe.Fori(1, HALF // 4) as j:
                down(j, 0, 4)
            down(0, 4 * (HALF // 4), HALF % 4, last=True)
            pe.wait_ge(u_ready, 2 + 2 * UP_ITERS)
            down(0, HALF, HALF % 4, first=True)
            with pe.Fori(0, HALF // 4 - 1) as j:
                down(j, HALF + HALF % 4, 4)
            down(HALF // 4 - 1, HALF + HALF % 4, 4, last=True)

        @block.vector
        def _(dve):
            V = nc.vector
            n = [0]

            def step(ins):
                n[0] += 1
                ins.then_inc(dve_step, 1)
                dve.wait_ge(dve_step, n[0])

            def split_lo(j, c, subs=(0, 1)):
                for s in subs:
                    dve.wait_ge(hi_done, 8 * j + (2 * c + s + 1))
                    V.tensor_tensor(wt_lo[:, (2 * c + s) % 4, :], raw[:, c % RAW, SUB * s:SUB * s + SUB],
                                    wt_hi[:, (2 * c + s) % 4, :].bitcast(F32), ALU.subtract).then_inc(lo_done, 1)

            def norm_lo(k, m):
                b, X = norm_bank(k, m), XT_OF[k]
                dve.wait_ge(xt_hi, 8 * k + m + 1)
                for i in range(2):
                    kk = 2 * m + i
                    ins = V.scalar_tensor_tensor(X[:, kk, T:2 * T], ps[:, b, T * i:T * i + T],
                                                 prm[:, GAIN_ROW[k] + kk:GAIN_ROW[k] + kk + 1],
                                                 X[:, kk, 0:T].bitcast(F32), ALU.mult, ALU.subtract)
                ins.then_inc(xt_ready, 1)

            def mean_squares():
                step(V.tensor_reduce(meansq[:, 0:TT], sumsq[:], AX.X, ALU.add))
                V.tensor_scalar(meansq[:, 0:TT], meansq[:, 0:TT], 1.0 / D, EPS, ALU.mult,
                                ALU.add).then_inc(meansq_ready, 1)

            def wide_add(nth, bank, half, subs):
                dve.wait_ge(tile0_full, nth)
                for i in range(4):
                    t, c = i // 2, i % 2
                    if i == 2:
                        dve.wait_ge(sub_used, subs)
                    col = 1024 * half + 512 * c
                    V.tensor_tensor(h[:, t, col:col + 512], h[:, t, col:col + 512], ps[:, bank + i, :],
                                    ALU.add).then_inc(h_added, 1)

            dve.wait_ge(bank_full[4], 1)
            V.tensor_copy(prm[:, 0:G_X], ps[:, 4, 0:G_X]).then_inc(prm_ready, 1)
            for s, ms in enumerate((range(4), (4, 5))):
                for m in ms:
                    norm_lo(0, m)
                split_lo(0, 0, [s])
            for m in (6, 7):
                norm_lo(0, m)
            split_lo(0, 1)

            def do(name, arg):
                if name == "evac_cols":
                    w, g = units[arg], cols_groups.index(arg)
                    b = w.banks[0]
                    dve.wait_ge(low_ready, g + 1)
                    dst = wk(w.dest, 2, T)
                    step(V.scalar_tensor_tensor(dst, ps[:, b:b + 2, 0:T], w.scale, low[:, g % 2, :, :],
                                                ALU.mult, ALU.add))
                    k = norm_of(w)
                    dve.wait_ge(row_ready, k + 1)
                    V.tensor_tensor(dst, dst, rms_row(k).unsqueeze(1).broadcast_to([P, 2, T]),
                                    ALU.mult).then_inc(proj_done, 1)
                elif name == "evac_rows":
                    w = units[arg]
                    b = w.banks[0]
                    dve.wait_ge(sub_used, 2 * arg + 2)
                    k = norm_of(w)
                    dve.wait_ge(rstd_ready, k + 1)
                    for t in range(TT):
                        ins = V.tensor_scalar(wk(w.dest, TT, w.nc)[:, t, :], ps[:, b + t, 0:w.nc],
                                              rms_col(k)[:, t:t + 1], None, ALU.mult)
                    ins.then_inc(proj_done, 1)
                elif name == "evac_wide":
                    wide_add(sorted(chunk0).index(arg) + 1, units[arg].banks[0], units[arg].half, 2 * arg + 2)
                elif name == "rms":
                    if arg == 0:
                        V.tensor_tensor_reduce(out=work[:, D:2 * D], in0=h[:, 1, :], in1=h[:, 1, :], scale=1.0,
                                               scalar=0.0, op0=ALU.mult, op1=ALU.add,
                                               accum_out=sumsq[:, 1, 0:1]).then_inc(stats_d, 1)
                        dve.wait_ge(stats_d, 1)
                    dve.wait_ge(stats_a, 2 * arg + 1)
                    if arg >= 2:
                        mean_squares()
                    else:
                        if arg == 1:
                            dve.wait_ge(rstd_ready, 1)
                        V.tensor_scalar(meansq[:, 0:TT], sumsq[:, :, arg], 1.0 / D, EPS, ALU.mult,
                                        ALU.add).then_inc(meansq_ready, 1)
                elif name == "diag":
                    dve.wait_ge(rstd_ready, arg + 1 + (arg >= 2))
                    if arg:
                        dve.wait_ge(row_ready, arg)
                    if arg == 1:
                        dve.wait_ge(bank_full[6], full[("head_o", FOX + SWA - 1), 6])
                    for t in range(TT):
                        ins = V.tensor_scalar(diag[:, P * t:P * t + P], ident[:], rms_col(arg)[:, t:t + 1],
                                              None, ALU.mult)
                    ins.then_inc(diag_ready, 1)
                elif name == "tables":
                    dve.wait_ge(small_in, 16 * N_SMALL)
                    dve.wait_ge(bank_full[4], full[name, 4])
                    V.tensor_copy(bias_row, ps[0:SWA, 4, 0:P]).then_inc(prm_ready, 1)
                    V.tensor_copy(prm[:, G_X:NPRM], ps[:, 4, P:P + NPRM - G_X]).then_inc(prm_ready, 1)
                    dve.wait_ge(bank_full[5], full[name, 5])
                    V.tensor_copy(conv[:].rearrange("p a b -> p (a b)"), ps[:, 5, 0:8 * FT]).then_inc(prm_ready, 1)
                elif name == "norm_t":
                    for m in range(arg[1], arg[2]):
                        norm_lo(arg[0], m)
                elif name == "gates_split":
                    dve.wait_ge(gate_split, 1)
                    V.tensor_tensor(gate_parts[:, 1], gate_w_in, gate_parts[:, 0].bitcast(F32),
                                    ALU.subtract).then_inc(gate_split, 1)
                elif name == "gates":
                    dve.wait_ge(bank_full[7], full[name, 7])
                    dve.wait_ge(row_ready, 1)
                    V.tensor_tensor(glr_t, ps[glr_rows, 7, 0:T], rms_row(0)[glr_rows],
                                    ALU.mult).then_inc(gate_t_ready, 1)
                    step(V.tensor_tensor(f_z, ps[0:FOX, 7, 0:T], rms_row(0)[0:FOX], ALU.mult))
                    V.tensor_scalar(f_z, f_z, b_fox[:], None, ALU.add).then_inc(gate_t_ready, 1)
                    dve.wait_ge(gate_t_ready, 2)
                    step(V.tensor_scalar(f_m, f_z, 0.0, None, ALU.min))
                    V.scalar_tensor_tensor(f_e, f_m, 2.0, f_z, ALU.mult, ALU.subtract).then_inc(gate_t_ready, 1)
                elif name == "fox_gates":
                    dve.wait_ge(gate_a, 1)
                    dve.wait_ge(c_ready, 3)
                    step(V.tensor_tensor(f_m, f_m, f_e, ALU.subtract))
                    step(V.tensor_tensor_scan(f_z, ones[0:FOX, :], f_m, 0.0, ALU.mult, ALU.add))
                    V.tensor_scalar(neg_c, f_z, -1.0, None, ALU.mult)
                    for i in range(FOX):
                        ins = V.tensor_scalar(c_sel[:, i, :], f_z, sel[:, i, 0:1], None, ALU.mult)
                    ins.then_inc(fox_ready, 1)
                elif name == "head_s":
                    kind, i, a = arg
                    r = a % 3
                    b = score_bank(arg)
                    dve.wait_ge(bank_full[b], full[(name, a), b])
                    if a == 0:
                        dve.wait_ge(bias_out, 16)
                    if a >= 3:
                        b = 6 if a - 3 == FOX + SWA + 1 else 5
                        dve.wait_ge(bank_full[b], full[("head_t", a - 3), b])
                    w0, w1 = (T, 2 * T) if kind == "x" else (P, 3 * P)
                    src = ps[:, score_bank(arg), :] if kind == "x" else probs[:, r, :]
                    if kind == "fox":
                        V.tensor_tensor(probs[:, r, 0:T], ps[:, 4, 0:T], fox_mask[:], ALU.add)
                        step(V.tensor_tensor(probs[:, r, T:w1], ps[:, 4, T:w1], fox_mask[:, 0:P], ALU.add))
                    if kind == "swa":
                        dve.wait_ge(bias_done, 2)
                        V.tensor_tensor(probs[:, r, 0:T], ps[:, 4, 0:T],
                                        bias_m[:, i, :, :].rearrange("p m k -> p (m k)"), ALU.add)
                        step(V.tensor_tensor(probs[:, r, T:w1], ps[:, 4, T:w1], bias_m[:, i, 0, :], ALU.add))
                    V.tensor_reduce(rowmax[:, r, 0:1], src[:, 0:w0], AX.X, ALU.max)
                    step(V.tensor_reduce(rowmax[:, r, 1:2], src[:, w0:w1], AX.X, ALU.max))
                    if kind == "swa":
                        V.tensor_scalar(negmax[:, r, :], rowmax[:, r, :], sinks[:, i:i + 1], -1.0, ALU.max,
                                        ALU.mult).then_inc(scored, 1)
                    else:
                        V.tensor_scalar(negmax[:, r, :], rowmax[:, r, :], -1.0, None, ALU.mult).then_inc(scored, 1)
                elif name == "head_n":
                    kind, i, a = arg
                    r = a % 3
                    dve.wait_ge(exped, a + 1)
                    w0, w1 = (T, 2 * T) if kind == "x" else (P, 3 * P)
                    if kind == "swa":
                        step(V.tensor_tensor(den[:, r, :], den[:, r, :], sink_e[:, r, :], ALU.add))
                    step(V.reciprocal(rden[:, r, :], den[:, r, :]))
                    V.tensor_scalar(probs[:, r, 0:w0], probs[:, r, 0:w0], rden[:, r, 0:1], None, ALU.mult)
                    V.tensor_scalar(probs[:, r, w0:w1], probs[:, r, w0:w1], rden[:, r, 1:2], None,
                                    ALU.mult).then_inc(normed, 1)
                elif name == "gla_z":
                    dve.wait_ge(bank_full[7], full[name, 7])
                    dve.wait_ge(bank_full[4], full[("head_s", FOX - 1), 4])
                    for c in range(2):
                        ins = V.tensor_scalar(g_z[:, T * c:T * c + T], ps[:, 7, T * c:T * c + T],
                                              prm[:, B_GATE + c:B_GATE + c + 1], None, ALU.add)
                    step(ins)
                    step(V.tensor_scalar(g_m, g_z, 0.0, None, ALU.min))
                    V.scalar_tensor_tensor(g_e, g_m, 2.0, g_z, ALU.mult, ALU.subtract).then_inc(gla_d, 1)
                elif name == "gla_decay":
                    dve.wait_ge(gla_a, 1)
                    step(V.tensor_tensor(g_m, g_m, g_e, ALU.subtract))
                    step(V.tensor_scalar(g_m, g_m, 1.0 / 16.0, None, ALU.mult))
                    for c in range(2 * NCH):
                        at = slice(CHUNK * c, CHUNK * c + CHUNK)
                        ins = V.tensor_tensor_scan(g_b[:, at], ones[:, 0:CHUNK], g_m[:, at], 0.0, ALU.mult, ALU.add)
                    ins.then_inc(gla_d, 1)
                elif name == "gla_scale":
                    dve.wait_ge(bank_full[6], full[("head_o", FOX - 1), 6])
                    dve.wait_ge(gla_d, 2)
                    b4 = g_b.rearrange("p (n c) -> p n c", c=CHUNK)
                    V.tensor_tensor(g_kend_t.rearrange("p (n c) -> p n c", c=CHUNK),
                                    b4[:, :, CHUNK - 1:CHUNK].broadcast_to([P, 2 * NCH, CHUNK]), b4,
                                    ALU.subtract).then_inc(gla_d, 1)
                    dve.wait_ge(gla_a, 4)
                    dve.wait_ge(proj_done, PROJ["gq"])
                    step(V.tensor_tensor(g_kend_t, g_kend_t, wk(GK, 512), ALU.mult))
                    V.tensor_tensor(wk(GK, 512), wk(GK, 512), g_m, ALU.mult)
                    V.tensor_tensor(wk(GQ, 512), wk(GQ, 512), g_z, ALU.mult).then_inc(gla_d, 1)
                elif name == "gla_scores":
                    dve.wait_ge(bank_full[7], full[name, 7])
                    V.tensor_copy(g_kend, ps[:, 7, :].rearrange("p (t n) -> p t n", t=TT)).then_inc(gla_d, 1)
                elif name == "gla_kv":
                    dve.wait_ge(gla_p, 2)
                    dve.wait_ge(bank_full[4], full[name, 4])
                    dve.wait_ge(bank_full[7], full[name, 7])
                    for par in range(2):
                        rows = slice(64 * par, 64 * par + 64)
                        ins = V.tensor_copy(g_s[rows, par::2, 0, :],
                                            ps[rows, 4, 0:T].rearrange("p (h n) -> p h n", h=2))
                    step(ins)
                    for c, b, at in ((1, 7, 0), (2, 4, T)):
                        for par in range(2):
                            rows = slice(64 * par, 64 * par + 64)
                            for i in range(2):
                                last = T * i + CHUNK * c + CHUNK - 1
                                ins = V.scalar_tensor_tensor(g_s[rows, 2 * i + par, c, :],
                                                             g_s[rows, 2 * i + par, c - 1, :],
                                                             g_z[rows, last:last + 1],
                                                             ps[rows, b, at + P * i:at + P * i + P], ALU.mult, ALU.add)
                        if c == 1:
                            step(ins)
                    ins.then_inc(gla_d, 1)
                elif name == "gla_out":
                    dve.wait_ge(bank_full[6], full[name, 6])
                    dve.wait_ge(bank_full[7], full[name, 7])
                    V.tensor_copy(g_o, ps[:, 6:8, :]).then_inc(gla_d, 1)
                elif name == "gla_rms":
                    dve.wait_ge(gla_d, 7)
                    step(V.tensor_tensor(g_sq, g_o, g_o, ALU.mult))
                    step(V.tensor_reduce(meansq[:, 0:8], g_sq.rearrange("p t (h n) -> p (t h) n", n=GLA_DV), AX.X,
                                         ALU.add))
                    V.tensor_scalar(meansq[:, 0:8], meansq[:, 0:8], 1.0 / GLA_DV, EPS, ALU.mult,
                                    ALU.add).then_inc(meansq_ready, 1)
                elif name == "gla_norm":
                    dve.wait_ge(rstd_ready, 3)
                    o8 = g_o.rearrange("p t (h n) -> p (t h) n", n=GLA_DV)
                    V.tensor_tensor(o8, o8, rstd[:, 0:8].unsqueeze(2).broadcast_to([P, 8, GLA_DV]),
                                    ALU.mult).then_inc(gla_d, 1)
                elif name == "gla_o":
                    dve.wait_ge(gla_a, 6)
                    for b in (6, 7):
                        dve.wait_ge(bank_full[b], full[name, b])
                        at = 512 * (b - 6)
                        ins = V.scalar_tensor_tensor(wk(FK + at, 512), ps[:, b, :], prm[:, G_GLA:G_GLA + 1],
                                                     wk(GR + at, 512), ALU.mult, ALU.mult)
                    ins.then_inc(gla_done, 1)

            def stationary_lo(v):
                w = units[v]
                for s in range(2):
                    k, at = 2 * wides.index(v) + s, w.tiles[w.k0 + s]
                    dve.wait_ge(stat_hi, k + 1)
                    V.tensor_tensor(xt[w.ring][:, k % 4, T:2 * T], work[:, at:at + T],
                                    xt[w.ring][:, k % 4, 0:T].bitcast(F32), ALU.subtract).then_inc(stat_lo, 1)

            for u in range(len(units)):
                split_lo(0, u + LOOK, [0])
                for name, arg in early.get(u, []):
                    do(name, arg)
                before, after, last = stationary_of(u)
                for v in before:
                    stationary_lo(v)
                split_lo(0, u + LOOK, [1])
                for v in after:
                    stationary_lo(v)
                for name, arg in late.get(u, []):
                    do(name, arg)
                for v in last:
                    stationary_lo(v)

            def down_stat(j, c, k):
                for s in range(2):
                    dve.wait_ge(stat_hi, 8 * j + (STAT0 + 2 * (c - DOWN0) + s + 1))
                    X = xt["b"][:, (2 * c + s) % 4, :]
                    V.tensor_tensor(X[:, T:2 * T], act_t[:, bass.ds(j * (8 * T) + (k + s) * T, T)],
                                    X[:, 0:T].bitcast(F32), ALU.subtract).then_inc(stat_lo, 1)

            V.memset(u_pad[:, 0:2, 0:2], 0.0).then_inc(u_ready, 1)
            V.memset(u_pad[:, 2:3, 0:2], 0.0).then_inc(u_ready, 1)
            V.memset(u_pad[:, 3:4, 0:2], 0.0).then_inc(act_done, 1)
            dve.wait_ge(u_ready, 2)
            dve.wait_ge(act_done, 1)

            def up(j, first=False, last=False):
                for i in range(4):
                    split_lo(j, UP0 + i + LOOK)
                    if last and i >= 2:
                        down_stat(0, DOWN0 + i - 2, 2 * (i - 2))
                    if i % 2 == 0:
                        continue
                    side = i // 2
                    mine = slice(2 * side, 2 * side + 2)
                    dve.wait_ge(low_ready, 2 * j + (n_low + side + 1))
                    V.tensor_tensor(u_pad[:, mine, 2:2 + T], ps[:, mine, 0:T], low[:, side, :, :],
                                    ALU.add).then_inc(u_sum, 1)
                    dve.wait_ge(u_sum, 2 * j + (side + 1))
                    if first and side == 0:
                        dve.wait_ge(row_ready, 4)
                    V.tensor_tensor(u_pad[:, mine, 2:2 + T], u_pad[:, mine, 2:2 + T],
                                    rms_row(3).unsqueeze(1).broadcast_to([P, 2, T]), ALU.mult).then_inc(u_ready, 1)
                    dve.wait_ge(cv_init, 2 * j + (side + 1))
                    for tap, done in ((1, cv_tap), (0, cv_done)):
                        for c in range(2):
                            x2 = 2 * side + c
                            ct = 2 * j + (FT * side + c)
                            ins = V.scalar_tensor_tensor(cv[:, x2, :], u_pad[:, x2, tap:tap + T],
                                                         conv[:, tap, bass.ds(ct, 1)], cv[:, x2, :], ALU.mult, ALU.add)
                        ins.then_inc(done, 1)
                        dve.wait_ge(done, 2 * j + (side + 1))
                dve.wait_ge(silu_done, j + 1)
                V.tensor_tensor(act_t[:, bass.ds(j * (2 * T), 2 * T)].rearrange("p (a b) -> p a b", a=2), cv[:, 0:2, :],
                                cv[:, 2:4, :], ALU.mult).then_inc(act_done, 1)

            up(0, first=True)
            with dve.Fori(1, UP_ITERS - 1) as j:
                up(j)
            up(UP_ITERS - 1, last=True)

            def down(j, x):
                for i in range(4):
                    split_lo(j, DOWN0 + x + i)
                    down_stat(j, DOWN0 + x + i, 2 * ((x + i) % HALF))

            with dve.Fori(0, HALF // 4) as j:
                down(j, LOOK)
            for i in range(LOOK):
                split_lo(0, DOWN0 + HALF + i)
                down_stat(0, DOWN0 + HALF + i, 2 * i)
            wide_add(5, 4, 0, 2 * (DOWN0 + HALF))
            with dve.Fori(0, HALF // 4) as j:
                down(j, HALF + LOOK)
            wide_add(6, 0, 1, 2 * (DOWN0 + 2 * HALF))
            dve.wait_ge(stats_a, 9)
            mean_squares()
            dve.wait_ge(rstd_ready, 6)
            dve.wait_ge(raw_in[GAIN % RAW], 16 * (GAIN // RAW + 1))
            for c in range(4):
                for t in range(TT):
                    y = h[:, t, 512 * c:512 * c + 512]
                    V.scalar_tensor_tensor(y, y, rms_col(4)[:, t:t + 1], raw[:, GAIN % RAW, 512 * c:512 * c + 512],
                                           ALU.mult, ALU.mult).then_inc(out_ready, 1)


_INS = ["x", "mem", "w_in", "b_fox_f", "swa_sinks", "t5_bias", "w_gla_gate", "b_gla_gate", "gla_norm", "w_mix_out",
        "norm_mix", "norm_xattn", "norm_mem", "wq_x", "wkv_x", "wo_x", "norm_ffn", "w_up", "conv_w", "conv_b",
        "w_down", "final_norm"]


def kernel(**inputs):
    import concourse.bacc as bacc
    from concourse.bass_utils import run_bass_kernel_spmd

    nc = bacc.Bacc("TRN2", target_bir_lowering=False, num_devices=1)
    arrays, args = {}, []
    for name in _INS + ["t5_onehot"]:
        a = onehot_table() if name == "t5_onehot" else np.ascontiguousarray(inputs[name])
        arrays[f"in_{name}"] = a
        args.append(nc.dram_tensor(f"in_{name}", a.shape, mybir.dt.from_np(a.dtype), kind="ExternalInput").ap())
    out = nc.dram_tensor("out_y", inputs["x"].shape, F32, kind="ExternalOutput").ap()
    trunk(nc, *args, out)
    r = run_bass_kernel_spmd(nc, [arrays], core_ids=[0])
    return r.results[0]["out_y"]
```
